# Optimizing a Trainium2 kernel written in Bass

```python
import math
import jax, jax.numpy as jnp
from jax import lax
import numpy as np

D_MODEL = 1024
BATCH = 1
SEQ = 256
DEPTH = 2

N_A_LAYERS = DEPTH // 2
N_B_LAYERS = DEPTH - N_A_LAYERS
N_DENSE_LAYERS = (DEPTH + 1) // 2
N_MOE_LAYERS = DEPTH // 2

N_META = 16

RG_BLOCK_WIDTH = 128
D_RNN = (4 * D_MODEL // 3) // RG_BLOCK_WIDTH * RG_BLOCK_WIDTH
N_RG_BLOCKS = D_RNN // RG_BLOCK_WIDTH
CONV_WIDTH = 4
RG_C = 8.0

N_HEADS = D_MODEL // 64
QK_NOPE = 64
QK_ROPE = 32
V_HEAD = 64
KV_LORA = D_MODEL // 4
Q_LORA = 3 * D_MODEL // 8
ROPE_THETA = 10000.0
Q_BLOCK = 128

D_FF = 3 * D_MODEL
N_EXPERTS = 8
TOP_K = 2
E_FF = 7 * D_MODEL // 2

RMS_EPS = 1e-6

kernel_name = "yoco_rglru_mla_moe_hybrid"

def rms_norm(x, gain):
    xf = x.astype(jnp.float32)
    y = xf * lax.rsqrt(jnp.mean(xf * xf, axis=-1, keepdims=True) + RMS_EPS) * gain.astype(jnp.float32)
    return y.astype(x.dtype)

def rope_tables(t_len):
    pos = jnp.arange(t_len, dtype=jnp.float32)
    inv = ROPE_THETA ** (-jnp.arange(0, QK_ROPE, 2, dtype=jnp.float32) / QK_ROPE)
    ang = pos[:, None] * inv[None, :]
    return jnp.cos(ang), jnp.sin(ang)

def apply_rope(x, cos, sin):
    xf = x.astype(jnp.float32)
    x1, x2 = jnp.split(xf, 2, axis=-1)
    out = jnp.concatenate([x1 * cos - x2 * sin, x2 * cos + x1 * sin], axis=-1)
    return out.astype(x.dtype)

def _lru_combine(e1, e2):
    a1, b1 = e1
    a2, b2 = e2
    return a1 * a2, a2 * b1 + b2

def rglru_block(u, w_in, conv_w, conv_b, ga_w, ga_b, gx_w, gx_b, lam, w_out):
    b, t, _ = u.shape
    y, xr = jnp.split(u @ w_in, 2, axis=-1)
    xp = jnp.pad(xr, ((0, 0), (CONV_WIDTH - 1, 0), (0, 0)))
    xc = conv_b + sum(xp[:, k:k + t] * conv_w[k] for k in range(CONV_WIDTH))
    xb = xc.reshape(b, t, N_RG_BLOCKS, RG_BLOCK_WIDTH)
    r = jax.nn.sigmoid(jnp.einsum('btnc,ncd->btnd', xb, ga_w).reshape(b, t, D_RNN) + ga_b)
    ig = jax.nn.sigmoid(jnp.einsum('btnc,ncd->btnd', xb, gx_w).reshape(b, t, D_RNN) + gx_b)
    log_a = -RG_C * r.astype(jnp.float32) * jax.nn.softplus(-lam.astype(jnp.float32))
    a = jnp.exp(log_a)
    bx = jnp.sqrt(-jnp.expm1(2.0 * log_a)) * (ig * xc).astype(jnp.float32)
    _, hs = lax.associative_scan(_lru_combine, (a, bx), axis=1)
    return (jax.nn.gelu(y) * hs.astype(u.dtype)) @ w_out

def shared_latent_kv(h, kv_norm, w_dkv, latent_norm, w_ukv, cos, sin):
    b, t, _ = h.shape
    u = rms_norm(h, kv_norm)
    ckv, k_rope = jnp.split(u @ w_dkv, [KV_LORA], axis=-1)
    ckv = rms_norm(ckv, latent_norm)
    kv = (ckv @ w_ukv).reshape(b, t, N_HEADS, QK_NOPE + V_HEAD)
    k_nope, v = jnp.split(kv, [QK_NOPE], axis=-1)
    k_rope = apply_rope(k_rope, cos, sin)
    return k_nope, k_rope, v

def mla_block(u, k_nope, k_rope, v, w_dq, q_norm, w_uq, w_o, cos, sin):
    b, t, _ = u.shape
    cq = rms_norm(u @ w_dq, q_norm)
    q = (cq @ w_uq).reshape(b, t, N_HEADS, QK_NOPE + QK_ROPE)
    q_nope, q_rope = jnp.split(q, [QK_NOPE], axis=-1)
    q_rope = apply_rope(q_rope, cos[:, None, :], sin[:, None, :])
    n_blk = -(-t // Q_BLOCK)
    pad = n_blk * Q_BLOCK - t
    padt = lambda z: jnp.pad(z, [(0, 0), (0, pad)] + [(0, 0)] * (z.ndim - 2))
    q_nope, q_rope, kn, kr, vv = padt(q_nope), padt(q_rope), padt(k_nope), padt(k_rope), padt(v)
    scale = (QK_NOPE + QK_ROPE) ** -0.5
    neg = jnp.finfo(jnp.float32).min
    outs = []
    for blk in range(n_blk):
        s0, e = blk * Q_BLOCK, (blk + 1) * Q_BLOCK
        s = (jnp.einsum('bqhd,bkhd->bhqk', q_nope[:, s0:e], kn[:, :e])
             + jnp.einsum('bqhr,bkr->bhqk', q_rope[:, s0:e], kr[:, :e])).astype(jnp.float32) * scale
        mask = jnp.arange(s0, e)[:, None] >= jnp.arange(e)[None, :]
        p = jax.nn.softmax(jnp.where(mask, s, neg), axis=-1).astype(vv.dtype)
        outs.append(jnp.einsum('bhqk,bkhd->bqhd', p, vv[:, :e]))
    o = jnp.concatenate(outs, axis=1)[:, :t].reshape(b, t, N_HEADS * V_HEAD)
    return o @ w_o

def swiglu(u, w_gate_up, w_down):
    g, up = jnp.split(u @ w_gate_up, 2, axis=-1)
    return (jax.nn.silu(g) * up) @ w_down

def moe_swiglu(u, router_w, router_b, w_gate_up, w_down):
    b, t, d = u.shape
    tok = u.reshape(b * t, d)
    logits = (tok @ router_w).astype(jnp.float32) + router_b.astype(jnp.float32)
    probs = jax.nn.softmax(logits, axis=-1)
    top_p, top_i = lax.top_k(probs, TOP_K)
    top_p = top_p / jnp.sum(top_p, axis=-1, keepdims=True)
    gate = jnp.sum(jax.nn.one_hot(top_i, N_EXPERTS, dtype=jnp.float32) * top_p[..., None], axis=1)
    y = jnp.zeros_like(tok)
    for ex in range(N_EXPERTS):
        y = y + gate[:, ex:ex + 1].astype(tok.dtype) * swiglu(tok, w_gate_up[ex], w_down[ex])
    return y.reshape(b, t, d)

def setup_inputs(seed: int = 0) -> dict:
    key = jax.random.key(seed)
    ks = iter(jax.random.split(key, 48))
    nrm = lambda shape, fan_in: jax.random.normal(next(ks), shape, jnp.float32) * (fan_in ** -0.5)
    gain = lambda shape: 1.0 + 0.02 * jax.random.normal(next(ks), shape, jnp.float32)
    small = lambda shape, s=0.02: s * jax.random.normal(next(ks), shape, jnp.float32)
    na, nb, nd, nm = N_A_LAYERS, N_B_LAYERS, N_DENSE_LAYERS, N_MOE_LAYERS
    a_c = jax.random.uniform(next(ks), (na, D_RNN), jnp.float32, 0.9, 0.999)
    a_base = a_c ** (1.0 / RG_C)
    lam = jnp.log(a_base) - jnp.log1p(-a_base)
    return {
        "x": jax.random.normal(next(ks), (BATCH, SEQ, D_MODEL), jnp.float32),
        "meta_tokens": jax.random.normal(next(ks), (N_META, D_MODEL), jnp.float32),
        "a_pre_norm": gain((na, D_MODEL)),
        "a_w_in": nrm((na, D_MODEL, 2 * D_RNN), D_MODEL),
        "a_conv_w": nrm((na, CONV_WIDTH, D_RNN), CONV_WIDTH),
        "a_conv_b": small((na, D_RNN)),
        "a_gate_a_w": nrm((na, N_RG_BLOCKS, RG_BLOCK_WIDTH, RG_BLOCK_WIDTH), RG_BLOCK_WIDTH),
        "a_gate_a_b": small((na, D_RNN)),
        "a_gate_x_w": nrm((na, N_RG_BLOCKS, RG_BLOCK_WIDTH, RG_BLOCK_WIDTH), RG_BLOCK_WIDTH),
        "a_gate_x_b": small((na, D_RNN)),
        "a_lambda": lam,
        "a_w_out": nrm((na, D_RNN, D_MODEL), D_RNN),
        "a_post_norm": gain((na, D_MODEL)),
        "kv_norm": gain((D_MODEL,)),
        "kv_w_dkv": nrm((D_MODEL, KV_LORA + QK_ROPE), D_MODEL),
        "kv_latent_norm": gain((KV_LORA,)),
        "kv_w_ukv": nrm((KV_LORA, N_HEADS * (QK_NOPE + V_HEAD)), KV_LORA),
        "b_pre_norm": gain((nb, D_MODEL)),
        "b_w_dq": nrm((nb, D_MODEL, Q_LORA), D_MODEL),
        "b_q_norm": gain((nb, Q_LORA)),
        "b_w_uq": nrm((nb, Q_LORA, N_HEADS * (QK_NOPE + QK_ROPE)), Q_LORA),
        "b_w_o": nrm((nb, N_HEADS * V_HEAD, D_MODEL), N_HEADS * V_HEAD),
        "b_post_norm": gain((nb, D_MODEL)),
        "f_pre_norm": gain((nd, D_MODEL)),
        "f_w_gate_up": nrm((nd, D_MODEL, 2 * D_FF), D_MODEL),
        "f_w_down": nrm((nd, D_FF, D_MODEL), D_FF),
        "f_post_norm": gain((nd, D_MODEL)),
        "m_pre_norm": gain((nm, D_MODEL)),
        "m_router_w": nrm((nm, D_MODEL, N_EXPERTS), D_MODEL),
        "m_router_b": small((nm, N_EXPERTS), 0.01),
        "m_w_gate_up": nrm((nm, N_EXPERTS, D_MODEL, 2 * E_FF), D_MODEL),
        "m_w_down": nrm((nm, N_EXPERTS, E_FF, D_MODEL), E_FF),
        "m_post_norm": gain((nm, D_MODEL)),
    }

def reference(x, meta_tokens,
              a_pre_norm, a_w_in, a_conv_w, a_conv_b, a_gate_a_w, a_gate_a_b, a_gate_x_w, a_gate_x_b,
              a_lambda, a_w_out, a_post_norm,
              kv_norm, kv_w_dkv, kv_latent_norm, kv_w_ukv,
              b_pre_norm, b_w_dq, b_q_norm, b_w_uq, b_w_o, b_post_norm,
              f_pre_norm, f_w_gate_up, f_w_down, f_post_norm,
              m_pre_norm, m_router_w, m_router_b, m_w_gate_up, m_w_down, m_post_norm):
    b = x.shape[0]
    h = jnp.concatenate([jnp.broadcast_to(meta_tokens.astype(x.dtype)[None], (b, N_META, x.shape[2])), x], axis=1)
    t = h.shape[1]
    cos, sin = rope_tables(t)
    k_nope = k_rope = v = None
    for layer in range(DEPTH):
        if layer < N_A_LAYERS:
            i = layer
            mix = rglru_block(rms_norm(h, a_pre_norm[i]), a_w_in[i], a_conv_w[i], a_conv_b[i],
                              a_gate_a_w[i], a_gate_a_b[i], a_gate_x_w[i], a_gate_x_b[i],
                              a_lambda[i], a_w_out[i])
            h = h + rms_norm(mix, a_post_norm[i])
        else:
            if layer == N_A_LAYERS:
                k_nope, k_rope, v = shared_latent_kv(h, kv_norm, kv_w_dkv, kv_latent_norm, kv_w_ukv, cos, sin)
            i = layer - N_A_LAYERS
            mix = mla_block(rms_norm(h, b_pre_norm[i]), k_nope, k_rope, v,
                            b_w_dq[i], b_q_norm[i], b_w_uq[i], b_w_o[i], cos, sin)
            h = h + rms_norm(mix, b_post_norm[i])
        j = layer // 2
        if layer % 2 == 0:
            ff = swiglu(rms_norm(h, f_pre_norm[j]), f_w_gate_up[j], f_w_down[j])
            h = h + rms_norm(ff, f_post_norm[j])
        else:
            ff = moe_swiglu(rms_norm(h, m_pre_norm[j]), m_router_w[j], m_router_b[j], m_w_gate_up[j], m_w_down[j])
            h = h + rms_norm(ff, m_post_norm[j])
    return h[:, N_META:]


_drawn_inputs = setup_inputs


def setup_inputs(seed=0):
    import zlib

    import numpy as np

    out = dict(_drawn_inputs(seed))
    spreads = {}
    factors = {'a_gate_a_b': 4.531, 'b_q_norm': 8.0, 'm_post_norm': 6.145}
    for name, (base, spread) in spreads.items():
        noise = np.random.default_rng([zlib.crc32(name.encode()), seed]).standard_normal(out[name].shape)
        drawn = base * np.exp(spread * noise) if base else spread * noise
        out[name] = __import__('jax').numpy.asarray(drawn.astype(out[name].dtype))
    for name, factor in factors.items():
        out[name] = (out[name] * factor).astype(out[name].dtype)
    return out
```

```python
from contextlib import ExitStack

import numpy as np
import concourse.bass as bass
from concourse import mybir

ALU = mybir.AluOpType
ACT = mybir.ActivationFunctionType
F32 = mybir.dt.float32
F32R = mybir.dt.float32r
I32 = mybir.dt.int32
AX_X = mybir.AxisListType.X

P = 128
D = 1024
KD = D // P
META, SEQ = 16, 256
T = META + SEQ
TB = [(0, 128), (128, 128), (256, 16)]
RNN = 1280
RB = RNN // P
HB = RB // 2
CONV = 4
HEADS, NOPE, ROPE, VD = 16, 64, 32, 64
QK = NOPE + ROPE
LORA, QLORA = 256, 384
KL, KQ = LORA // P, QLORA // P
FF = 3072
KF = FF // P
NE, TOPK = 8, 2
EF = 3584
NT = 512
UT = EF // NT
KE = EF // P
EPS = 1e-6

CHUNK = 2048
RAW, SPLIT = 6, 3
BANKS = 6

PARAM = {}
_n = 0
for _name, _w in (("a_pre", KD), ("conv_w", CONV * RB), ("conv_b", RB), ("ga_b", RB), ("gx_b", RB), ("lam", RB),
                  ("a_post", KD), ("kv_norm", KD), ("latent", KL), ("b_pre", KD), ("q_norm", KQ), ("b_post", KD),
                  ("f_pre", KD), ("f_post", KD), ("m_pre", KD), ("eps", 1), ("router_w", KD * NE)):
    PARAM[_name] = (_n, _n + _w)
    _n += _w
NPARAM = _n

CONST = {}
_n = 0
for _name, _w in (("ident", P), ("ones", P), ("tri", P), ("iota", P), ("valid", 3), ("expert", 3 * NE),
                  ("mask0", 128), ("mask1", 256), ("mask2", T), ("cos", T), ("sin", T)):
    CONST[_name] = (_n, _n + _w)
    _n += _w
NCONST = _n


def chunk_plan():
    plan = [("xr", j, KD * 256) for j in range(RB // 2)]
    plan += [("ga", 0, RB * P), ("gx", 0, RB * P)]
    plan += [("y", j, KD * 256) for j in range(RB // 2)]
    plan += [("a_out", j, RB * P) for j in range(KD)]
    for j in range(KF // 2):
        plan += [("f_gate", j, KD * 256), ("f_up", j, KD * 256)]
    plan += [("f_down", j, KD * 256) for j in range(12)]
    plan += [("dkv", 0, KD * LORA), ("dkr", 0, KD * ROPE), ("dq", 0, KD * 256), ("dq", 1, KD * 128)]
    plan += [("ukv", j, KL * D) for j in range(2)]
    plan += [("uq", j, KQ * 4 * QK) for j in range(4)]
    plan += [("b_out", j, KD * 256) for j in range(4)]
    return plan


PLAN = chunk_plan()
CH = {(name, j): n for n, (name, j, _) in enumerate(PLAN)}
NC0 = len(PLAN)
EC = 4 * UT + KE // 2
assert EC % RAW == 0 and EC % SPLIT == 0


def tile_plan():
    plan = [("hT", c, "V") for c in range(KD)]
    plan += [("st_a", 0, "A")] + [("xr", m, "A") for m in range(RB)]
    for half in range(2):
        plan += [(g, m, "A") for m in range(half * HB, half * HB + HB) for g in ("r", "i")]
    plan += [("y", m, "A") for m in range(RB)] + [("a_out", m, "A") for m in range(KD)] + [("st_ao", 0, "A")]
    plan += [("st_f", 0, "A")]
    for j in range(KF // 2):
        plan += [("f_g", 2 * j, "A"), ("f_g", 2 * j + 1, "A"), ("f_u", 2 * j, "V"), ("f_u", 2 * j + 1, "V")]
    plan += [("f_down", m, "A") for m in range(KD)] + [("st_fo", 0, "A")]
    plan += [("st_b", 0, "A")] + [("ckv", m, "A") for m in range(KL)] + [("krope", 0, "V")]
    plan += [("cq", m, "A") for m in range(KQ)] + [("st_ckv", 0, "A"), ("st_cq", 0, "A")]
    for half in range(2):
        plan += [("kn", 4 * half + m, "A") for m in range(4)] + [("v", (b, half), "A") for b in range(3)]
    for g in range(4):
        plan += [("qn", 2 * g, "A"), ("qn", 2 * g + 1, "A"), ("qro", g, "V"), ("qsw", g, "V")]
        for h in range(4 * g, 4 * g + 4):
            plan += [("s", (h, b), "V") for b in range(3)]
            if h:
                plan += [("pt", h - 1, "A"), ("o", h - 1, "A")]
    plan += [("pt", HEADS - 1, "A"), ("o", HEADS - 1, "A")]
    plan += [("b_out", m, "A") for m in range(KD)] + [("st_bo", 0, "A")]
    return plan


TILES = tile_plan()
TN = {(name, j): n for n, (name, j, _) in enumerate(TILES)}
EMPTIED = [sum(x[2] == TILES[n][2] for x in TILES[:n + 1]) for n in range(len(TILES))]


NORMS = ["st_a", "st_ao", "st_f", "st_fo", "st_b", "st_ckv", "st_cq", "st_bo"]



def pieces(name, k, src, dst):
    if name == "dkr":
        s = src[:, 0:k * ROPE].rearrange("p (k n) -> p k n", k=k)
        d = dst[:, 0:k * 3 * ROPE].rearrange("p (k n) -> p k n", k=k)
        h = ROPE // 2
        return [(d[:, :, 0:h], s[:, :, h:ROPE]), (d[:, :, h:ROPE], s[:, :, 0:h]),
                (d[:, :, ROPE:2 * ROPE], s), (d[:, :, 2 * ROPE:3 * ROPE], s)]
    if name == "uq":
        out = []
        for r in range(k):
            s = src[:, r * 4 * QK:(r + 1) * 4 * QK].rearrange("p (h n) -> p h n", h=4)
            d = dst[:, r * 512:(r + 1) * 512]
            n = d[:, 0:4 * NOPE].rearrange("p (h n) -> p h n", h=4)
            ro = d[:, 4 * NOPE:4 * QK].rearrange("p (h n) -> p h n", h=4)
            sw = d[:, 4 * QK:512].rearrange("p (h n) -> p h n", h=4)
            h = ROPE // 2
            out += [(n, s[:, :, 0:NOPE]), (ro, s[:, :, NOPE:QK]), (sw[:, :, 0:h], s[:, :, NOPE + h:QK]),
                    (sw[:, :, h:ROPE], s[:, :, NOPE:NOPE + h])]
        return out
    if name == "ukv":
        out = []
        for r in range(k):
            s = src[:, r * D:(r + 1) * D].rearrange("p (h n) -> p h n", h=8)
            for part in range(2):
                d = dst[:, r * D + 512 * part:r * D + 512 * part + 512].rearrange("p (h n) -> p h n", h=8)
                out.append((d, s[:, :, 64 * part:64 * part + 64]))
        return out
    return [(dst, src)]


def yoco_kernel(nc, w, params, consts, gain_rows, x_tok, out):
    with ExitStack() as ctx:
        def sb(name, shape, dt=F32, stack=None):
            return (stack or ctx).enter_context(nc.sbuf_tensor(name, shape, dt))

        def sem(name):
            return ctx.enter_context(nc.semaphore(name))

        raw = [sb(f"raw{i}", [P, CHUNK]) for i in range(RAW)]
        w_hi = [sb(f"w_hi{i}", [P, CHUNK], F32R) for i in range(SPLIT)]
        w_lo = [sb(f"w_lo{i}", [P, CHUNK], F32R) for i in range(SPLIT)]
        par = sb("par", [P, NPARAM])
        con = sb("con", [P, NCONST])
        small = sb("small", [P, 256])
        banks = [ctx.enter_context(nc.psum_tensor(f"bank{i}", [P, 512], F32)) for i in range(8)]

        def pr(name, c=None):
            a, b = PARAM[name]
            return par[:, a:b] if c is None else par[:, a + c:a + c + 1]

        def cn(name):
            a, b = CONST[name]
            return con[:, a:b]

        ident, ones, eps = cn("ident"), cn("ones"), pr("eps")

        body = ExitStack()
        hT = sb("hT", [P, KD, T], stack=body)
        rstd = sb("rstd", [P, T], stack=body)
        u_hi = sb("u_hi", [P, KD, T], F32R, stack=body)
        u_lo = sb("u_lo", [P, KD, T], F32R, stack=body)
        mix = sb("mix", [P, KD, T], stack=body)
        sq = sb("sq", [P, KD, T], stack=body)

        with ExitStack() as ph:
            x_in = sb("x_in", [P, 3, D], stack=ph)
        with ExitStack() as ph:
            xr_gy = sb("xr_gy", [P, RB, T + CONV - 1], stack=ph)
            xc = sb("xc", [P, RB, T], stack=ph)
            xc_hi = sb("xc_hi", [P, RB, T], F32R, stack=ph)
            xc_lo = sb("xc_lo", [P, RB, T], F32R, stack=ph)
            ig = sb("ig", [P, HB, T], stack=ph)
        r_la, th = mix[:, 0:HB, :], sq[:, 0:HB, :]
        with ExitStack() as ph:
            f_silu = sb("f_silu", [P, 2, T], stack=ph)
            f_h = sb("f_h", [P, 4, T], stack=ph)
            hid_hi = sb("hid_hi", [P, KF, T], F32R, stack=ph)
            hid_lo = sb("hid_lo", [P, KF, T], F32R, stack=ph)
        with ExitStack() as ph:
            ckv = sb("ckv", [P, KL, T], stack=ph)
            ckv_hi = sb("ckv_hi", [P, KL, 3 * P], F32R, stack=ph)
            ckv_lo = sb("ckv_lo", [P, KL, 3 * P], F32R, stack=ph)
            cq = sb("cq", [P, KQ, T], stack=ph)
            cq_hi = sb("cq_hi", [P, KQ, T], F32R, stack=ph)
            cq_lo = sb("cq_lo", [P, KQ, T], F32R, stack=ph)
            kT = sb("kT", [QK, HEADS, T], stack=ph)
            v_tok = sb("v_tok", [P, 3, D], stack=ph)
            qT = sb("qT", [QK, 4, T], stack=ph)
            rope_a = sb("rope_a", [P, T], stack=ph)
            s_sb = sb("s_sb", [P, 2, 656], stack=ph)
            pT = sb("pT", [P, 432], stack=ph)
        body.close()
        k_temp, rope_b = qT[:, 0, :], cq[:, 0, :]
        SC = [(0, 128), (128, 256), (384, T)]

        eh_hi = sb("eh_hi", [P, KE, P], F32R)
        h_tok = sb("h_tok", [P, 3, D])
        u_thi = sb("u_thi", [P, 3, D], F32R)
        u_tlo = sb("u_tlo", [P, 3, D], F32R)
        y_acc = sb("y_acc", [P, 3, D])
        x_hi = sb("x_hi", [P, KD, P], F32R)
        x_lo = sb("x_lo", [P, KD, P], F32R)
        eh_lo = sb("eh_lo", [P, KE, P], F32R)
        e_silu = sb("e_silu", [P, NT])
        e_h = sb("e_h", [P, 2, NT])
        sel = sb("sel", [P, 3, P], F32R)
        selT = sb("selT", [P, 3, P], F32R)
        grow = sb("grow", [P, D])
        rbias = sb("rbias", [P, NE])
        gw = sb("gw", [P, KD, NE])
        rt = sb("rt", [P, 10, 3 * NE])
        cur = sb("cur", [P, 8])
        rounds_i = sb("rounds_i", [1, 1], I32)
        y_hi, y_lo = (x[:].rearrange("p k n -> p (k n)") for x in (x_hi, x_lo))

        landed = [sem(f"landed{i}") for i in range(RAW)]
        hi_done, lo_done = sem("hi_done"), sem("lo_done")
        in_const, in_par, in_x, in_rows = sem("in_const"), sem("in_par"), sem("in_x"), sem("in_rows")
        pe_done = sem("pe_done")
        emptied = {"A": sem("emptied_by_act"), "V": sem("emptied_by_dve")}
        dve_step = sem("dve_step")
        sq_ready, norm_f32, act_hi, act_lo, res_done = (
            sem("sq_ready"), sem("norm_f32"), sem("act_hi"), sem("act_lo"), sem("res_done"))
        conv_done, xc_hi_done, xc_lo_done = sem("conv_done"), sem("xc_hi_done"), sem("xc_lo_done")
        lam_abs, lam_exp = sem("lam_abs"), sem("lam_exp")
        loga_ready, a_ready, root_in, root_done, scan_done = (
            sem("loga_ready"), sem("a_ready"), sem("root_in"), sem("root_done"), sem("scan_done"))
        z_f32, z_hi, z_lo = sem("z_f32"), sem("z_hi"), sem("z_lo")
        fhi_done, flo_done = sem("fhi_done"), sem("flo_done")
        krope_done, krope_copied, qrope_done = sem("krope_done"), sem("krope_copied"), sem("qrope_done")
        max_done, exp_done, prob_done = sem("max_done"), sem("exp_done"), sem("prob_done")
        gw_done, hsum_done, rstd_t = sem("gw_done"), sem("hsum_done"), sem("h_std_done")
        u_tok_done, logit_in, logit_exp, assigned = (
            sem("u_tok_done"), sem("logit_in"), sem("logit_exp"), sem("assigned"))
        rounds_ready = sem("rounds_ready")
        h_tok_done = sem("h_tok_done")
        sel_done, x_hi_done, x_lo_done, selT_done, gate_done = (
            sem("sel_done"), sem("x_hi_done"), sem("x_lo_done"), sem("selT_done"), sem("gate_done"))
        silu_done, eh_done, eh_hi_done, eh_lo_done = (
            sem("silu_done"), sem("eh_done"), sem("eh_hi_done"), sem("eh_lo_done"))
        y_hi_done, y_lo_done, added = sem("y_hi_done"), sem("y_lo_done"), sem("added")
        loop_step = sem("loop_step")
        fin_sum, fin_std, fin_done, out_written = (
            sem("fin_sum"), sem("fin_std"), sem("fin_done"), sem("out_written"))

        c8 = small[:, 0:RB]
        lt = [small[:, 16 * k + 16:16 * k + 16 + RB] for k in range(6)]
        smax, nbias, rsum, rcp = (small[:, 128 + 16 * k:128 + 16 * k + 6] for k in range(4))
        mss, mrs = small[:, 192:195], small[:, 208:211]

        def rows(a):
            return a.rearrange("(k p) n -> p k n", p=P)

        w_in, w_ao, w_gu, w_dn = (rows(w[n][0]) for n in ("a_w_in", "a_w_out", "f_w_gate_up", "f_w_down"))
        w_dq, w_uq, w_bo = (rows(w[n][0]) for n in ("b_w_dq", "b_w_uq", "b_w_o"))
        w_dkv, w_ukv = rows(w["kv_w_dkv"]), rows(w["kv_w_ukv"])
        ga, gx = (w[n][0].rearrange("n c d -> c n d") for n in ("a_gate_a_w", "a_gate_x_w"))

        def source(name, j):
            return {
                "xr": lambda: w_in[:, :, RNN + 256 * j:RNN + 256 * j + 256],
                "y": lambda: w_in[:, :, 256 * j:256 * j + 256],
                "ga": lambda: ga, "gx": lambda: gx,
                "a_out": lambda: w_ao[:, :, P * j:P * j + P],
                "f_gate": lambda: w_gu[:, :, 256 * j:256 * j + 256],
                "f_up": lambda: w_gu[:, :, FF + 256 * j:FF + 256 * j + 256],
                "f_down": lambda: w_dn[:, KD * (j % 3):KD * (j % 3) + KD, 256 * (j // 3):256 * (j // 3) + 256],
                "dkv": lambda: w_dkv[:, :, 0:LORA],
                "dkr": lambda: w_dkv[:, :, LORA:LORA + ROPE],
                "dq": lambda: w_dq[:, :, 256 * j:min(256 * j + 256, QLORA)],
                "ukv": lambda: w_ukv[:, :, D * j:D * j + D],
                "uq": lambda: w_uq[:, :, 4 * QK * j:4 * QK * (j + 1)],
                "b_out": lambda: w_bo[:, :, 256 * j:256 * j + 256],
            }[name]()

        def split_views(n, buf):
            name, j, cols = PLAN[n]
            k = source(name, j).shape[1]
            cols = {"dkr": KD * 3 * ROPE, "uq": KQ * 512}.get(name, cols)
            return buf[n % SPLIT][:, 0:cols].rearrange("p (k n) -> p k n", k=k)

        step = {}
        block = ctx.enter_context(nc.Block())

        @block.tensor
        def _(pe):
            count = [0]

            def mark(ins, *keys):
                ins.then_inc(pe_done, 1)
                count[0] += 1
                for key in keys:
                    step[key] = count[0]

            def bank_of(name, j):
                n = TN[(name, j)]
                if n >= BANKS:
                    pe.wait_ge(emptied[TILES[n - BANKS][2]], EMPTIED[n - BANKS])
                return banks[n % BANKS]

            def chunk(name, j):
                n = CH[(name, j)]
                pe.wait_ge(lo_done, n + 1)
                return split_views(n, w_hi), split_views(n, w_lo)

            def product(o, a, b, start, stop):
                nc.tensor.matmul(o, a[0], b[0], start=start, stop=False)
                nc.tensor.matmul(o, a[0], b[1], start=False, stop=False)
                return nc.tensor.matmul(o, a[1], b[0], start=False, stop=stop)

            def columns_tile(name, m, wc, c0, act, kn, width=P, *keys):
                ps = bank_of(name, m)
                for k in range(kn):
                    last = product(ps[0:width, 0:T], [x[:, k, c0:c0 + width] for x in wc],
                                   [x[:, k, 0:T] for x in act], k == 0, k == kn - 1)
                mark(last, ("tile", TN[(name, m)]), *keys)

            def sum_tile(name, src, kn):
                pe.wait_ge(sq_ready, NORMS.index(name) + 1)
                ps = bank_of(name, 0)
                for k in range(kn):
                    last = nc.tensor.matmul(ps[:, 0:T], ones, src[:, k, :], start=(k == 0), stop=(k == kn - 1))
                mark(last, ("tile", TN[(name, 0)]))

            u = (u_hi, u_lo)
            pe.wait_ge(in_const, 16)
            pe.wait_ge(in_x, 48)
            for c in range(KD):
                ps = bank_of("hT", c)
                for b, (t0, n) in enumerate(TB):
                    last = nc.tensor.transpose(ps[:, t0:t0 + n], x_in[0:n, b, c * P:(c + 1) * P], ident[0:n, 0:n])
                mark(last, ("tile", TN[("hT", c)]))
            sum_tile("st_a", sq, KD)
            pe.wait_ge(act_lo, 1)
            for j in range(RB // 2):
                wc = chunk("xr", j)
                for m in (2 * j, 2 * j + 1):
                    columns_tile("xr", m, wc, P * (m % 2), u, KD, P, *([("chunk", CH[("xr", j)])] if m % 2 else []))
            wa, wx = chunk("ga", 0), chunk("gx", 0)
            for m in range(RB):
                pe.wait_ge(xc_lo_done, m + 1)
                for name, wc, key in (("r", wa, "ga"), ("i", wx, "gx")):
                    ps = bank_of(name, m)
                    last = product(ps[:, 0:T], [x[:, m, :] for x in wc], (xc_hi[:, m, :], xc_lo[:, m, :]), True, True)
                    mark(last, ("tile", TN[(name, m)]), *([("chunk", CH[(key, 0)])] if m == RB - 1 else []))
            for j in range(RB // 2):
                wc = chunk("y", j)
                for m in (2 * j, 2 * j + 1):
                    columns_tile("y", m, wc, P * (m % 2), u, KD, P, *([("chunk", CH[("y", j)])] if m % 2 else []))
            pe.wait_ge(z_lo, 2)
            for m in range(KD):
                columns_tile("a_out", m, chunk("a_out", m), 0, (xc_hi, xc_lo), RB, P, ("chunk", CH[("a_out", m)]))
            sum_tile("st_ao", sq, KD)
            sum_tile("st_f", sq, KD)
            pe.wait_ge(act_lo, 2)
            for j in range(KF // 2):
                for name, key in (("f_g", "f_gate"), ("f_u", "f_up")):
                    wc = chunk(key, j)
                    for m in (2 * j, 2 * j + 1):
                        columns_tile(name, m, wc, P * (m % 2), u, KD, P, *([("chunk", CH[(key, j)])] if m % 2 else []))
            pe.wait_ge(flo_done, KF)
            for q in range(KD // 2):
                ps = [bank_of("f_down", 2 * q + i) for i in range(2)]
                for r in range(3):
                    wc = chunk("f_down", 3 * q + r)
                    for i in range(2):
                        for k in range(KD):
                            f = KD * r + k
                            last = product(ps[i][:, 0:T], [x[:, k, P * i:P * i + P] for x in wc],
                                           (hid_hi[:, f, :], hid_lo[:, f, :]), f == 0, f == KF - 1)
                        if r == 2:
                            mark(last, ("tile", TN[("f_down", 2 * q + i)]),
                                 *([("chunk", CH[("f_down", 3 * q + r)])] if i else []))
                    if r < 2:
                        mark(last, ("chunk", CH[("f_down", 3 * q + r)]))
            sum_tile("st_fo", sq, KD)
            sum_tile("st_b", sq, KD)
            pe.wait_ge(act_lo, 3)
            wc = chunk("dkv", 0)
            for m in range(KL):
                columns_tile("ckv", m, wc, P * m, u, KD, P, *([("chunk", CH[("dkv", 0)])] if m else []))
            columns_tile("krope", 0, chunk("dkr", 0), 0, u, KD, QK, ("chunk", CH[("dkr", 0)]))
            pe.wait_ge(act_lo, 4)
            for m in range(KQ):
                columns_tile("cq", m, chunk("dq", m // 2), P * (m % 2), u, KD, P,
                             *([("chunk", CH[("dq", m // 2)])] if m else []))
            sum_tile("st_ckv", sq, KL)
            sum_tile("st_cq", sq[:, KL:KL + KQ, :], KQ)
            pe.wait_ge(act_lo, 5)
            for half in range(2):
                wc = chunk("ukv", half)
                for m in range(4 * half, 4 * half + 4):
                    columns_tile("kn", m, wc, P * (m % 4), (ckv_hi, ckv_lo), KL)
                for b, (t0, n) in enumerate(TB):
                    ps = bank_of("v", (b, half))
                    for k in range(KL):
                        last = product(ps[:, :], [x[:, k, t0:t0 + P] for x in (ckv_hi, ckv_lo)],
                                       [x[:, k, 512:1024] for x in wc], k == 0, k == KL - 1)
                    mark(last, ("tile", TN[("v", (b, half))]), *([("chunk", CH[("ukv", half)])] if b == 2 else []))

            def weigh(h):
                pe.wait_ge(prob_done, h + 1)
                ps = bank_of("pt", h)
                p = s_sb[:, h % 2, :]
                for b, (t0, n) in enumerate(TB):
                    for kb in range(b + 1):
                        c, kn = SC[b][0] + P * kb, TB[kb][1]
                        o = (0, 144, 160)[kb] + t0
                        last = nc.tensor.transpose(ps[0:kn, o:o + n], p[0:n, c:c + kn], ident[0:n, 0:n])
                mark(last, ("tile", TN[("pt", h)]))
                ps = bank_of("o", h)
                pe.wait_ge(emptied["A"], EMPTIED[TN[("pt", h)]])
                for kb, (t0, kn) in enumerate(TB):
                    o = (0, 144, 160)[kb] + t0
                    last = nc.tensor.matmul(ps[0:VD, t0:T], v_tok[0:kn, kb, VD * h:VD * h + VD], pT[0:kn, o:o + T - t0],
                                            start=(kb == 0), stop=(kb == 2))
                mark(last, ("tile", TN[("o", h)]))

            pe.wait_ge(act_lo, 6)
            for g in range(4):
                wc = chunk("uq", g)
                for i, (name, m) in enumerate((("qn", 2 * g), ("qn", 2 * g + 1), ("qro", g), ("qsw", g))):
                    columns_tile(name, m, wc, P * i, (cq_hi, cq_lo), KQ, P, *([("chunk", CH[("uq", g)])] if i == 3 else []))
                for h in range(4 * g, 4 * g + 4):
                    if h % 4 == 0:
                        pe.wait_ge(emptied["A"], EMPTIED[TN[("qn", 2 * g + 1)]])
                        pe.wait_ge(qrope_done, g + 1)
                        pe.wait_ge(krope_copied, 1)
                    for b, (t0, n) in enumerate(TB):
                        ps = bank_of("s", (h, b))
                        mark(nc.tensor.matmul(ps[0:n, 0:SC[b][1]], qT[:, h % 4, t0:t0 + n], kT[:, h, 0:SC[b][1]],
                                              start=True, stop=True), ("tile", TN[("s", (h, b))]))
                    if h:
                        weigh(h - 1)
            weigh(HEADS - 1)
            pe.wait_ge(act_lo, 7)
            for j in range(4):
                wc = chunk("b_out", j)
                for m in (2 * j, 2 * j + 1):
                    columns_tile("b_out", m, wc, P * (m % 2), u, KD, P, *([("chunk", CH[("b_out", j)])] if m % 2 else []))
            sum_tile("st_bo", sq, KD)

            pe.wait_ge(res_done, 3)
            for b, (t0, n) in enumerate(TB):
                for half in range(2):
                    for c in range(4):
                        last = nc.tensor.transpose(banks[2 * b + half][0:n, P * c:P * c + P],
                                                   hT[:, 4 * half + c, t0:t0 + n], ident)
                    mark(last, ("h_tok", b, half))
            pe.wait_ge(gw_done, 1)
            for b, (t0, n) in enumerate(TB):
                for k in range(KD):
                    last = nc.tensor.matmul(banks[6][0:n, NE * b:NE * b + NE], hT[:, k, t0:t0 + n], gw[:, k, :],
                                            start=(k == 0), stop=(k == KD - 1))
            mark(last, "logits")
            pe.wait_ge(assigned, 1)
            a = rt[:, 0, :]
            for b in range(3):
                for bb in range(b + 1):
                    last = nc.tensor.matmul(banks[7][:, NE * b:NE * b + NE], cn("tri") if bb == b else ones,
                                            a[:, NE * bb:NE * bb + NE], start=(bb == 0), stop=(bb == b))
            for bb in range(3):
                last = nc.tensor.matmul(banks[7][:, 3 * NE:4 * NE], ones, a[:, NE * bb:NE * bb + NE],
                                        start=(bb == 0), stop=(bb == 2))
            mark(last, "positions")
            pe.wait_ge(h_tok_done, 6)
            pe.wait_ge(u_tok_done, 1)
            pe.wait_ge(rounds_ready, 1)
            rounds = pe.value_load(rounds_i[0:1, 0:1], min_val=1, max_val=3)
            base = step["loop"] = count[0]

            def expert(it):
                def emark(ins, *keys):
                    mark(ins, *(("e",) + key for key in keys))

                def echunk(c):
                    pe.wait_ge(lo_done, it * EC + (NC0 + c + 1))
                    s = (NC0 + c) % SPLIT
                    k = 4 if c < 4 * UT else 2
                    return [x[s][:].rearrange("p (k n) -> p k n", k=k) for x in (w_hi, w_lo)]

                pe.wait_ge(sel_done, it + 1)
                for part, src in enumerate((u_thi, u_tlo)):
                    for k in range(KD):
                        for b in range(3):
                            last = nc.tensor.matmul(banks[2 * part + k // 4][:, P * (k % 4):P * (k % 4) + P],
                                                    src[:, b, P * k:P * k + P], sel[:, b, :],
                                                    start=(b == 0), stop=(b == 2))
                    emark(last, ("x", part))
                for b in range(3):
                    last = nc.tensor.transpose(banks[6][:, P * b:P * b + P], sel[:, b, :].bitcast(F32), ident)
                emark(last, ("selT",))
                for b in range(3):
                    last = nc.tensor.matmul(banks[7][:, 0:1], sel[:, b, :].bitcast(F32), cur[:, 3 + b:4 + b],
                                            start=(b == 0), stop=(b == 2))
                emark(last, ("gate",))
                pe.wait_ge(x_hi_done, it + 1)
                pe.wait_ge(x_lo_done, it + 1)

                def turn(j):
                    pe.wait_ge(eh_done, it * UT + (j + 1))
                    if j:
                        pe.wait_ge(eh_lo_done, it * UT + j)
                    else:
                        pe.wait_ge(selT_done, it + 1)
                    for f in range(4):
                        last = nc.tensor.transpose(banks[6][:, P * f:P * f + P], e_h[:, j % 2, P * f:P * f + P], ident)
                    emark(last, ("turned", j))

                for j in range(UT):
                    if j >= 2:
                        pe.wait_ge(eh_done, it * UT + (j - 1))
                    for g in range(2):
                        ps = banks[2 * (j % 2) + g]
                        for kh in range(2):
                            c = 4 * j + 2 * g + kh
                            wc = echunk(c)
                            for k in range(4):
                                kk = 4 * kh + k
                                last = product(ps[:, :], (x_hi[:, kk, :], x_lo[:, kk, :]), [x[:, k, :] for x in wc],
                                               kk == 0, kk == KD - 1)
                            emark(last, ("chunk", c), *([("up", j)] if g and kh else []))
                    if j:
                        turn(j - 1)
                for d in range(KE // 2):
                    wc = echunk(4 * UT + d)
                    if d == 0:
                        pe.wait_ge(y_lo_done, it)
                    if d == 3:
                        turn(UT - 1)
                    pe.wait_ge(eh_lo_done, it * UT + ((2 * d + 1) // 4 + 1))
                    for n in range(2):
                        for f in range(2):
                            ff = 2 * d + f
                            last = product(banks[4 + n][:, :], (eh_hi[:, ff, :], eh_lo[:, ff, :]),
                                           [x[:, f, NT * n:NT * n + NT] for x in wc], ff == 0, ff == KE - 1)
                    emark(last, ("chunk", 4 * UT + d))
                pe.wait_ge(eh_done, (it + 1) * UT)
                pe.wait_ge(gate_done, it + 1)
                pe.wait_ge(y_lo_done, it + 1)
                for b in range(3):
                    for n in range(2):
                        ps = banks[(0, 1, 2, 3, 6, 7)[2 * b + n]]
                        for part, y in enumerate((y_hi, y_lo)):
                            last = nc.tensor.matmul(ps[:, :], selT[:, b, :], y[:, NT * n:NT * n + NT],
                                                    start=(part == 0), stop=(part == 1))
                        emark(last, ("scattered", 2 * b + n))
                pe.wait_ge(added, (it + 1) * 6)

            with pe.Fori(0, rounds) as r:
                with pe.Fori(0, NE) as e:
                    expert(r * NE + e)
            step["per_expert"] = count[0] - base

        def at(eng, *key):
            eng.wait_ge(pe_done, step[key if len(key) > 1 else key[0]])

        def at_tile(eng, name, j):
            at(eng, "tile", TN[(name, j)])
            return banks[TN[(name, j)] % BANKS]

        def at_expert(eng, it, *key):
            eng.wait_ge(pe_done, it * step["per_expert"] + step[("e",) + key])

        def slot_free(eng, n):
            if n >= SPLIT:
                at(eng, "chunk", n - SPLIT)

        def slot_free_in_loop(eng, it, c):
            if c >= SPLIT:
                at_expert(eng, it, "chunk", c - SPLIT)
            else:
                eng.wait_ge(pe_done, it * step["per_expert"] + (step[("e", "chunk", EC + c - SPLIT)] - step["per_expert"]))

        @block.sync
        def _(sp):
            sp.dma_start(con[:], consts).then_inc(in_const, 16)
            for b, (t0, n) in enumerate(TB):
                sp.dma_start(x_in[0:n, b, :], x_tok[t0:t0 + n, :]).then_inc(in_x, 16)
            sp.dma_start(par[:], params).then_inc(in_par, 16)

            for n, (name, j, cols) in enumerate(PLAN):
                if n >= RAW:
                    sp.wait_ge(lo_done, n - RAW + 1)
                src = source(name, j)
                sp.dma_start(raw[n % RAW][:, 0:cols].rearrange("p (k n) -> p k n", k=src.shape[1]), src)\
                    .then_inc(landed[n % RAW], 16)

            def expert_loads(it, e):
                up = w["m_w_gate_up"][0, bass.ds(e, 1)].rearrange("a (k p) n -> p (a k) n", p=P)
                dn = w["m_w_down"][0, bass.ds(e, 1)].rearrange("a (k p) n -> p (a k) n", p=P)
                for c in range(EC):
                    slot = (NC0 + c) % RAW
                    sp.wait_ge(lo_done, it * EC + (NC0 + c - RAW + 1))
                    if c < 4 * UT:
                        j, g, kh = c // 4, c // 2 % 2, c % 2
                        src = up[:, 4 * kh:4 * kh + 4, EF * g + NT * j:EF * g + NT * j + NT]
                    else:
                        f = 2 * (c - 4 * UT)
                        src = dn[:, f:f + 2, :]
                    sp.dma_start(raw[slot][:].rearrange("p (k n) -> p k n", k=src.shape[1]), src)\
                        .then_inc(landed[slot], 16)

            with sp.Fori(0, NE) as e:
                expert_loads(e, e)
            sp.wait_ge(rounds_ready, 1)
            rounds = sp.value_load(rounds_i[0:1, 0:1], min_val=1, max_val=3)
            with sp.If(rounds > 1):
                with sp.Fori(1, rounds) as r:
                    with sp.Fori(0, NE) as e:
                        expert_loads(r * NE + e, e)
            sp.wait_ge(fin_done, 3)
            sp.dma_start(out[0:P - META, :], y_acc[META:P, 0, :]).then_inc(out_written, 16)
            sp.dma_start(out[P - META:2 * P - META, :], y_acc[:, 1, :]).then_inc(out_written, 16)
            sp.dma_start(out[2 * P - META:SEQ, :], y_acc[0:META, 2, :]).then_inc(out_written, 16)
            sp.wait_ge(out_written, 48)

        @block.gpsimd
        def _(pool):
            pool.wait_ge(krope_done, 1)
            nc.gpsimd.tensor_copy(kT[NOPE:QK, :, :], rope_a[NOPE:QK, None, :].to_broadcast([ROPE, HEADS, T]))\
                .then_inc(krope_copied, 1)
            pool.wait_ge(res_done, 3)
            pool.dma_start(y_acc[:, 0, :], gain_rows[0:1, 0:D].to_broadcast([P, D])).then_inc(in_rows, 16)
            pool.dma_start(grow[:], gain_rows[0:1, D:2 * D].to_broadcast([P, D])).then_inc(in_rows, 16)
            pool.dma_start(rbias[:], gain_rows[0:1, 2 * D:2 * D + NE].to_broadcast([P, NE])).then_inc(in_rows, 16)

        @block.scalar
        def _(act):
            issued = [0]

            def ahead(n):
                while issued[0] <= min(n, NC0 - 1):
                    c = issued[0]
                    name, j, cols = PLAN[c]
                    act.wait_ge(landed[c % RAW], 16 * (c // RAW + 1))
                    slot_free(act, c)
                    src, dst = raw[c % RAW][:, 0:cols], w_hi[c % SPLIT]
                    dst = dst[:, 0:cols] if name not in ("dkr", "uq") else dst[:, :]
                    for d, s in pieces(name, source(name, j).shape[1], src, dst):
                        last = nc.scalar.copy(d, s)
                    last.then_inc(hi_done, 1)
                    issued[0] += 1

            def empty(name, j, dst, func=ACT.Copy, rows=None, **kw):
                ps = at_tile(act, name, j)
                nc.scalar.activation(dst, ps[rows or slice(0, P), 0:dst.shape[-1]], func, **kw)\
                    .then_inc(emptied["A"], 1)

            def squares(name, dst, src):
                nc.scalar.activation(dst, src, ACT.Square).then_inc(sq_ready, 1)

            def root(name, n):
                empty(name, 0, rstd[:, :], ACT.Sqrt, bias=eps, scale=1.0 / n)

            def rounded(n, dst, src):
                act.wait_ge(norm_f32, n)
                nc.scalar.copy(dst, src).then_inc(act_hi, 1)

            ahead(1)
            act.wait_ge(emptied["V"], KD)
            squares("st_a", sq[:], hT[:])
            ahead(2)
            act.wait_ge(in_par, 16)
            root("st_a", D)
            act.wait_ge(lam_abs, 1)
            nc.scalar.activation(lt[2], lt[1], ACT.Exp, scale=-1.0).then_inc(lam_exp, 1)
            rounded(1, u_hi[:], sq[:])
            done_conv = 0
            for j in range(RB // 2):
                ahead(CH[("xr", j)] + 2)
                for m in (2 * j, 2 * j + 1):
                    empty("xr", m, xr_gy[:, m, CONV - 1:])
                for m in range(2 * j - 2, 2 * j) if j else ():
                    act.wait_ge(conv_done, m + 1)
                    nc.scalar.copy(xc_hi[:, m, :], xc[:, m, :]).then_inc(xc_hi_done, 1)
            for m in (RB - 2, RB - 1):
                act.wait_ge(conv_done, m + 1)
                nc.scalar.copy(xc_hi[:, m, :], xc[:, m, :]).then_inc(xc_hi_done, 1)
            for half in range(2):
                if half:
                    act.wait_ge(scan_done, 1)
                for i in range(HB):
                    m = half * HB + i
                    empty("r", m, r_la[:, i, :], ACT.Sigmoid, bias=pr("ga_b", m))
                    empty("i", m, ig[:, i, :], ACT.Sigmoid, bias=pr("gx_b", m))
                if half:
                    ahead(CH[("y", 0)] + 2)
                act.wait_ge(loga_ready, half + 1)
                nc.scalar.activation(th, r_la, ACT.Tanh)
                nc.scalar.activation(r_la, r_la, ACT.Exp).then_inc(a_ready, 1)
                act.wait_ge(root_in, half + 1)
                nc.scalar.activation(th, th, ACT.Sqrt, scale=-1.0).then_inc(root_done, 1)
            for j in range(RB // 2):
                ahead(CH[("y", j)] + 2)
                for m in (2 * j, 2 * j + 1):
                    empty("y", m, xr_gy[:, m, 0:T], ACT.Gelu_apprx_tanh)
            for half in range(2):
                act.wait_ge(z_f32, half + 1)
                nc.scalar.copy(xc_hi[:, half * HB:half * HB + HB, :], xc[:, half * HB:half * HB + HB, :])\
                    .then_inc(z_hi, 1)
            for m in range(KD):
                ahead(CH[("a_out", m)] + 2)
                empty("a_out", m, mix[:, m, :])
            act.wait_ge(emptied["A"], EMPTIED[TN[("a_out", KD - 1)]])
            squares("st_ao", sq[:], mix[:])
            root("st_ao", D)
            act.wait_ge(res_done, 1)
            squares("st_f", sq[:], hT[:])
            root("st_f", D)
            rounded(2, u_hi[:], sq[:])

            def f_round(m):
                act.wait_ge(emptied["V"], EMPTIED[TN[("f_u", m)]])
                nc.scalar.copy(hid_hi[:, m, :], f_h[:, m % 4, :]).then_inc(fhi_done, 1)

            for j in range(KF // 2):
                ahead(CH[("f_gate", j)] + 2)
                for m in (2 * j, 2 * j + 1):
                    if m >= 2:
                        act.wait_ge(emptied["V"], EMPTIED[TN[("f_u", m - 2)]])
                    empty("f_g", m, f_silu[:, m % 2, :], ACT.Silu)
                ahead(CH[("f_up", j)] + 2)
                if j:
                    f_round(2 * j - 2)
                    f_round(2 * j - 1)
            f_round(KF - 2)
            f_round(KF - 1)
            for q in range(KD // 2):
                for r in range(3):
                    ahead(CH[("f_down", 3 * q + r)] + 2)
                for m in (2 * q, 2 * q + 1):
                    empty("f_down", m, mix[:, m, :])
            act.wait_ge(emptied["A"], EMPTIED[TN[("f_down", KD - 1)]])
            squares("st_fo", sq[:], mix[:])
            root("st_fo", D)
            act.wait_ge(res_done, 2)
            squares("st_b", sq[:], hT[:])
            root("st_b", D)
            rounded(3, u_hi[:], sq[:])
            ahead(CH[("dkv", 0)] + 2)
            for m in range(KL):
                empty("ckv", m, ckv[:, m, :])
            ahead(CH[("dkr", 0)] + 2)
            at(act, "tile", TN[("krope", 0)])
            rounded(4, u_hi[:], mix[:])
            ahead(CH[("dq", 0)] + 2)
            for m in range(KQ):
                empty("cq", m, cq[:, m, :])
            act.wait_ge(act_lo, 3)
            act.wait_ge(emptied["A"], EMPTIED[TN[("cq", KQ - 1)]])
            squares("st_ckv", sq[:, 0:KL, :], ckv[:])
            squares("st_cq", sq[:, KL:KL + KQ, :], cq[:])
            root("st_ckv", LORA)
            act.wait_ge(norm_f32, 5)
            root("st_cq", QLORA)
            rounded(5, ckv_hi[:, :, 0:T], ckv[:])
            rounded(6, cq_hi[:], cq[:])
            for half in range(2):
                ahead(CH[("ukv", half)] + 2)
                for m in range(4 * half, 4 * half + 4):
                    ps = at_tile(act, "kn", m)
                    nc.scalar.copy(kT[0:NOPE, 2 * m, :], ps[0:NOPE, 0:T])
                    nc.scalar.copy(kT[0:NOPE, 2 * m + 1, :], ps[NOPE:P, 0:T]).then_inc(emptied["A"], 1)
                for b, (t0, n) in enumerate(TB):
                    empty("v", (b, half), v_tok[0:n, b, 512 * half:512 * half + 512], rows=slice(0, n))

            def take_weighed(h):
                ps = at_tile(act, "pt", h)
                if h:
                    at(act, "tile", TN[("o", h - 1)])
                nc.scalar.copy(pT[:, 0:416], ps[:, 0:416])
                nc.scalar.copy(pT[0:META, 416:432], ps[0:META, 416:432]).then_inc(emptied["A"], 1)
                r = VD * (h % 2)
                empty("o", h, sq[r:r + VD, h // 2, :], rows=slice(0, VD))

            for g in range(4):
                ahead(CH[("uq", g)] + 2)
                for m in (2 * g, 2 * g + 1):
                    ps = at_tile(act, "qn", m)
                    i = 2 * (m % 2)
                    nc.scalar.copy(qT[0:NOPE, i, :], ps[0:NOPE, 0:T])
                    nc.scalar.copy(qT[0:NOPE, i + 1, :], ps[NOPE:P, 0:T]).then_inc(emptied["A"], 1)
                for h in range(4 * g, 4 * g + 4):
                    act.wait_ge(max_done, h + 1)
                    for b, (t0, n) in enumerate(TB):
                        c, kn = SC[b]
                        i = 3 * (h % 2) + b
                        last = nc.scalar.activation(s_sb[0:n, h % 2, c:c + kn], s_sb[0:n, h % 2, c:c + kn], ACT.Exp,
                                                    bias=nbias[0:n, i:i + 1], scale=QK ** -0.5,
                                                    accum_out=rsum[0:n, i:i + 1])
                    last.then_inc(exp_done, 1)
                    if h:
                        take_weighed(h - 1)
            take_weighed(HEADS - 1)
            act.wait_ge(emptied["A"], EMPTIED[TN[("o", HEADS - 1)]])
            nc.scalar.copy(u_hi[:], sq[:]).then_inc(act_hi, 1)
            for j in range(4):
                ahead(CH[("b_out", j)] + 2)
                for m in (2 * j, 2 * j + 1):
                    empty("b_out", m, mix[:, m, :])
            act.wait_ge(emptied["A"], EMPTIED[TN[("b_out", KD - 1)]])
            act.wait_ge(act_lo, 7)
            squares("st_bo", sq[:], mix[:])
            root("st_bo", D)

            for b, (t0, n) in enumerate(TB):
                for half in range(2):
                    at(act, "h_tok", b, half)
                    nc.scalar.copy(h_tok[0:n, b, 512 * half:512 * half + 512], banks[2 * b + half][0:n, :])\
                        .then_inc(h_tok_done, 1)
            act.wait_ge(h_tok_done, 6)
            for b, (t0, n) in enumerate(TB):
                nc.scalar.activation(y_acc[0:n, 1, :], h_tok[0:n, b, :], ACT.Square,
                                     accum_out=mss[0:n, b:b + 1]).then_inc(hsum_done, 1)
                act.wait_ge(hsum_done, b + 1)
            nc.scalar.activation(mrs, mss, ACT.Sqrt, bias=eps, scale=1.0 / D).then_inc(rstd_t, 1)
            act.wait_ge(logit_in, 1)
            nc.scalar.activation(rt[:, 2, :], rt[:, 2, :], ACT.Exp).then_inc(logit_exp, 1)
            act.wait_ge(rounds_ready, 1)
            rounds = act.value_load(rounds_i[0:1, 0:1], min_val=1, max_val=3)

            def expert(it):
                def split(c):
                    slot = (NC0 + c) % RAW
                    act.wait_ge(landed[slot], it * (16 * EC // RAW) + 16 * ((NC0 + c) // RAW + 1))
                    slot_free_in_loop(act, it, c)
                    nc.scalar.copy(w_hi[(NC0 + c) % SPLIT][:], raw[slot][:]).then_inc(hi_done, 1)

                def silu(j):
                    at_expert(act, it, "up", j)
                    act.wait_ge(eh_done, it * UT + j)
                    nc.scalar.activation(e_silu[:], banks[2 * (j % 2)][:, :], ACT.Silu).then_inc(silu_done, 1)

                def round_hidden(j):
                    at_expert(act, it, "turned", j)
                    nc.scalar.copy(eh_hi[:, 4 * j:4 * j + 4, :], banks[6][:, :].rearrange("p (f n) -> p f n", f=4))\
                        .then_inc(eh_hi_done, 1)

                split(0)
                at_expert(act, it, "x", 0)
                xf = x_hi[:].rearrange("p k n -> p (k n)")
                nc.scalar.copy(xf[:, 0:512], banks[0][:, :])
                nc.scalar.copy(xf[:, 512:1024], banks[1][:, :]).then_inc(x_hi_done, 1)
                at_expert(act, it, "selT")
                nc.scalar.copy(selT[:], banks[6][:, 0:3 * P].rearrange("p (b n) -> p b n", b=3))\
                    .then_inc(selT_done, 1)
                for c in range(1, EC):
                    split(c)
                    if c >= 5 and (c - 5) % 4 == 0 and (c - 5) // 4 < UT:
                        silu((c - 5) // 4)
                    if c >= 9 and (c - 9) % 4 == 0 and (c - 9) // 4 < UT:
                        round_hidden((c - 9) // 4)
                at_expert(act, it, "chunk", EC - 1)
                act.wait_ge(gate_done, it + 1)
                for n in range(2):
                    last = nc.scalar.activation(y_hi[:, NT * n:NT * n + NT], banks[4 + n][:, :], ACT.Copy,
                                                scale=cur[:, 6:7])
                last.then_inc(y_hi_done, 1)

            with act.Fori(0, rounds) as r:
                with act.Fori(0, NE) as e:
                    expert(r * NE + e)

            act.wait_ge(added, rounds * (NE * 6))
            act.wait_ge(u_tok_done, 1)
            for b, (t0, n) in enumerate(TB):
                for half in range(2):
                    i = 2 * b + half
                    nc.scalar.activation(e_h[0:n, half, :], y_acc[0:n, b, 512 * half:512 * half + 512],
                                         ACT.Square, accum_out=small[0:n, 220 + i:221 + i]).then_inc(fin_sum, 1)
                    act.wait_ge(fin_sum, i + 1)
            act.wait_ge(fin_std, 1)
            nc.scalar.activation(mrs, mss, ACT.Sqrt, bias=eps, scale=1.0 / D).then_inc(fin_std, 1)

        @block.vector
        def _(dve):
            issued = [0]
            steps = [0]

            def link(ins):
                ins.then_inc(dve_step, 1)
                steps[0] += 1
                dve.wait_ge(dve_step, steps[0])

            def ahead(n):
                while issued[0] <= min(n, NC0 - 1):
                    c = issued[0]
                    name, j, cols = PLAN[c]
                    dve.wait_ge(hi_done, c + 1)
                    k = source(name, j).shape[1]
                    full = name in ("dkr", "uq")
                    src, hi, lo = raw[c % RAW][:, 0:cols], w_hi[c % SPLIT][:], w_lo[c % SPLIT][:]
                    if not full:
                        hi, lo = hi[:, 0:cols], lo[:, 0:cols]
                    for (d, s), (h, _) in zip(pieces(name, k, src, lo), pieces(name, k, src, hi.bitcast(F32))):
                        last = nc.vector.tensor_tensor(d, s, h, ALU.subtract)
                    last.then_inc(lo_done, 1)
                    issued[0] += 1

            def reciprocal_of_root(name):
                dve.wait_ge(emptied["A"], EMPTIED[TN[(name, 0)]])
                link(nc.vector.reciprocal(rstd[:, :], rstd[:, :]))

            def normalise(dst, src, gain, kn):
                for k in range(kn):
                    last = nc.vector.scalar_tensor_tensor(out=dst[:, k, :], in0=src[:, k, :], scalar=pr(gain, k),
                                                          in1=rstd[:, :], op0=ALU.mult, op1=ALU.mult)
                return last

            def remainder(n, dst, src, hi):
                dve.wait_ge(act_hi, n)
                nc.vector.tensor_tensor(dst, src, hi.bitcast(F32), ALU.subtract).then_inc(act_lo, 1)

            def residual(name, gain):
                reciprocal_of_root(name)
                link(normalise(sq, mix, gain, KD))
                nc.vector.tensor_tensor(hT[:], hT[:], sq[:], ALU.add).then_inc(res_done, 1)

            link(nc.vector.memset(small[:], 0.0))
            for c in range(KD):
                ps = at_tile(dve, "hT", c)
                nc.vector.tensor_copy(hT[:, c, :], ps[:, 0:T]).then_inc(emptied["V"], 1)
            link(nc.vector.memset(xr_gy[:, :, 0:CONV - 1], 0.0))
            ahead(1)
            dve.wait_ge(in_par, 16)
            link(nc.vector.tensor_scalar(lt[0], pr("lam"), -1.0, None, ALU.mult))
            nc.vector.tensor_tensor(lt[1], pr("lam"), lt[0], ALU.max).then_inc(lam_abs, 1)
            reciprocal_of_root("st_a")
            normalise(sq, hT, "a_pre", KD).then_inc(norm_f32, 1)
            remainder(1, u_lo[:], sq[:], u_hi[:])
            ahead(2)
            dve.wait_ge(lam_exp, 1)
            link(nc.vector.tensor_scalar(lt[3], lt[2], 2.0, None, ALU.add))
            link(nc.vector.reciprocal(lt[3], lt[3]))
            link(nc.vector.tensor_tensor(lt[3], lt[2], lt[3], ALU.mult))
            link(nc.vector.tensor_tensor(lt[4], lt[3], lt[3], ALU.mult))
            link(nc.vector.tensor_scalar(lt[5], lt[4], 1.0 / 19, None, ALU.mult))
            for d in (17, 15, 13, 11, 9, 7, 5, 3):
                link(nc.vector.scalar_tensor_tensor(out=lt[5], in0=lt[5], scalar=1.0 / d, in1=lt[4],
                                                    op0=ALU.add, op1=ALU.mult))
            link(nc.vector.scalar_tensor_tensor(out=lt[5], in0=lt[5], scalar=1.0, in1=lt[3], op0=ALU.add, op1=ALU.mult))
            link(nc.vector.tensor_scalar(lt[0], lt[0], 0.0, None, ALU.max))
            link(nc.vector.scalar_tensor_tensor(out=c8, in0=lt[5], scalar=2.0, in1=lt[0], op0=ALU.mult, op1=ALU.add))
            link(nc.vector.tensor_scalar(c8, c8, -8.0, None, ALU.mult))

            def conv(m):
                dve.wait_ge(emptied["A"], EMPTIED[TN[("xr", m)]])
                link(nc.vector.tensor_scalar(xc[:, m, :], xr_gy[:, m, 0:T], pr("conv_w", m), pr("conv_b", m),
                                             ALU.mult, ALU.add))
                for k in range(1, CONV):
                    ins = nc.vector.scalar_tensor_tensor(out=xc[:, m, :], in0=xr_gy[:, m, k:k + T],
                                                         scalar=pr("conv_w", RB * k + m), in1=xc[:, m, :],
                                                         op0=ALU.mult, op1=ALU.add)
                    if k < CONV - 1:
                        link(ins)
                ins.then_inc(conv_done, 1)

            def conv_low(m):
                dve.wait_ge(xc_hi_done, m + 1)
                nc.vector.tensor_tensor(xc_lo[:, m, :], xc[:, m, :], xc_hi[:, m, :].bitcast(F32), ALU.subtract)\
                    .then_inc(xc_lo_done, 1)

            for j in range(RB // 2):
                ahead(CH[("xr", j)] + 2)
                conv(2 * j)
                conv(2 * j + 1)
                if j:
                    conv_low(2 * j - 2)
                    conv_low(2 * j - 1)
            conv_low(RB - 2)
            conv_low(RB - 1)
            for half in range(2):
                hs = slice(half * HB, half * HB + HB)
                dve.wait_ge(emptied["A"], EMPTIED[TN[("i", half * HB + HB - 1)]])
                if half:
                    ahead(CH[("y", 0)] + 2)
                nc.vector.tensor_tensor(r_la, r_la, c8[:, hs, None].to_broadcast([P, HB, T]), ALU.mult)\
                    .then_inc(loga_ready, 1)
                link(nc.vector.tensor_tensor(ig[:], ig[:], xc[:, hs, :], ALU.mult))
                dve.wait_ge(a_ready, half + 1)
                link(nc.vector.tensor_tensor(xc[:, hs, :], r_la, r_la, ALU.mult))
                nc.vector.scalar_tensor_tensor(out=th, in0=xc[:, hs, :], scalar=1.0, in1=th, op0=ALU.add,
                                               op1=ALU.mult).then_inc(root_in, 1)
                dve.wait_ge(root_done, half + 1)
                link(nc.vector.tensor_tensor(ig[:], ig[:], th, ALU.mult))
                for i in range(HB):
                    last = nc.vector.tensor_tensor_scan(xc[:, half * HB + i, :], r_la[:, i, :], ig[:, i, :], 0.0,
                                                        ALU.mult, ALU.add)
                last.then_inc(scan_done, 1)
            for half in range(2):
                hs = slice(half * HB, half * HB + HB)
                for j in range(RB // 2):
                    ahead(CH[("y", j)] + 2) if half or j < 3 else None
                dve.wait_ge(emptied["A"], EMPTIED[TN[("y", half * HB + HB - 1)]])
                dve.wait_ge(scan_done, 2)
                nc.vector.tensor_tensor(xc[:, hs, :], xc[:, hs, :], xr_gy[:, hs, 0:T], ALU.mult).then_inc(z_f32, 1)
            for half in range(2):
                hs = slice(half * HB, half * HB + HB)
                dve.wait_ge(z_hi, half + 1)
                nc.vector.tensor_tensor(xc_lo[:, hs, :], xc[:, hs, :], xc_hi[:, hs, :].bitcast(F32), ALU.subtract)\
                    .then_inc(z_lo, 1)
            for m in range(KD):
                ahead(CH[("a_out", m)] + 2)
            residual("st_ao", "a_post")
            reciprocal_of_root("st_f")
            normalise(sq, hT, "f_pre", KD).then_inc(norm_f32, 1)
            remainder(2, u_lo[:], sq[:], u_hi[:])

            def f_low(m):
                dve.wait_ge(fhi_done, m + 1)
                nc.vector.tensor_tensor(hid_lo[:, m, :], f_h[:, m % 4, :], hid_hi[:, m, :].bitcast(F32), ALU.subtract)\
                    .then_inc(flo_done, 1)

            for j in range(KF // 2):
                ahead(CH[("f_gate", j)] + 2)
                ahead(CH[("f_up", j)] + 2)
                for m in (2 * j, 2 * j + 1):
                    ps = at_tile(dve, "f_u", m)
                    dve.wait_ge(emptied["A"], EMPTIED[TN[("f_g", m)]])
                    if m >= 4:
                        dve.wait_ge(flo_done, m - 3)
                    nc.vector.tensor_tensor(f_h[:, m % 4, :], ps[:, 0:T], f_silu[:, m % 2, :], ALU.mult)\
                        .then_inc(emptied["V"], 1)
                if j:
                    f_low(2 * j - 2)
                    f_low(2 * j - 1)
            f_low(KF - 2)
            f_low(KF - 1)
            for q in range(KD // 2):
                for r in range(3):
                    ahead(CH[("f_down", 3 * q + r)] + 2)
            residual("st_fo", "f_post")
            reciprocal_of_root("st_b")
            normalise(sq, hT, "kv_norm", KD).then_inc(norm_f32, 1)
            normalise(mix, hT, "b_pre", KD).then_inc(norm_f32, 1)
            remainder(3, u_lo[:], sq[:], u_hi[:])
            nc.vector.memset(ckv_hi[:, :, T:].bitcast(F32), 0.0)
            nc.vector.memset(ckv_lo[:, :, T:].bitcast(F32), 0.0)
            ahead(CH[("dkv", 0)] + 2)
            ahead(CH[("dkr", 0)] + 2)
            ps = at_tile(dve, "krope", 0)
            nc.vector.tensor_tensor(rope_a[NOPE:QK, :], ps[NOPE:QK, 0:T], cn("cos")[NOPE:QK, :], ALU.mult)
            ins = nc.vector.tensor_tensor(k_temp[NOPE:QK, :], ps[0:ROPE, 0:T], cn("sin")[0:ROPE, :], ALU.mult)
            ins.then_inc(emptied["V"], 1)
            dve.wait_ge(emptied["V"], EMPTIED[TN[("krope", 0)]])
            nc.vector.tensor_tensor(rope_a[NOPE:QK, :], rope_a[NOPE:QK, :], k_temp[NOPE:QK, :], ALU.add)\
                .then_inc(krope_done, 1)
            remainder(4, u_lo[:], mix[:], u_hi[:])
            ahead(CH[("dq", 0)] + 2)
            reciprocal_of_root("st_ckv")
            normalise(ckv, ckv, "latent", KL).then_inc(norm_f32, 1)
            reciprocal_of_root("st_cq")
            normalise(cq, cq, "q_norm", KQ).then_inc(norm_f32, 1)
            remainder(5, ckv_lo[:, :, 0:T], ckv[:], ckv_hi[:, :, 0:T])
            remainder(6, cq_lo[:], cq[:], cq_hi[:])
            ahead(CH[("ukv", 0)] + 2)
            ahead(CH[("ukv", 1)] + 2)
            dve.wait_ge(krope_copied, 1)
            for g in range(4):
                ahead(CH[("uq", g)] + 2)
                ps = at_tile(dve, "qro", g)
                nc.vector.tensor_tensor(rope_a[:, :], ps[:, 0:T], cn("cos"), ALU.mult).then_inc(emptied["V"], 1)
                ps = at_tile(dve, "qsw", g)
                nc.vector.tensor_tensor(rope_b[:, :], ps[:, 0:T], cn("sin"), ALU.mult).then_inc(emptied["V"], 1)
                dve.wait_ge(emptied["V"], EMPTIED[TN[("qsw", g)]])
                link(nc.vector.tensor_tensor(rope_a[:, :], rope_a[:, :], rope_b[:, :], ALU.add))
                for i in range(4):
                    last = nc.vector.tensor_copy(qT[NOPE:QK, i, :], rope_a[ROPE * i:ROPE * i + ROPE, :])
                last.then_inc(qrope_done, 1)
                for h in range(4 * g, 4 * g + 4):
                    if h >= 2:
                        at(dve, "tile", TN[("pt", h - 2)])
                    i = 3 * (h % 2)
                    for b, (t0, n) in enumerate(TB):
                        c, kn = SC[b]
                        ps = at_tile(dve, "s", (h, b))
                        nc.vector.tensor_tensor_reduce(s_sb[0:n, h % 2, c:c + kn], ps[0:n, 0:kn],
                                                       cn(f"mask{b}")[0:n, :], 1.0, -3.0e38, ALU.add, ALU.max,
                                                       smax[0:n, i + b:i + b + 1]).then_inc(emptied["V"], 1)
                    dve.wait_ge(emptied["V"], EMPTIED[TN[("s", (h, 2))]])
                    nc.vector.tensor_scalar(nbias[:, i:i + 3], smax[:, i:i + 3], -(QK ** -0.5), None, ALU.mult)\
                        .then_inc(max_done, 1)
                    dve.wait_ge(exp_done, h + 1)
                    for b, (t0, n) in enumerate(TB):
                        ins = nc.vector.reciprocal(rcp[0:n, i + b:i + b + 1], rsum[0:n, i + b:i + b + 1])
                    link(ins)
                    for b, (t0, n) in enumerate(TB):
                        c, kn = SC[b]
                        last = nc.vector.tensor_scalar(s_sb[0:n, h % 2, c:c + kn], s_sb[0:n, h % 2, c:c + kn],
                                                       rcp[0:n, i + b:i + b + 1], None, ALU.mult)
                    last.then_inc(prob_done, 1)
            remainder(7, u_lo[:], sq[:], u_hi[:])
            for j in range(4):
                ahead(CH[("b_out", j)] + 2)
            residual("st_bo", "b_post")

            nc.vector.tensor_tensor(gw[:], pr("router_w").rearrange("p (k e) -> p k e", k=KD),
                                    pr("m_pre")[:, :, None].to_broadcast([P, KD, NE]), ALU.mult).then_inc(dve_step, 1)
            steps[0] += 1
            nc.vector.memset(banks[6][:, 0:3 * NE], 0.0).then_inc(gw_done, 1)
            a_, g_, lg, p_, o1, o2, pos, t_ = (rt[:, k, :] for k in range(8))
            cols = rt[:, 9, :]
            m1, i1, m2, i2, s_, t3, c_ = (cols[:, 3 * k:3 * k + 3] for k in range(7))

            def v3(x):
                return x.rearrange("p (b e) -> p b e", b=3)

            def wide(x):
                return x[:, :, None].to_broadcast([P, 3, NE])

            dve.wait_ge(rstd_t, 1)
            link(nc.vector.reciprocal(mrs, mrs))
            at(dve, "logits")
            link(nc.vector.tensor_tensor(v3(lg), v3(banks[6][:, 0:3 * NE]), wide(mrs), ALU.mult))
            dve.wait_ge(in_rows, 48)
            link(nc.vector.tensor_tensor(v3(lg), v3(lg), rbias[:, None, :].to_broadcast([P, 3, NE]), ALU.add))
            link(nc.vector.tensor_reduce(m1, v3(lg), AX_X, ALU.max))
            nc.vector.tensor_tensor(v3(lg), v3(lg), wide(m1), ALU.subtract).then_inc(logit_in, 1)
            dve.wait_ge(logit_exp, 1)
            link(nc.vector.tensor_reduce(s_, v3(lg), AX_X, ALU.add))
            link(nc.vector.reciprocal(s_, s_))
            link(nc.vector.tensor_tensor(v3(p_), v3(lg), wide(s_), ALU.mult))
            for m_, i_, o_ in ((m1, i1, o1), (m2, i2, o2)):
                link(nc.vector.tensor_reduce(m_, v3(p_), AX_X, ALU.max))
                link(nc.vector.tensor_tensor(v3(t_), v3(p_), wide(m_), ALU.is_equal))
                link(nc.vector.scalar_tensor_tensor(out=t_, in0=t_, scalar=-float(NE), in1=cn("expert"),
                                                    op0=ALU.mult, op1=ALU.add))
                link(nc.vector.tensor_reduce(i_, v3(t_), AX_X, ALU.min))
                link(nc.vector.tensor_scalar(i_, i_, float(NE), None, ALU.add))
                link(nc.vector.tensor_tensor(v3(o_), v3(cn("expert")), wide(i_), ALU.is_equal))
                link(nc.vector.scalar_tensor_tensor(out=p_, in0=o_, scalar=-2.0, in1=p_, op0=ALU.mult, op1=ALU.add))
            link(nc.vector.tensor_tensor(t_, o1, o2, ALU.add))
            nc.vector.tensor_tensor(v3(a_), v3(t_), wide(cn("valid")), ALU.mult).then_inc(assigned, 1)
            link(nc.vector.tensor_tensor(s_, m1, m2, ALU.add))
            link(nc.vector.reciprocal(s_, s_))
            link(nc.vector.tensor_tensor(m1, m1, s_, ALU.mult))
            link(nc.vector.tensor_tensor(m2, m2, s_, ALU.mult))
            link(nc.vector.tensor_tensor(v3(o1), v3(o1), wide(m1), ALU.mult))
            link(nc.vector.tensor_tensor(v3(o2), v3(o2), wide(m2), ALU.mult))
            link(nc.vector.tensor_tensor(g_, o1, o2, ALU.add))
            at(dve, "positions")
            link(nc.vector.scalar_tensor_tensor(out=pos, in0=banks[7][:, 0:3 * NE], scalar=1.0, in1=a_,
                                                op0=ALU.add, op1=ALU.mult))
            link(nc.vector.tensor_scalar(pos, pos, -1.0, None, ALU.add))
            link(nc.vector.tensor_reduce(c_[:, 0:1], banks[7][:, 3 * NE:4 * NE], AX_X, ALU.max))
            link(nc.vector.tensor_scalar(c_[:, 1:2], c_[:, 0:1], float(P), 1.0, ALU.is_gt, ALU.add))
            link(nc.vector.tensor_scalar(c_[:, 2:3], c_[:, 0:1], 2.0 * P, None, ALU.is_gt))
            link(nc.vector.tensor_tensor(c_[:, 1:2], c_[:, 1:2], c_[:, 2:3], ALU.add))
            link(nc.vector.tensor_copy(rounds_i[0:1, 0:1], c_[0:1, 1:2]))
            link(nc.vector.memset(u_thi[:, 2, :].bitcast(F32), 0.0))
            link(nc.vector.memset(u_tlo[:, 2, :].bitcast(F32), 0.0))
            for b, (t0, n) in enumerate(TB):
                link(nc.vector.scalar_tensor_tensor(out=y_acc[0:n, 2, :], in0=h_tok[0:n, b, :],
                                                    scalar=mrs[0:n, b:b + 1], in1=y_acc[0:n, 0, :],
                                                    op0=ALU.mult, op1=ALU.mult))
                link(nc.vector.tensor_copy(u_thi[0:n, b, :], y_acc[0:n, 2, :]))
                link(nc.vector.tensor_tensor(u_tlo[0:n, b, :], y_acc[0:n, 2, :], u_thi[0:n, b, :].bitcast(F32),
                                             ALU.subtract))
            nc.vector.memset(y_acc[:], 0.0).then_inc(u_tok_done, 1)
            dve.wait_ge(u_tok_done, 1)
            nc.vector.memset(cur[:], 0.0).then_inc(rounds_ready, 1)
            dve.wait_ge(rounds_ready, 1)
            rounds = dve.value_load(rounds_i[0:1, 0:1], min_val=1, max_val=3)

            LINKS = 2

            def expert(it, e):
                done = [0]

                def elink(ins):
                    ins.then_inc(loop_step, 1)
                    done[0] += 1
                    dve.wait_ge(loop_step, it * LINKS + done[0])

                def split(c):
                    dve.wait_ge(hi_done, it * EC + (NC0 + c + 1))
                    s = (NC0 + c) % SPLIT
                    nc.vector.tensor_tensor(w_lo[s][:], raw[(NC0 + c) % RAW][:], w_hi[s][:].bitcast(F32), ALU.subtract)\
                        .then_inc(lo_done, 1)

                for b in range(3):
                    nc.vector.tensor_scalar(cur[:, b:b + 1], v3(pos)[:, b, bass.ds(e, 1)], 0.0, None, ALU.add)
                for b in range(3):
                    ins = nc.vector.tensor_scalar(cur[:, 3 + b:4 + b], v3(g_)[:, b, bass.ds(e, 1)], 0.0, None, ALU.add)
                elink(ins)
                for b in range(3):
                    ins = nc.vector.tensor_scalar(sel[:, b, :], cn("iota"), cur[:, b:b + 1], None, ALU.is_equal)
                ins.then_inc(sel_done, 1)
                for b in range(3):
                    ins = nc.vector.tensor_scalar(v3(pos)[:, b, bass.ds(e, 1)], cur[:, b:b + 1], -float(P), None,
                                                  ALU.add)
                elink(ins)
                split(0)
                at_expert(dve, it, "x", 1)
                xf = x_lo[:].rearrange("p k n -> p (k n)")
                nc.vector.tensor_copy(xf[:, 0:512], banks[2][:, :])
                nc.vector.tensor_copy(xf[:, 512:1024], banks[3][:, :]).then_inc(x_lo_done, 1)
                at_expert(dve, it, "gate")
                nc.vector.tensor_copy(cur[:, 6:7], banks[7][:, 0:1]).then_inc(gate_done, 1)

                def hidden(j):
                    dve.wait_ge(silu_done, it * UT + (j + 1))
                    if j >= 2:
                        at_expert(dve, it, "turned", j - 2)
                    nc.vector.tensor_tensor(e_h[:, j % 2, :], banks[2 * (j % 2) + 1][:, :], e_silu[:], ALU.mult)\
                        .then_inc(eh_done, 1)

                def low_hidden(j):
                    dve.wait_ge(eh_hi_done, it * UT + (j + 1))
                    nc.vector.tensor_tensor(eh_lo[:, 4 * j:4 * j + 4, :],
                                            banks[6][:, :].rearrange("p (f n) -> p f n", f=4),
                                            eh_hi[:, 4 * j:4 * j + 4, :].bitcast(F32), ALU.subtract)\
                        .then_inc(eh_lo_done, 1)

                for c in range(1, EC):
                    split(c)
                    if c >= 5 and (c - 5) % 4 == 0 and (c - 5) // 4 < UT:
                        hidden((c - 5) // 4)
                    if c >= 9 and (c - 9) % 4 == 0 and (c - 9) // 4 < UT:
                        low_hidden((c - 9) // 4)
                dve.wait_ge(y_hi_done, it + 1)
                dve.wait_ge(gate_done, it + 1)
                for n in range(2):
                    last = nc.vector.scalar_tensor_tensor(
                        out=y_lo[:, NT * n:NT * n + NT], in0=banks[4 + n][:, :], scalar=cur[:, 6:7],
                        in1=y_hi[:, NT * n:NT * n + NT].bitcast(F32), op0=ALU.mult, op1=ALU.subtract)
                last.then_inc(y_lo_done, 1)
                for b in range(3):
                    for n in range(2):
                        at_expert(dve, it, "scattered", 2 * b + n)
                        y = y_acc[:, b, NT * n:NT * n + NT]
                        nc.vector.tensor_tensor(y, y, banks[(0, 1, 2, 3, 6, 7)[2 * b + n]][:, :], ALU.add)\
                            .then_inc(added, 1)
                assert done[0] == LINKS

            with dve.Fori(0, rounds) as r:
                with dve.Fori(0, NE) as e:
                    expert(r * NE + e, e)

            dve.wait_ge(fin_sum, 6)
            halves = small[:, 220:226].rearrange("p (b h) -> p b h", h=2)
            nc.vector.tensor_reduce(mss, halves, AX_X, ALU.add).then_inc(fin_std, 1)
            dve.wait_ge(fin_std, 2)
            link(nc.vector.reciprocal(mrs, mrs))
            for b, (t0, n) in enumerate(TB):
                link(nc.vector.scalar_tensor_tensor(out=y_acc[0:n, b, :], in0=y_acc[0:n, b, :],
                                                    scalar=mrs[0:n, b:b + 1], in1=grow[0:n, :],
                                                    op0=ALU.mult, op1=ALU.mult))
                nc.vector.tensor_tensor(y_acc[0:n, b, :], y_acc[0:n, b, :], h_tok[0:n, b, :], ALU.add)\
                    .then_inc(fin_done, 1)


_WEIGHTS = ["a_w_in", "a_gate_a_w", "a_gate_x_w", "a_w_out", "kv_w_dkv", "kv_w_ukv", "b_w_dq", "b_w_uq", "b_w_o",
            "f_w_gate_up", "f_w_down", "m_w_gate_up", "m_w_down"]
_VECTORS = {"a_pre": "a_pre_norm", "conv_b": "a_conv_b", "ga_b": "a_gate_a_b", "gx_b": "a_gate_x_b",
            "lam": "a_lambda", "a_post": "a_post_norm", "kv_norm": "kv_norm", "latent": "kv_latent_norm",
            "b_pre": "b_pre_norm", "q_norm": "b_q_norm", "b_post": "b_post_norm", "f_pre": "f_pre_norm",
            "f_post": "f_post_norm", "m_pre": "m_pre_norm"}


def shape_constants():
    c = np.zeros((P, NCONST), np.float32)

    def put(name, x):
        c[:, CONST[name][0]:CONST[name][1]] = x

    put("ident", np.eye(P))
    put("ones", 1.0)
    put("tri", np.arange(P)[:, None] < np.arange(P)[None, :])
    put("iota", np.arange(P)[None, :])
    put("valid", [[float(i < n) for _, n in TB] for i in range(P)])
    put("expert", np.tile(np.arange(NE) + NE, 3)[None, :])
    for b, (t0, n) in enumerate(TB):
        width = CONST[f"mask{b}"][1] - CONST[f"mask{b}"][0]
        put(f"mask{b}", np.where(np.arange(width)[None, :] <= t0 + np.arange(P)[:, None], 0.0, -1.0e30))
    half = ROPE // 2
    inv = np.float32(10000.0) ** (-np.arange(0, ROPE, 2, dtype=np.float32) / np.float32(ROPE))
    ang = (np.arange(T, dtype=np.float32)[:, None] * inv[None, :]).astype(np.float32)
    cos, sin = np.cos(ang).T, np.sin(ang).T
    assert cos.shape == (half, T)
    put("cos", np.tile(cos, (P // half, 1)))
    put("sin", np.tile(np.concatenate([-sin, sin]), (P // ROPE, 1)))
    return c


def kernel(**inputs):
    import concourse.bacc as _bacc
    from concourse.bass_utils import run_bass_kernel_spmd as _run

    x = {k: np.ascontiguousarray(v) for k, v in inputs.items()}
    params = np.zeros((P, NPARAM), np.float32)

    def put(name, v):
        params[:, PARAM[name][0]:PARAM[name][1]] = v

    for name, key in _VECTORS.items():
        put(name, x[key].reshape(-1, P).T)
    put("conv_w", x["a_conv_w"].reshape(-1, P).T)
    put("router_w", x["m_router_w"][0].reshape(KD, P, NE).transpose(1, 0, 2).reshape(P, KD * NE))
    put("eps", EPS)
    arrays = {n: x[n] for n in _WEIGHTS}
    arrays["params"] = params
    arrays["consts"] = shape_constants()
    arrays["gain_rows"] = np.concatenate([x["m_pre_norm"].reshape(1, -1), x["m_post_norm"].reshape(1, -1),
                                          x["m_router_b"].reshape(1, -1)], axis=1)
    arrays["tokens"] = np.concatenate([x["meta_tokens"], x["x"][0]], axis=0)
    nc = _bacc.Bacc("TRN2", target_bir_lowering=False, num_devices=1)
    aps = {n: nc.dram_tensor(f"in_{n}", a.shape, F32, kind="ExternalInput").ap() for n, a in arrays.items()}
    out = nc.dram_tensor("out_0", (SEQ, D), F32, kind="ExternalOutput").ap()
    yoco_kernel(nc, aps, aps["params"], aps["consts"], aps["gain_rows"], aps["tokens"], out)
    r = _run(nc, [{f"in_{n}": a for n, a in arrays.items()}], core_ids=[0])
    return r.results[0]["out_0"].reshape(1, SEQ, D)
```

```python
from contextlib import ExitStack

import numpy as np
import concourse.bass as bass
from concourse import mybir

ALU = mybir.AluOpType
ACT = mybir.ActivationFunctionType
F32 = mybir.dt.float32
F32R = mybir.dt.float32r
I32 = mybir.dt.int32
AX_X = mybir.AxisListType.X

P = 128
D = 1024
KD = D // P
META, SEQ = 16, 256
T = META + SEQ
TB = [(0, 128), (128, 128), (256, 16)]
RNN = 1280
RB = RNN // P
HB = RB // 2
CONV = 4
HEADS, NOPE, ROPE, VD = 16, 64, 32, 64
QK = NOPE + ROPE
LORA, QLORA = 256, 384
KL, KQ = LORA // P, QLORA // P
FF = 3072
KF = FF // P
NE, TOPK = 8, 2
EF = 3584
NT = 512
UT = EF // NT
KE = EF // P
EPS = 1e-6

CHUNK = 2048
RAW, SPLIT = 6, 3
LAG = 2
BANKS = 6

PARAM = {}
_n = 0
for _name, _w in (("a_pre", KD), ("conv_w", CONV * RB), ("conv_b", RB), ("ga_b", RB), ("gx_b", RB), ("lam", RB),
                  ("a_post", KD), ("kv_norm", KD), ("latent", KL), ("b_pre", KD), ("q_norm", KQ), ("b_post", KD),
                  ("f_pre", KD), ("f_post", KD), ("m_pre", KD), ("eps", 1), ("router_w", KD * NE)):
    PARAM[_name] = (_n, _n + _w)
    _n += _w
NPARAM = _n

CONST = {}
_n = 0
for _name, _w in (("ident", P), ("ones", P), ("tri", P), ("iota", P), ("valid", 3), ("expert", 3 * NE),
                  ("mask0", 128), ("mask1", 256), ("mask2", T), ("cos", T), ("sin", T)):
    CONST[_name] = (_n, _n + _w)
    _n += _w
NCONST = _n


def chunk_plan():
    plan = [("xr", j, KD * 256) for j in range(RB // 2)]
    plan += [("ga", 0, RB * P), ("gx", 0, RB * P)]
    plan += [("y", j, KD * 256) for j in range(RB // 2)]
    plan += [("a_out", j, RB * P) for j in range(KD)]
    for j in range(KF // 2):
        plan += [("f_gate", j, KD * 256), ("f_up", j, KD * 256)]
    plan += [("f_down", j, KD * 256) for j in range(12)]
    plan += [("dkv", 0, KD * LORA), ("dkr", 0, KD * ROPE), ("dq", 0, KD * 256), ("dq", 1, KD * 128)]
    plan += [("ukv", j, KL * D) for j in range(2)]
    plan += [("uq", j, KQ * 4 * QK) for j in range(4)]
    plan += [("b_out", j, KD * 256) for j in range(4)]
    return plan


PLAN = chunk_plan()
CH = {(name, j): n for n, (name, j, _) in enumerate(PLAN)}
NC0 = len(PLAN)
EC = 4 * UT + KE // 2
assert EC % RAW == 0 and EC % SPLIT == 0


def tile_plan():
    plan = [("hT", c, "V") for c in range(KD)]
    plan += [("xr", m, "A") for m in range(RB)]
    for half in range(2):
        plan += [(g, m, "A") for m in range(half * HB, half * HB + HB) for g in ("r", "i")]
    plan += [("y", m, "A") for m in range(RB)] + [("a_out", m, "A") for m in range(KD)]
    for j in range(KF // 2):
        plan += [("f_g", 2 * j, "A"), ("f_g", 2 * j + 1, "A"), ("f_u", 2 * j, "V"), ("f_u", 2 * j + 1, "V")]
    plan += [("f_down", m, "A") for m in range(KD)] + [("ckv", m, "A") for m in range(KL)] + [("krope", 0, "V")]
    plan += [("cq", m, "A") for m in range(KQ)]
    for half in range(2):
        plan += [("kn", 4 * half + m, "A") for m in range(4)] + [("v", (b, half), "A") for b in range(3)]
    for g in range(4):
        plan += [("qn", 2 * g, "A"), ("qn", 2 * g + 1, "A"), ("qro", g, "V"), ("qsw", g, "V")]
        for h in range(4 * g, 4 * g + 4):
            plan += [("s", (h, b), "V") for b in range(3)]
            if h >= LAG:
                plan += [("pt", h - LAG, "A")]
            if h > LAG:
                plan += [("o", h - LAG - 1, "A")]
    for h in range(HEADS - LAG, HEADS):
        plan += [("pt", h, "A"), ("o", h - 1, "A")]
    plan += [("o", HEADS - 1, "A")]
    plan += [("b_out", m, "A") for m in range(KD)]
    return plan


TILES = tile_plan()
TN = {(name, j): n for n, (name, j, _) in enumerate(TILES)}
EMPTIED = [sum(x[2] == TILES[n][2] for x in TILES[:n + 1]) for n in range(len(TILES))]


NORMS = [("a", KD), ("ao", KD), ("f", KD), ("fo", KD), ("b", KD), ("ckv", KL), ("cq", KQ), ("bo", KD)]
NORM = {name: i for i, (name, _) in enumerate(NORMS)}
PARTS = [("a", KD), ("f", KD), ("kv", KD), ("b", KD), ("ckv", KL), ("cq", KQ), ("o", KD)]
PART = {name: sum(k for _, k in PARTS[:i]) for i, (name, _) in enumerate(PARTS)}
NORMED = PART
RES = {"ao": 0, "fo": KD, "bo": 2 * KD}
SQ = {"a": 0, "f": KD, "b": 2 * KD}



def pieces(name, k, src, dst):
    if name == "dkr":
        s = src[:, 0:k * ROPE].rearrange("p (k n) -> p k n", k=k)
        d = dst[:, 0:k * 3 * ROPE].rearrange("p (k n) -> p k n", k=k)
        h = ROPE // 2
        return [(d[:, :, 0:h], s[:, :, h:ROPE]), (d[:, :, h:ROPE], s[:, :, 0:h]),
                (d[:, :, ROPE:2 * ROPE], s), (d[:, :, 2 * ROPE:3 * ROPE], s)]
    if name == "uq":
        out = []
        for r in range(k):
            s = src[:, r * 4 * QK:(r + 1) * 4 * QK].rearrange("p (h n) -> p h n", h=4)
            d = dst[:, r * 512:(r + 1) * 512]
            n = d[:, 0:4 * NOPE].rearrange("p (h n) -> p h n", h=4)
            ro = d[:, 4 * NOPE:4 * QK].rearrange("p (h n) -> p h n", h=4)
            sw = d[:, 4 * QK:512].rearrange("p (h n) -> p h n", h=4)
            h = ROPE // 2
            out += [(n, s[:, :, 0:NOPE]), (ro, s[:, :, NOPE:QK]), (sw[:, :, 0:h], s[:, :, NOPE + h:QK]),
                    (sw[:, :, h:ROPE], s[:, :, NOPE:NOPE + h])]
        return out
    if name == "ukv":
        out = []
        for r in range(k):
            s = src[:, r * D:(r + 1) * D].rearrange("p (h n) -> p h n", h=8)
            for part in range(2):
                d = dst[:, r * D + 512 * part:r * D + 512 * part + 512].rearrange("p (h n) -> p h n", h=8)
                out.append((d, s[:, :, 64 * part:64 * part + 64]))
        return out
    return [(dst, src)]


def yoco_kernel(nc, w, params, consts, gain_rows, x_tok, out):
    with ExitStack() as ctx:
        def sb(name, shape, dt=F32, stack=None):
            return (stack or ctx).enter_context(nc.sbuf_tensor(name, shape, dt))

        def sem(name):
            return ctx.enter_context(nc.semaphore(name))

        raw = [sb(f"raw{i}", [P, CHUNK]) for i in range(RAW)]
        w_hi = [sb(f"w_hi{i}", [P, CHUNK], F32R) for i in range(SPLIT)]
        w_lo = [sb(f"w_lo{i}", [P, CHUNK], F32R) for i in range(SPLIT)]
        par = sb("par", [P, NPARAM])
        con = sb("con", [P, NCONST])
        small = sb("small", [P, 256])
        banks = [ctx.enter_context(nc.psum_tensor(f"bank{i}", [P, 512], F32)) for i in range(8)]

        def pr(name, c=None):
            a, b = PARAM[name]
            return par[:, a:b] if c is None else par[:, a + c:a + c + 1]

        def cn(name):
            a, b = CONST[name]
            return con[:, a:b]

        ident, ones, eps = cn("ident"), cn("ones"), pr("eps")

        body = ExitStack()
        hT = sb("hT", [P, KD, T], stack=body)
        rstd = sb("rstd", [P, 2, T], stack=body)
        u_hi = sb("u_hi", [P, KD, T], F32R, stack=body)
        u_lo = sb("u_lo", [P, KD, T], F32R, stack=body)
        mix_sq = sb("mix_sq", [P, 2 * KD, T], stack=body)
        mix = mix_sq[:, 0:KD, :]
        sq = mix_sq[:, KD:2 * KD, :]

        with ExitStack() as ph:
            x_in = sb("x_in", [P, 3, D], stack=ph)
        with ExitStack() as ph:
            xr_gy = sb("xr_gy", [P, RB, T + CONV - 1], stack=ph)
            xc = sb("xc", [P, RB, T], stack=ph)
            xc_hi = sb("xc_hi", [P, RB, T], F32R, stack=ph)
            xc_lo = sb("xc_lo", [P, RB, T], F32R, stack=ph)
            ig = sb("ig", [P, RB, T], stack=ph)
        r_la = mix_sq[:, 0:RB, :]
        th = mix_sq[:, RB:RB + HB, :]
        with ExitStack() as ph:
            f_silu = sb("f_silu", [P, 2, T], stack=ph)
            f_h = sb("f_h", [P, 4, T], stack=ph)
            hid_hi = sb("hid_hi", [P, KF, T], F32R, stack=ph)
            hid_lo = sb("hid_lo", [P, KF, T], F32R, stack=ph)
        with ExitStack() as ph:
            ckv = sb("ckv", [P, KL, T], stack=ph)
            ckv_hi = sb("ckv_hi", [P, KL, 3 * P], F32R, stack=ph)
            ckv_lo = sb("ckv_lo", [P, KL, 3 * P], F32R, stack=ph)
            cq = sb("cq", [P, KQ, T], stack=ph)
            cq_hi = sb("cq_hi", [P, KQ, T], F32R, stack=ph)
            cq_lo = sb("cq_lo", [P, KQ, T], F32R, stack=ph)
            with ExitStack() as ph2:
                ub_hi = sb("ub_hi", [P, KD, T], F32R, stack=ph2)
                ub_lo = sb("ub_lo", [P, KD, T], F32R, stack=ph2)
            kT = sb("kT", [QK, HEADS, T], stack=ph)
            v_tok = sb("v_tok", [P, 3, D], stack=ph)
            qT = sb("qT", [QK, 4, T], stack=ph)
            rope_a = sb("rope_a", [P, T], stack=ph)
            pT = sb("pT", [P, 2, 432], stack=ph)
        s_sb = mix.rearrange("p k n -> p (k n)")[:, 0:3 * 656].rearrange("p (h n) -> p h n", h=3)
        body.close()
        k_temp, rope_b = qT[:, 0, :], cq[:, 0, :]
        SC = [(0, 128), (128, 256), (384, T)]

        eh_hi = sb("eh_hi", [P, KE, P], F32R)
        h_tok = sb("h_tok", [P, 3, D])
        u_thi = sb("u_thi", [P, 3, D], F32R)
        u_tlo = sb("u_tlo", [P, 3, D], F32R)
        y_acc = sb("y_acc", [P, 3, D])
        x_hi = sb("x_hi", [P, KD, P], F32R)
        x_lo = sb("x_lo", [P, KD, P], F32R)
        eh_lo = sb("eh_lo", [P, KE, P], F32R)
        e_silu = sb("e_silu", [P, NT])
        e_h = sb("e_h", [P, 2, NT])
        y_exp = sb("y_exp", [P, D])
        sel = sb("sel", [P, 3, P], F32R)
        selT = sb("selT", [P, 3, P])
        grow = sb("grow", [P, D])
        rbias = sb("rbias", [P, NE])
        gw = sb("gw", [P, KD, NE])
        rt = sb("rt", [P, 10, 3 * NE])
        cur = sb("cur", [P, 8])
        rounds_i = sb("rounds_i", [1, 1], I32)
        m_gain = e_h[:].rearrange("p a n -> p (a n)")

        landed = [sem(f"landed{i}") for i in range(RAW)]
        hi_done, lo_done = sem("hi_done"), sem("lo_done")
        in_const, in_par, in_x, in_rows = sem("in_const"), sem("in_par"), sem("in_x"), sem("in_rows")
        pe_done = sem("pe_done")
        emptied = {"A": sem("emptied_by_act"), "V": sem("emptied_by_dve")}
        dve_step = sem("dve_step")
        sq_ready, root_taken, norm_f32, act_hi, act_lo, res_scaled, res_done = (
            sem("sq_ready"), sem("root_taken"), sem("norm_f32"), sem("act_hi"), sem("act_lo"), sem("res_scaled"),
            sem("res_done"))
        conv_done, xc_hi_done, xc_lo_done = sem("conv_done"), sem("xc_hi_done"), sem("xc_lo_done")
        lam_abs, lam_exp = sem("lam_abs"), sem("lam_exp")
        loga_ready, a_ready, root_in, root_done, scan_done = (
            sem("loga_ready"), sem("a_ready"), sem("root_in"), sem("root_done"), sem("scan_done"))
        gated, gelu_done = sem("gated"), sem("gelu_done")
        z_f32, z_hi, z_lo = sem("z_f32"), sem("z_hi"), sem("z_lo")
        fhi_done, flo_done = sem("fhi_done"), sem("flo_done")
        krope_done, krope_copied, qrope_done = sem("krope_done"), sem("krope_copied"), sem("qrope_done")
        max_done, exp_done, prob_done = sem("max_done"), sem("exp_done"), sem("prob_done")
        gw_done, hsum_done, rstd_t = sem("gw_done"), sem("hsum_done"), sem("h_std_done")
        u_tok_done, logit_in, logit_exp, assigned = (
            sem("u_tok_done"), sem("logit_in"), sem("logit_exp"), sem("assigned"))
        rounds_ready = sem("rounds_ready")
        h_tok_done = sem("h_tok_done")
        sel_done, x_hi_done, x_lo_done, selT_done, gate_done = (
            sem("sel_done"), sem("x_hi_done"), sem("x_lo_done"), sem("selT_done"), sem("gate_done"))
        silu_done, eh_done, eh_hi_done, eh_lo_done = (
            sem("silu_done"), sem("eh_done"), sem("eh_hi_done"), sem("eh_lo_done"))
        y_done, added = sem("y_done"), sem("added")
        h_scaled, u_f32_done, u_hi_done = sem("h_scaled"), sem("u_f32_done"), sem("u_hi_done")
        pads_zeroed, mrs_done = sem("pads_zeroed"), sem("mrs_done")
        loop_step = sem("loop_step")
        fin_sum, fin_std, fin_done, out_written = (
            sem("fin_sum"), sem("fin_std"), sem("fin_done"), sem("out_written"))

        c8 = small[:, 0:RB]
        lt = [small[:, 16 * k + 16:16 * k + 16 + RB] for k in range(6)]
        smax, nbias, rsum, rcp = (small[:, 112 + 16 * k:112 + 16 * k + 9] for k in range(4))
        mss, mrs = small[:, 192:195], small[:, 208:211]

        def rows(a):
            return a.rearrange("(k p) n -> p k n", p=P)

        w_in, w_ao, w_gu, w_dn = (rows(w[n][0]) for n in ("a_w_in", "a_w_out", "f_w_gate_up", "f_w_down"))
        w_dq, w_uq, w_bo = (rows(w[n][0]) for n in ("b_w_dq", "b_w_uq", "b_w_o"))
        w_dkv, w_ukv = rows(w["kv_w_dkv"]), rows(w["kv_w_ukv"])
        ga, gx = (w[n][0].rearrange("n c d -> c n d") for n in ("a_gate_a_w", "a_gate_x_w"))

        def source(name, j):
            return {
                "xr": lambda: w_in[:, :, RNN + 256 * j:RNN + 256 * j + 256],
                "y": lambda: w_in[:, :, 256 * j:256 * j + 256],
                "ga": lambda: ga, "gx": lambda: gx,
                "a_out": lambda: w_ao[:, :, P * j:P * j + P],
                "f_gate": lambda: w_gu[:, :, 256 * j:256 * j + 256],
                "f_up": lambda: w_gu[:, :, FF + 256 * j:FF + 256 * j + 256],
                "f_down": lambda: w_dn[:, KD * (j % 3):KD * (j % 3) + KD, 256 * (j // 3):256 * (j // 3) + 256],
                "dkv": lambda: w_dkv[:, :, 0:LORA],
                "dkr": lambda: w_dkv[:, :, LORA:LORA + ROPE],
                "dq": lambda: w_dq[:, :, 256 * j:min(256 * j + 256, QLORA)],
                "ukv": lambda: w_ukv[:, :, D * j:D * j + D],
                "uq": lambda: w_uq[:, :, 4 * QK * j:4 * QK * (j + 1)],
                "b_out": lambda: w_bo[:, :, 256 * j:256 * j + 256],
            }[name]()

        def split_views(n, buf):
            name, j, cols = PLAN[n]
            k = source(name, j).shape[1]
            cols = {"dkr": KD * 3 * ROPE, "uq": KQ * 512}.get(name, cols)
            return buf[n % SPLIT][:, 0:cols].rearrange("p (k n) -> p k n", k=k)

        step = {}
        block = ctx.enter_context(nc.Block())

        @block.tensor
        def _(pe):
            count = [0]

            def mark(ins, *keys):
                ins.then_inc(pe_done, 1)
                count[0] += 1
                for key in keys:
                    step[key] = count[0]

            def bank_of(name, j):
                n = TN[(name, j)]
                if n >= BANKS:
                    pe.wait_ge(emptied[TILES[n - BANKS][2]], EMPTIED[n - BANKS])
                return banks[n % BANKS]

            def chunk(name, j):
                n = CH[(name, j)]
                pe.wait_ge(lo_done, n + 1)
                return split_views(n, w_hi), split_views(n, w_lo)

            def product(o, a, b, start, stop):
                nc.tensor.matmul(o, a[0], b[0], start=start, stop=False)
                nc.tensor.matmul(o, a[0], b[1], start=False, stop=False)
                return nc.tensor.matmul(o, a[1], b[0], start=False, stop=stop)

            def columns_tile(name, m, wc, c0, act, kn, width=P, *keys, need=None):
                ps = bank_of(name, m)
                for k in range(kn):
                    if need:
                        pe.wait_ge(act_lo, PART[need] + k + 1)
                    last = product(ps[0:width, 0:T], [x[:, k, c0:c0 + width] for x in wc],
                                   [x[:, k, 0:T] for x in act], k == 0, k == kn - 1)
                mark(last, ("tile", TN[(name, m)]), *keys)

            def sum_block(name, src, k):
                kn = NORMS[NORM[name]][1]
                ps = banks[6 + NORM[name] % 2]
                last = nc.tensor.matmul(ps[:, 0:T], ones, src, start=(k == 0), stop=(k == kn - 1))
                if k == kn - 1:
                    mark(last, ("sum", name))

            def sum_taken(name):
                for k in range(KD):
                    pe.wait_ge(sq_ready, SQ[name] + k + 1)
                    sum_block(name, sq[:, k, :], k)

            def sum_emptied(name, tile, m, src):
                pe.wait_ge(emptied["A"], EMPTIED[TN[(tile, m)]])
                sum_block(name, src, m)

            u = (u_hi, u_lo)
            pe.wait_ge(in_const, 16)
            pe.wait_ge(in_x, 48)
            for c in range(KD):
                ps = bank_of("hT", c)
                for b, (t0, n) in enumerate(TB):
                    last = nc.tensor.transpose(ps[:, t0:t0 + n], x_in[0:n, b, c * P:(c + 1) * P], ident[0:n, 0:n])
                mark(last, ("tile", TN[("hT", c)]))
            sum_taken("a")
            for j in range(RB // 2):
                wc = chunk("xr", j)
                for m in (2 * j, 2 * j + 1):
                    columns_tile("xr", m, wc, P * (m % 2), u, KD, P, *([("chunk", CH[("xr", j)])] if m % 2 else []),
                                 need=None if m else "a")
            wa, wx = chunk("ga", 0), chunk("gx", 0)
            for m in range(RB):
                pe.wait_ge(xc_lo_done, m + 1)
                for name, wc, key in (("r", wa, "ga"), ("i", wx, "gx")):
                    ps = bank_of(name, m)
                    last = product(ps[:, 0:T], [x[:, m, :] for x in wc], (xc_hi[:, m, :], xc_lo[:, m, :]), True, True)
                    mark(last, ("tile", TN[(name, m)]), *([("chunk", CH[(key, 0)])] if m == RB - 1 else []))
            for j in range(RB // 2):
                wc = chunk("y", j)
                for m in (2 * j, 2 * j + 1):
                    columns_tile("y", m, wc, P * (m % 2), u, KD, P, *([("chunk", CH[("y", j)])] if m % 2 else []))
            for m in range(KD):
                if m == 0:
                    pe.wait_ge(z_lo, 2)
                columns_tile("a_out", m, chunk("a_out", m), 0, (xc_hi, xc_lo), RB, P, ("chunk", CH[("a_out", m)]))
                if m:
                    sum_emptied("ao", "a_out", m - 1, sq[:, m - 1, :])
            sum_emptied("ao", "a_out", KD - 1, sq[:, KD - 1, :])
            sum_taken("f")
            for j in range(KF // 2):
                for name, key in (("f_g", "f_gate"), ("f_u", "f_up")):
                    wc = chunk(key, j)
                    for m in (2 * j, 2 * j + 1):
                        columns_tile(name, m, wc, P * (m % 2), u, KD, P, *([("chunk", CH[(key, j)])] if m % 2 else []),
                                     need="f" if (name, m) == ("f_g", 0) else None)
            for q in range(KD // 2):
                ps = [bank_of("f_down", 2 * q + i) for i in range(2)]
                for r in range(3):
                    wc = chunk("f_down", 3 * q + r)
                    if q == 0:
                        pe.wait_ge(flo_done, KD * (r + 1))
                    for i in range(2):
                        for k in range(KD):
                            f = KD * r + k
                            last = product(ps[i][:, 0:T], [x[:, k, P * i:P * i + P] for x in wc],
                                           (hid_hi[:, f, :], hid_lo[:, f, :]), f == 0, f == KF - 1)
                        if r == 2:
                            mark(last, ("tile", TN[("f_down", 2 * q + i)]),
                                 *([("chunk", CH[("f_down", 3 * q + r)])] if i else []))
                    if r < 2:
                        mark(last, ("chunk", CH[("f_down", 3 * q + r)]))
                if q:
                    for m in (2 * q - 2, 2 * q - 1):
                        sum_emptied("fo", "f_down", m, sq[:, m, :])
            for m in (KD - 2, KD - 1):
                sum_emptied("fo", "f_down", m, sq[:, m, :])
            sum_taken("b")
            wc = chunk("dkv", 0)
            for m in range(KL):
                columns_tile("ckv", m, wc, P * m, u, KD, P, *([("chunk", CH[("dkv", 0)])] if m else []),
                             need=None if m else "kv")
            columns_tile("krope", 0, chunk("dkr", 0), 0, u, KD, QK, ("chunk", CH[("dkr", 0)]))
            for m in range(KQ):
                columns_tile("cq", m, chunk("dq", m // 2), P * (m % 2), (ub_hi, ub_lo), KD, P,
                             *([("chunk", CH[("dq", m // 2)])] if m else []), need=None if m else "b")
                if m == 0:
                    for k in range(KL):
                        sum_emptied("ckv", "ckv", k, sq[:, k, :])
            for k in range(KQ):
                sum_emptied("cq", "cq", k, sq[:, KL + k, :])
            pe.wait_ge(act_lo, PART["ckv"] + KL)
            for half in range(2):
                wc = chunk("ukv", half)
                for m in range(4 * half, 4 * half + 4):
                    columns_tile("kn", m, wc, P * (m % 4), (ckv_hi, ckv_lo), KL)
                for b, (t0, n) in enumerate(TB):
                    ps = bank_of("v", (b, half))
                    for k in range(KL):
                        last = product(ps[:, :], [x[:, k, t0:t0 + P] for x in (ckv_hi, ckv_lo)],
                                       [x[:, k, 512:1024] for x in wc], k == 0, k == KL - 1)
                    mark(last, ("tile", TN[("v", (b, half))]), *([("chunk", CH[("ukv", half)])] if b == 2 else []))

            def turn_probs(h):
                pe.wait_ge(prob_done, h + 1)
                ps = bank_of("pt", h)
                p = s_sb[:, h % 3, :]
                for b, (t0, n) in enumerate(TB):
                    for kb in range(b + 1):
                        c, kn = SC[b][0] + P * kb, TB[kb][1]
                        o = (0, 144, 160)[kb] + t0
                        last = nc.tensor.transpose(ps[0:kn, o:o + n], p[0:n, c:c + kn], ident[0:n, 0:n])
                mark(last, ("tile", TN[("pt", h)]))

            def weigh(h):
                ps = bank_of("o", h)
                pe.wait_ge(emptied["A"], EMPTIED[TN[("pt", h)]])
                for kb, (t0, kn) in enumerate(TB):
                    o = (0, 144, 160)[kb] + t0
                    last = nc.tensor.matmul(ps[0:VD, t0:T], v_tok[0:kn, kb, VD * h:VD * h + VD], pT[0:kn, h % 2, o:o + T - t0],
                                            start=(kb == 0), stop=(kb == 2))
                mark(last, ("tile", TN[("o", h)]))

            pe.wait_ge(act_lo, PART["cq"] + KQ)
            for g in range(4):
                wc = chunk("uq", g)
                for i, (name, m) in enumerate((("qn", 2 * g), ("qn", 2 * g + 1), ("qro", g), ("qsw", g))):
                    columns_tile(name, m, wc, P * i, (cq_hi, cq_lo), KQ, P, *([("chunk", CH[("uq", g)])] if i == 3 else []))
                for h in range(4 * g, 4 * g + 4):
                    if h % 4 == 0:
                        pe.wait_ge(emptied["A"], EMPTIED[TN[("qn", 2 * g + 1)]])
                        pe.wait_ge(qrope_done, g + 1)
                        pe.wait_ge(krope_copied, 1)
                    for b, (t0, n) in enumerate(TB):
                        ps = bank_of("s", (h, b))
                        mark(nc.tensor.matmul(ps[0:n, 0:SC[b][1]], qT[:, h % 4, t0:t0 + n], kT[:, h, 0:SC[b][1]],
                                              start=True, stop=True), ("tile", TN[("s", (h, b))]))
                    if h >= LAG:
                        turn_probs(h - LAG)
                    if h > LAG:
                        weigh(h - LAG - 1)
            for h in range(HEADS - LAG, HEADS):
                turn_probs(h)
                weigh(h - 1)
            weigh(HEADS - 1)
            for j in range(4):
                wc = chunk("b_out", j)
                for m in (2 * j, 2 * j + 1):
                    columns_tile("b_out", m, wc, P * (m % 2), u, KD, P, *([("chunk", CH[("b_out", j)])] if m % 2 else []),
                                 need=None if m else "o")
                if j:
                    for m in (2 * j - 2, 2 * j - 1):
                        sum_emptied("bo", "b_out", m, sq[:, m, :])
            for m in (KD - 2, KD - 1):
                sum_emptied("bo", "b_out", m, sq[:, m, :])

            for half in range(2):
                pe.wait_ge(res_done, RES["bo"] + 4 * half + 4)
                for b, (t0, n) in enumerate(TB):
                    for c in range(4):
                        last = nc.tensor.transpose(banks[2 * b + half][0:n, P * c:P * c + P],
                                                   hT[:, 4 * half + c, t0:t0 + n], ident)
                    mark(last, ("h_tok", b, half))
            pe.wait_ge(gw_done, 1)
            for b, (t0, n) in enumerate(TB):
                for k in range(KD):
                    last = nc.tensor.matmul(banks[6][0:n, NE * b:NE * b + NE], hT[:, k, t0:t0 + n], gw[:, k, :],
                                            start=(k == 0), stop=(k == KD - 1))
            mark(last, "logits")
            pe.wait_ge(assigned, 1)
            a = rt[:, 0, :]
            for b in range(3):
                for bb in range(b + 1):
                    last = nc.tensor.matmul(banks[7][:, NE * b:NE * b + NE], cn("tri") if bb == b else ones,
                                            a[:, NE * bb:NE * bb + NE], start=(bb == 0), stop=(bb == b))
            for bb in range(3):
                last = nc.tensor.matmul(banks[7][:, 3 * NE:4 * NE], ones, a[:, NE * bb:NE * bb + NE],
                                        start=(bb == 0), stop=(bb == 2))
            mark(last, "positions")
            pe.wait_ge(h_tok_done, 6)

            def gather(done):
                for part, src in enumerate((u_thi, u_tlo)):
                    for k in range(KD):
                        for b in range(3):
                            last = nc.tensor.matmul(banks[2 * part + k // 4][:, P * (k % 4):P * (k % 4) + P],
                                                    src[:, b, P * k:P * k + P], sel[:, b, :],
                                                    start=(b == 0), stop=(b == 2))
                    done(last, part)

            pe.wait_ge(u_tok_done, 3)
            pe.wait_ge(sel_done, 1)
            gather(lambda last, part: mark(last, ("first_x", part)))
            pe.wait_ge(rounds_ready, 1)
            rounds = pe.value_load(rounds_i[0:1, 0:1], min_val=1, max_val=3)
            base = step["loop"] = count[0]

            def expert(it):
                def emark(ins, *keys):
                    mark(ins, *(("e",) + key for key in keys))

                def echunk(c):
                    pe.wait_ge(lo_done, it * EC + (NC0 + c + 1))
                    s = (NC0 + c) % SPLIT
                    k = 4 if c < 4 * UT else 2
                    return [x[s][:].rearrange("p (k n) -> p k n", k=k) for x in (w_hi, w_lo)]

                pe.wait_ge(x_hi_done, it + 1)
                pe.wait_ge(x_lo_done, it + 1)

                def turn(j):
                    pe.wait_ge(eh_done, it * UT + (j + 1))
                    if j:
                        pe.wait_ge(eh_lo_done, it * UT + j)
                    else:
                        pe.wait_ge(added, it * 6 + 1)
                    for f in range(4):
                        last = nc.tensor.transpose(banks[6][:, P * f:P * f + P], e_h[:, j % 2, P * f:P * f + P], ident)
                    emark(last, ("turned", j))

                for j in range(UT):
                    if j >= 2:
                        pe.wait_ge(eh_done, it * UT + (j - 1))
                    if j == 1:
                        pe.wait_ge(added, it * 6 + 1)
                    for g in range(2):
                        ps = banks[2 * (j % 2) + g]
                        for kh in range(2):
                            c = 4 * j + 2 * g + kh
                            wc = echunk(c)
                            for k in range(4):
                                kk = 4 * kh + k
                                last = product(ps[:, :], (x_hi[:, kk, :], x_lo[:, kk, :]), [x[:, k, :] for x in wc],
                                               kk == 0, kk == KD - 1)
                            emark(last, ("chunk", c), *([("up", j)] if g and kh else []))
                    if j:
                        turn(j - 1)
                for d in range(KE // 2):
                    wc = echunk(4 * UT + d)
                    if d == 1:
                        for b in range(3):
                            last = nc.tensor.matmul(banks[7][:, 0:1], sel[:, b, :].bitcast(F32), cur[:, 3 + b:4 + b],
                                                    start=(b == 0), stop=(b == 2))
                        emark(last, ("gate",))
                    if d == 3:
                        turn(UT - 1)
                    if d == 5:
                        pe.wait_ge(eh_lo_done, (it + 1) * UT)
                        for b in range(3):
                            last = nc.tensor.transpose(banks[6][:, P * b:P * b + P], sel[:, b, :].bitcast(F32), ident)
                        emark(last, ("selT",))
                    if d == 9:
                        pe.wait_ge(sel_done, it + 2)
                        pe.wait_ge(eh_done, (it + 1) * UT)
                        gather(lambda last, part: emark(last, ("x", part)))
                    pe.wait_ge(eh_lo_done, it * UT + ((2 * d + 1) // 4 + 1))
                    for n in range(2):
                        for f in range(2):
                            ff = 2 * d + f
                            last = product(banks[4 + n][:, :], (eh_hi[:, ff, :], eh_lo[:, ff, :]),
                                           [x[:, f, NT * n:NT * n + NT] for x in wc], ff == 0, ff == KE - 1)
                    emark(last, ("chunk", 4 * UT + d))
                pe.wait_ge(selT_done, it + 1)
                for n in range(2):
                    pe.wait_ge(y_done, it * 2 + (n + 1))
                    if n == 0:
                        pe.wait_ge(x_lo_done, it + 2)
                    for b in range(3):
                        i = 3 * n + b
                        last = nc.tensor.matmul(banks[(6, 7, 2, 3, 4, 5)[i]][:, :], selT[:, b, :],
                                                y_exp[:, NT * n:NT * n + NT], start=True, stop=True)
                        emark(last, ("scattered", i))

            with pe.Fori(0, rounds) as r:
                with pe.Fori(0, NE) as e:
                    expert(r * NE + e)
            step["per_expert"] = count[0] - base

        def at(eng, *key):
            eng.wait_ge(pe_done, step[key if len(key) > 1 else key[0]])

        def at_tile(eng, name, j):
            at(eng, "tile", TN[(name, j)])
            return banks[TN[(name, j)] % BANKS]

        def at_expert(eng, it, *key):
            eng.wait_ge(pe_done, it * step["per_expert"] + step[("e",) + key])

        def slot_free(eng, n):
            if n >= SPLIT:
                at(eng, "chunk", n - SPLIT)

        def slot_free_in_loop(eng, it, c):
            if c >= SPLIT:
                at_expert(eng, it, "chunk", c - SPLIT)
            else:
                eng.wait_ge(pe_done, it * step["per_expert"] + (step[("e", "chunk", EC + c - SPLIT)] - step["per_expert"]))

        @block.sync
        def _(sp):
            sp.dma_start(con[:], consts).then_inc(in_const, 16)
            for b, (t0, n) in enumerate(TB):
                sp.dma_start(x_in[0:n, b, :], x_tok[t0:t0 + n, :]).then_inc(in_x, 16)
            sp.dma_start(par[:], params).then_inc(in_par, 16)

            for n, (name, j, cols) in enumerate(PLAN):
                if n >= RAW:
                    sp.wait_ge(lo_done, n - RAW + 1)
                src = source(name, j)
                sp.dma_start(raw[n % RAW][:, 0:cols].rearrange("p (k n) -> p k n", k=src.shape[1]), src)\
                    .then_inc(landed[n % RAW], 16)

            def expert_loads(it, e, chunks=EC):
                up = w["m_w_gate_up"][0, bass.ds(e, 1)].rearrange("a (k p) n -> p (a k) n", p=P)
                dn = w["m_w_down"][0, bass.ds(e, 1)].rearrange("a (k p) n -> p (a k) n", p=P)
                for c in range(chunks):
                    slot = (NC0 + c) % RAW
                    sp.wait_ge(lo_done, it * EC + (NC0 + c - RAW + 1))
                    if c < 4 * UT:
                        j, g, kh = c // 4, c // 2 % 2, c % 2
                        src = up[:, 4 * kh:4 * kh + 4, EF * g + NT * j:EF * g + NT * j + NT]
                    else:
                        f = 2 * (c - 4 * UT)
                        src = dn[:, f:f + 2, :]
                    sp.dma_start(raw[slot][:].rearrange("p (k n) -> p k n", k=src.shape[1]), src)\
                        .then_inc(landed[slot], 16)

            with sp.Fori(0, NE) as e:
                expert_loads(e, e)
            sp.wait_ge(rounds_ready, 1)
            rounds = sp.value_load(rounds_i[0:1, 0:1], min_val=1, max_val=3)
            with sp.If(rounds > 1):
                with sp.Fori(1, rounds) as r:
                    with sp.Fori(0, NE) as e:
                        expert_loads(r * NE + e, e)
            expert_loads(rounds * NE, 0, 2)
            sp.wait_ge(fin_done, 3)
            sp.dma_start(out[0:P - META, :], y_acc[META:P, 0, :]).then_inc(out_written, 16)
            sp.dma_start(out[P - META:2 * P - META, :], y_acc[:, 1, :]).then_inc(out_written, 16)
            sp.dma_start(out[2 * P - META:SEQ, :], y_acc[0:META, 2, :]).then_inc(out_written, 16)
            sp.wait_ge(out_written, 48)

        @block.gpsimd
        def _(pool):
            pool.wait_ge(krope_done, 1)
            at(pool, "tile", TN[("cq", KQ - 1)])
            nc.gpsimd.tensor_copy(kT[NOPE:QK, :, :], rope_a[NOPE:QK, None, :].to_broadcast([ROPE, HEADS, T]))\
                .then_inc(krope_copied, 1)
            pool.wait_ge(res_done, RES["bo"] + 1)
            pool.dma_start(m_gain, gain_rows[0:1, 0:D].to_broadcast([P, D])).then_inc(in_rows, 16)
            pool.dma_start(grow[:], gain_rows[0:1, D:2 * D].to_broadcast([P, D])).then_inc(in_rows, 16)
            pool.dma_start(rbias[:], gain_rows[0:1, 2 * D:2 * D + NE].to_broadcast([P, NE])).then_inc(in_rows, 16)
            pool.wait_ge(res_done, RES["bo"] + KD)
            nc.gpsimd.memset(u_thi[:, 2, :].bitcast(F32), 0.0)
            nc.gpsimd.memset(u_tlo[:, 2, :].bitcast(F32), 0.0).then_inc(pads_zeroed, 1)
            pool.wait_ge(in_rows, 48)
            for b, (t0, n) in enumerate(TB):
                pool.wait_ge(h_scaled, b + 1)
                nc.gpsimd.tensor_tensor(y_acc[0:n, b, :], y_acc[0:n, b, :], m_gain[0:n, :], ALU.mult)\
                    .then_inc(u_f32_done, 1)
            for b, (t0, n) in enumerate(TB):
                pool.wait_ge(u_hi_done, b + 1)
                nc.gpsimd.tensor_tensor(u_tlo[0:n, b, :], y_acc[0:n, b, :], u_thi[0:n, b, :].bitcast(F32),
                                        ALU.subtract).then_inc(u_tok_done, 1)
            pool.wait_ge(u_tok_done, 3)
            nc.gpsimd.memset(y_acc[:], 0.0).then_inc(added, 1)

        @block.scalar
        def _(act):
            issued = [0]

            def ahead(n):
                while issued[0] <= min(n, NC0 - 1):
                    c = issued[0]
                    name, j, cols = PLAN[c]
                    act.wait_ge(landed[c % RAW], 16 * (c // RAW + 1))
                    slot_free(act, c)
                    src, dst = raw[c % RAW][:, 0:cols], w_hi[c % SPLIT]
                    dst = dst[:, 0:cols] if name not in ("dkr", "uq") else dst[:, :]
                    for d, s in pieces(name, source(name, j).shape[1], src, dst):
                        last = nc.scalar.copy(d, s)
                    last.then_inc(hi_done, 1)
                    issued[0] += 1

            def empty(name, j, dst, func=ACT.Copy, rows=None, **kw):
                ps = at_tile(act, name, j)
                nc.scalar.activation(dst, ps[rows or slice(0, P), 0:dst.shape[-1]], func, **kw)\
                    .then_inc(emptied["A"], 1)

            def empty_squared(name, m, dst, square):
                ps = at_tile(act, name, m)
                nc.scalar.activation(dst, ps[:, 0:T], ACT.Copy)
                nc.scalar.activation(square, ps[:, 0:T], ACT.Square).then_inc(emptied["A"], 1)

            def squares(after, n):
                for k in range(KD):
                    act.wait_ge(after, n + k + 1)
                    nc.scalar.activation(sq[:, k, :], hT[:, k, :], ACT.Square).then_inc(sq_ready, 1)

            def root(name):
                i, kn = NORM[name], NORMS[NORM[name]][1]
                at(act, "sum", name)
                nc.scalar.activation(rstd[:, i % 2, :], banks[6 + i % 2][:, 0:T], ACT.Sqrt, bias=eps,
                                     scale=1.0 / (kn * P)).then_inc(root_taken, 1)

            def rounded(name, dst, src, kn):
                for k in range(kn):
                    act.wait_ge(norm_f32, NORMED[name] + k + 1)
                    nc.scalar.copy(dst[:, k, 0:T], src[:, k, :]).then_inc(act_hi, 1)

            ahead(1)
            squares(emptied["V"], 0)
            ahead(2)
            act.wait_ge(in_par, 16)
            root("a")
            rounded("a", u_hi, sq, KD)
            act.wait_ge(lam_abs, 1)
            nc.scalar.activation(lt[2], lt[1], ACT.Exp, scale=-1.0).then_inc(lam_exp, 1)
            for j in range(RB // 2):
                ahead(CH[("xr", j)] + 2)
                for m in (2 * j, 2 * j + 1):
                    empty("xr", m, xr_gy[:, m, CONV - 1:])
                for m in range(2 * j - 2, 2 * j) if j else ():
                    act.wait_ge(conv_done, m + 1)
                    nc.scalar.copy(xc_hi[:, m, :], xc[:, m, :]).then_inc(xc_hi_done, 1)
            for m in (RB - 2, RB - 1):
                act.wait_ge(conv_done, m + 1)
                nc.scalar.copy(xc_hi[:, m, :], xc[:, m, :]).then_inc(xc_hi_done, 1)
            ahead(CH[("y", 0)])
            for m in range(RB):
                empty("r", m, r_la[:, m, :], ACT.Sigmoid, bias=pr("ga_b", m))
                empty("i", m, ig[:, m, :], ACT.Sigmoid, bias=pr("gx_b", m))

            def take_y(j):
                ahead(CH[("y", j)] + 2)
                for m in (2 * j, 2 * j + 1):
                    empty("y", m, xr_gy[:, m, 0:T])

            for half in range(2):
                act.wait_ge(loga_ready, half + 1)
                if half:
                    act.wait_ge(scan_done, 1)
                a = r_la[:, half * HB:half * HB + HB, :]
                nc.scalar.activation(th, a, ACT.Tanh)
                nc.scalar.activation(a, a, ACT.Exp).then_inc(a_ready, 1)
                take_y(2 * half)
                act.wait_ge(root_in, half + 1)
                nc.scalar.activation(th, th, ACT.Sqrt, scale=-1.0).then_inc(root_done, 1)
                take_y(2 * half + 1)
            take_y(4)

            def gelu_half(half):
                y = xr_gy[:, half * HB:half * HB + HB, 0:T]
                act.wait_ge(emptied["A"], EMPTIED[TN[("y", half * HB + HB - 1)]])
                nc.scalar.activation(y, y, ACT.Gelu_apprx_tanh).then_inc(gelu_done, 1)

            gelu_half(0)
            gelu_half(1)
            for half in range(2):
                act.wait_ge(z_f32, half + 1)
                nc.scalar.copy(xc_hi[:, half * HB:half * HB + HB, :], xc[:, half * HB:half * HB + HB, :])\
                    .then_inc(z_hi, 1)
            for m in range(KD):
                ahead(CH[("a_out", m)] + 2)
                empty_squared("a_out", m, mix[:, m, :], sq[:, m, :])
            root("ao")
            squares(res_done, RES["ao"])
            root("f")
            rounded("f", u_hi, sq, KD)

            def f_round(m):
                act.wait_ge(emptied["V"], EMPTIED[TN[("f_u", m)]])
                nc.scalar.copy(hid_hi[:, m, :], f_h[:, m % 4, :]).then_inc(fhi_done, 1)

            for j in range(KF // 2):
                ahead(CH[("f_gate", j)] + 2)
                for m in (2 * j, 2 * j + 1):
                    if m >= 2:
                        act.wait_ge(emptied["V"], EMPTIED[TN[("f_u", m - 2)]])
                    empty("f_g", m, f_silu[:, m % 2, :], ACT.Silu)
                ahead(CH[("f_up", j)] + 2)
                if j:
                    f_round(2 * j - 2)
                    f_round(2 * j - 1)
            f_round(KF - 2)
            f_round(KF - 1)
            for q in range(KD // 2):
                for r in range(3):
                    ahead(CH[("f_down", 3 * q + r)] + 2)
                for m in (2 * q, 2 * q + 1):
                    empty_squared("f_down", m, mix[:, m, :], sq[:, m, :])
            root("fo")
            squares(res_done, RES["fo"])
            root("b")
            rounded("kv", u_hi, sq, KD)
            rounded("b", ub_hi, mix, KD)
            ahead(CH[("dkv", 0)] + 2)
            for m in range(KL):
                empty_squared("ckv", m, ckv[:, m, :], sq[:, m, :])
            ahead(CH[("dkr", 0)] + 2)
            for m in range(KQ):
                ahead(CH[("dq", m // 2)] + 2)
                empty_squared("cq", m, cq[:, m, :], sq[:, KL + m, :])
                if m == 0:
                    root("ckv")
            root("cq")
            rounded("ckv", ckv_hi, ckv, KL)
            rounded("cq", cq_hi, cq, KQ)
            for half in range(2):
                ahead(CH[("ukv", half)] + 2)
                for m in range(4 * half, 4 * half + 4):
                    ps = at_tile(act, "kn", m)
                    nc.scalar.copy(kT[0:NOPE, 2 * m, :], ps[0:NOPE, 0:T])
                    nc.scalar.copy(kT[0:NOPE, 2 * m + 1, :], ps[NOPE:P, 0:T]).then_inc(emptied["A"], 1)
                for b, (t0, n) in enumerate(TB):
                    empty("v", (b, half), v_tok[0:n, b, 512 * half:512 * half + 512], rows=slice(0, n))
            for h in range(HEADS + LAG + 2):
                if h < HEADS:
                    if h % 4 == 0:
                        g = h // 4
                        ahead(CH[("uq", g)] + 2)
                        for m in (2 * g, 2 * g + 1):
                            ps = at_tile(act, "qn", m)
                            i = 2 * (m % 2)
                            nc.scalar.copy(qT[0:NOPE, i, :], ps[0:NOPE, 0:T])
                            nc.scalar.copy(qT[0:NOPE, i + 1, :], ps[NOPE:P, 0:T]).then_inc(emptied["A"], 1)
                    act.wait_ge(max_done, h + 1)
                    for b, (t0, n) in enumerate(TB):
                        c, kn = SC[b]
                        i = 3 * (h % 3) + b
                        last = nc.scalar.activation(s_sb[0:n, h % 3, c:c + kn], s_sb[0:n, h % 3, c:c + kn], ACT.Exp,
                                                    bias=nbias[0:n, i:i + 1], scale=QK ** -0.5,
                                                    accum_out=rsum[0:n, i:i + 1])
                    last.then_inc(exp_done, 1)
                if LAG <= h < HEADS + LAG:
                    t = h - LAG
                    ps = at_tile(act, "pt", t)
                    if t >= 2:
                        at(act, "tile", TN[("o", t - 2)])
                    nc.scalar.copy(pT[:, t % 2, 0:416], ps[:, 0:416])
                    nc.scalar.copy(pT[0:META, t % 2, 416:432], ps[0:META, 416:432]).then_inc(emptied["A"], 1)
                if LAG < h < HEADS + LAG + 1:
                    t = h - LAG - 1
                    r = VD * (t % 2)
                    empty("o", t, sq[r:r + VD, t // 2, :], rows=slice(0, VD))
                if h >= LAG + 3 and h % 2:
                    k = (h - LAG - 3) // 2
                    act.wait_ge(emptied["A"], EMPTIED[TN[("o", 2 * k + 1)]])
                    nc.scalar.copy(u_hi[:, k, :], sq[:, k, :]).then_inc(act_hi, 1)
            for j in range(4):
                ahead(CH[("b_out", j)] + 2)
                for m in (2 * j, 2 * j + 1):
                    empty_squared("b_out", m, mix[:, m, :], sq[:, m, :])

            def split(it, c, free):
                slot = (NC0 + c) % RAW
                act.wait_ge(landed[slot], it * (16 * EC // RAW) + 16 * ((NC0 + c) // RAW + 1))
                free()
                nc.scalar.copy(w_hi[(NC0 + c) % SPLIT][:], raw[slot][:]).then_inc(hi_done, 1)

            root("bo")
            for c in range(2):
                split(0, c, lambda: slot_free(act, NC0 + c))

            for half in range(2):
                for b, (t0, n) in enumerate(TB):
                    at(act, "h_tok", b, half)
                    nc.scalar.copy(h_tok[0:n, b, 512 * half:512 * half + 512], banks[2 * b + half][0:n, :])\
                        .then_inc(h_tok_done, 1)
            act.wait_ge(h_tok_done, 6)
            for b, (t0, n) in enumerate(TB):
                nc.scalar.activation(y_acc[0:n, b, :], h_tok[0:n, b, :], ACT.Square,
                                     accum_out=mss[0:n, b:b + 1]).then_inc(hsum_done, 1)
            act.wait_ge(hsum_done, 3)
            nc.scalar.activation(mrs, mss, ACT.Sqrt, bias=eps, scale=1.0 / D).then_inc(rstd_t, 1)
            act.wait_ge(mrs_done, 1)
            for b, (t0, n) in enumerate(TB):
                nc.scalar.activation(y_acc[0:n, b, :], h_tok[0:n, b, :], ACT.Copy, scale=mrs[0:n, b:b + 1])\
                    .then_inc(h_scaled, 1)
            act.wait_ge(logit_in, 1)
            nc.scalar.activation(rt[:, 2, :], rt[:, 2, :], ACT.Exp).then_inc(logit_exp, 1)
            act.wait_ge(pads_zeroed, 1)
            for b, (t0, n) in enumerate(TB):
                act.wait_ge(u_f32_done, b + 1)
                nc.scalar.copy(u_thi[0:n, b, :], y_acc[0:n, b, :]).then_inc(u_hi_done, 1)

            def take_x():
                xf = x_hi[:].rearrange("p k n -> p (k n)")
                nc.scalar.copy(xf[:, 0:512], banks[0][:, :])
                nc.scalar.copy(xf[:, 512:1024], banks[1][:, :]).then_inc(x_hi_done, 1)

            at(act, "first_x", 0)
            take_x()
            act.wait_ge(rounds_ready, 1)
            rounds = act.value_load(rounds_i[0:1, 0:1], min_val=1, max_val=3)

            def expert(it):
                for c in range(EC):
                    split(it, c + 2, lambda: slot_free_in_loop(act, it, c + 2))
                    if c % 4 == 0 and 1 <= c // 4 <= UT:
                        j = c // 4 - 1
                        at_expert(act, it, "up", j)
                        if j:
                            act.wait_ge(eh_done, it * UT + j)
                        nc.scalar.activation(e_silu[:], banks[2 * (j % 2)][:, :], ACT.Silu).then_inc(silu_done, 1)
                    if c % 4 == 0 and 2 <= c // 4 <= UT + 1:
                        j = c // 4 - 2
                        at_expert(act, it, "turned", j)
                        nc.scalar.copy(eh_hi[:, 4 * j:4 * j + 4, :],
                                       banks[6][:, :].rearrange("p (f n) -> p f n", f=4)).then_inc(eh_hi_done, 1)
                    if c == 4 * UT + 6:
                        at_expert(act, it, "selT")
                        nc.scalar.copy(selT[:], banks[6][:, 0:3 * P].rearrange("p (b n) -> p b n", b=3))\
                            .then_inc(selT_done, 1)
                    if c == 4 * UT + 10:
                        at_expert(act, it, "x", 0)
                        take_x()
                at_expert(act, it, "chunk", EC - 1)
                act.wait_ge(gate_done, it + 1)
                for n in range(2):
                    nc.scalar.activation(y_exp[:, NT * n:NT * n + NT], banks[4 + n][:, :], ACT.Copy,
                                         scale=cur[:, 6:7]).then_inc(y_done, 1)

            with act.Fori(0, rounds) as r:
                with act.Fori(0, NE) as e:
                    expert(r * NE + e)

            act.wait_ge(added, rounds * (NE * 6) + 1)
            for b, (t0, n) in enumerate(TB):
                for half in range(2):
                    i = 2 * b + half
                    nc.scalar.activation(e_h[0:n, half, :], y_acc[0:n, b, 512 * half:512 * half + 512],
                                         ACT.Square, accum_out=small[0:n, 220 + i:221 + i]).then_inc(fin_sum, 1)
                    act.wait_ge(fin_sum, i + 1)
            act.wait_ge(fin_std, 1)
            nc.scalar.activation(mrs, mss, ACT.Sqrt, bias=eps, scale=1.0 / D).then_inc(fin_std, 1)

        @block.vector
        def _(dve):
            issued = [0]
            steps = [0]

            def link(ins):
                ins.then_inc(dve_step, 1)
                steps[0] += 1
                dve.wait_ge(dve_step, steps[0])

            def ahead(n):
                while issued[0] <= min(n, NC0 - 1):
                    c = issued[0]
                    name, j, cols = PLAN[c]
                    dve.wait_ge(hi_done, c + 1)
                    k = source(name, j).shape[1]
                    full = name in ("dkr", "uq")
                    src, hi, lo = raw[c % RAW][:, 0:cols], w_hi[c % SPLIT][:], w_lo[c % SPLIT][:]
                    if not full:
                        hi, lo = hi[:, 0:cols], lo[:, 0:cols]
                    for (d, s), (h, _) in zip(pieces(name, k, src, lo), pieces(name, k, src, hi.bitcast(F32))):
                        last = nc.vector.tensor_tensor(d, s, h, ALU.subtract)
                    last.then_inc(lo_done, 1)
                    issued[0] += 1

            def reciprocal_of_root(name):
                i = NORM[name]
                dve.wait_ge(root_taken, i + 1)
                link(nc.vector.reciprocal(rstd[:, i % 2, :], rstd[:, i % 2, :]))
                return rstd[:, i % 2, :]

            def scaled(dst, src, gain, k, r):
                return nc.vector.scalar_tensor_tensor(out=dst[:, k, :], in0=src[:, k, :], scalar=pr(gain, k),
                                                      in1=r, op0=ALU.mult, op1=ALU.mult)

            def normalise(parts, r):
                blocks = [(p, k) for p in parts for k in range(p[6])]
                for i in range(len(blocks) + 2):
                    if i < len(blocks):
                        (name, lo, hi, dst, src, gain, _), k = blocks[i]
                        scaled(dst, src, gain, k, r).then_inc(norm_f32, 1)
                    if i >= 2:
                        (name, lo, hi, dst, src, gain, _), k = blocks[i - 2]
                        dve.wait_ge(act_hi, PART[name] + k + 1)
                        nc.vector.tensor_tensor(lo[:, k, 0:T], dst[:, k, :], hi[:, k, 0:T].bitcast(F32),
                                                ALU.subtract).then_inc(act_lo, 1)

            def residual(name, gain):
                r = reciprocal_of_root(name)
                for k in range(KD + 1):
                    if k < KD:
                        scaled(mix, mix, gain, k, r).then_inc(res_scaled, 1)
                    if k:
                        dve.wait_ge(res_scaled, RES[name] + k)
                        nc.vector.tensor_tensor(hT[:, k - 1, :], hT[:, k - 1, :], mix[:, k - 1, :], ALU.add)\
                            .then_inc(res_done, 1)
                dve.wait_ge(res_done, RES[name] + KD)

            link(nc.vector.memset(small[:], 0.0))
            link(nc.vector.memset(rsum, 1.0))
            for c in range(KD):
                ps = at_tile(dve, "hT", c)
                nc.vector.tensor_copy(hT[:, c, :], ps[:, 0:T]).then_inc(emptied["V"], 1)
            link(nc.vector.memset(xr_gy[:, :, 0:CONV - 1], 0.0))
            ahead(1)
            dve.wait_ge(in_par, 16)
            link(nc.vector.tensor_scalar(lt[0], pr("lam"), -1.0, None, ALU.mult))
            nc.vector.tensor_tensor(lt[1], pr("lam"), lt[0], ALU.max).then_inc(lam_abs, 1)
            normalise([("a", u_lo, u_hi, sq, hT, "a_pre", KD)], reciprocal_of_root("a"))
            ahead(2)

            def softplus():
                dve.wait_ge(lam_exp, 1)
                link(nc.vector.tensor_scalar(lt[3], lt[2], 2.0, None, ALU.add))
                link(nc.vector.reciprocal(lt[3], lt[3]))
                link(nc.vector.tensor_tensor(lt[3], lt[2], lt[3], ALU.mult))
                link(nc.vector.tensor_tensor(lt[4], lt[3], lt[3], ALU.mult))
                link(nc.vector.tensor_scalar(lt[5], lt[4], 1.0 / 19, None, ALU.mult))
                for d in (17, 15, 13, 11, 9, 7, 5, 3):
                    link(nc.vector.scalar_tensor_tensor(out=lt[5], in0=lt[5], scalar=1.0 / d, in1=lt[4],
                                                        op0=ALU.add, op1=ALU.mult))
                link(nc.vector.scalar_tensor_tensor(out=lt[5], in0=lt[5], scalar=1.0, in1=lt[3],
                                                    op0=ALU.add, op1=ALU.mult))
                link(nc.vector.tensor_scalar(lt[0], lt[0], 0.0, None, ALU.max))
                link(nc.vector.scalar_tensor_tensor(out=c8, in0=lt[5], scalar=2.0, in1=lt[0],
                                                    op0=ALU.mult, op1=ALU.add))
                link(nc.vector.tensor_scalar(c8, c8, -8.0, None, ALU.mult))

            def conv(m):
                dve.wait_ge(emptied["A"], EMPTIED[TN[("xr", m)]])
                link(nc.vector.tensor_scalar(xc[:, m, :], xr_gy[:, m, 0:T], pr("conv_w", m), pr("conv_b", m),
                                             ALU.mult, ALU.add))
                for k in range(1, CONV):
                    ins = nc.vector.scalar_tensor_tensor(out=xc[:, m, :], in0=xr_gy[:, m, k:k + T],
                                                         scalar=pr("conv_w", RB * k + m), in1=xc[:, m, :],
                                                         op0=ALU.mult, op1=ALU.add)
                    if k < CONV - 1:
                        link(ins)
                ins.then_inc(conv_done, 1)

            def conv_low(m):
                dve.wait_ge(xc_hi_done, m + 1)
                nc.vector.tensor_tensor(xc_lo[:, m, :], xc[:, m, :], xc_hi[:, m, :].bitcast(F32), ALU.subtract)\
                    .then_inc(xc_lo_done, 1)

            for j in range(RB // 2):
                ahead(CH[("xr", j)] + 2)
                conv(2 * j)
                conv(2 * j + 1)
                if j:
                    conv_low(2 * j - 2)
                    conv_low(2 * j - 1)
            conv_low(RB - 2)
            conv_low(RB - 1)
            ahead(CH[("y", 0)])
            softplus()
            for half in range(2):
                hs = slice(half * HB, half * HB + HB)
                dve.wait_ge(emptied["A"], EMPTIED[TN[("i", half * HB + HB - 1)]])
                nc.vector.tensor_tensor(r_la[:, hs, :], r_la[:, hs, :], c8[:, hs, None].to_broadcast([P, HB, T]),
                                        ALU.mult).then_inc(loga_ready, 1)
                nc.vector.tensor_tensor(ig[:, hs, :], ig[:, hs, :], xc[:, hs, :], ALU.mult).then_inc(gated, 1)
            for half in range(2):
                hs = slice(half * HB, half * HB + HB)
                if half == 0:
                    dve.wait_ge(gated, 2)
                dve.wait_ge(a_ready, half + 1)
                link(nc.vector.tensor_tensor(xc[:, hs, :], r_la[:, hs, :], r_la[:, hs, :], ALU.mult))
                nc.vector.scalar_tensor_tensor(out=th, in0=xc[:, hs, :], scalar=1.0, in1=th, op0=ALU.add,
                                               op1=ALU.mult).then_inc(root_in, 1)
                ahead(CH[("y", 2 * half)] + 2)
                dve.wait_ge(root_done, half + 1)
                link(nc.vector.tensor_tensor(ig[:, hs, :], ig[:, hs, :], th, ALU.mult))
                for i in range(half * HB, half * HB + HB):
                    last = nc.vector.tensor_tensor_scan(xc[:, i, :], r_la[:, i, :], ig[:, i, :], 0.0,
                                                        ALU.mult, ALU.add)
                last.then_inc(scan_done, 1)
                ahead(CH[("y", 2 * half + 1)] + 2)
            ahead(CH[("y", 4)] + 2)
            dve.wait_ge(scan_done, 2)
            for half in range(2):
                hs = slice(half * HB, half * HB + HB)
                dve.wait_ge(gelu_done, half + 1)
                nc.vector.tensor_tensor(xc[:, hs, :], xc[:, hs, :], xr_gy[:, hs, 0:T], ALU.mult).then_inc(z_f32, 1)
            for half in range(2):
                hs = slice(half * HB, half * HB + HB)
                dve.wait_ge(z_hi, half + 1)
                nc.vector.tensor_tensor(xc_lo[:, hs, :], xc[:, hs, :], xc_hi[:, hs, :].bitcast(F32), ALU.subtract)\
                    .then_inc(z_lo, 1)
            for m in range(KD):
                ahead(CH[("a_out", m)] + 2)
            residual("ao", "a_post")
            normalise([("f", u_lo, u_hi, sq, hT, "f_pre", KD)], reciprocal_of_root("f"))

            def f_low(m):
                dve.wait_ge(fhi_done, m + 1)
                nc.vector.tensor_tensor(hid_lo[:, m, :], f_h[:, m % 4, :], hid_hi[:, m, :].bitcast(F32), ALU.subtract)\
                    .then_inc(flo_done, 1)

            for j in range(KF // 2):
                ahead(CH[("f_gate", j)] + 2)
                ahead(CH[("f_up", j)] + 2)
                for m in (2 * j, 2 * j + 1):
                    ps = at_tile(dve, "f_u", m)
                    dve.wait_ge(emptied["A"], EMPTIED[TN[("f_g", m)]])
                    if m >= 4:
                        dve.wait_ge(flo_done, m - 3)
                    nc.vector.tensor_tensor(f_h[:, m % 4, :], ps[:, 0:T], f_silu[:, m % 2, :], ALU.mult)\
                        .then_inc(emptied["V"], 1)
                if j:
                    f_low(2 * j - 2)
                    f_low(2 * j - 1)
            f_low(KF - 2)
            f_low(KF - 1)
            for q in range(KD // 2):
                for r in range(3):
                    ahead(CH[("f_down", 3 * q + r)] + 2)
            residual("fo", "f_post")
            normalise([("kv", u_lo, u_hi, sq, hT, "kv_norm", KD), ("b", ub_lo, ub_hi, mix, hT, "b_pre", KD)],
                      reciprocal_of_root("b"))
            nc.vector.memset(ckv_hi[:, :, T:].bitcast(F32), 0.0)
            nc.vector.memset(ckv_lo[:, :, T:].bitcast(F32), 0.0)
            ahead(CH[("dkv", 0)] + 2)
            ahead(CH[("dkr", 0)] + 2)
            ps = at_tile(dve, "krope", 0)
            nc.vector.tensor_tensor(rope_a[NOPE:QK, :], ps[NOPE:QK, 0:T], cn("cos")[NOPE:QK, :], ALU.mult)
            ins = nc.vector.tensor_tensor(k_temp[NOPE:QK, :], ps[0:ROPE, 0:T], cn("sin")[0:ROPE, :], ALU.mult)
            ins.then_inc(emptied["V"], 1)
            dve.wait_ge(emptied["V"], EMPTIED[TN[("krope", 0)]])
            nc.vector.tensor_tensor(rope_a[NOPE:QK, :], rope_a[NOPE:QK, :], k_temp[NOPE:QK, :], ALU.add)\
                .then_inc(krope_done, 1)
            ahead(CH[("dq", 1)] + 2)
            normalise([("ckv", ckv_lo, ckv_hi, ckv, ckv, "latent", KL)], reciprocal_of_root("ckv"))
            normalise([("cq", cq_lo, cq_hi, cq, cq, "q_norm", KQ)], reciprocal_of_root("cq"))
            ahead(CH[("ukv", 0)] + 2)
            ahead(CH[("ukv", 1)] + 2)
            nc.vector.tensor_tensor(gw[:], pr("router_w").rearrange("p (k e) -> p k e", k=KD),
                                    pr("m_pre")[:, :, None].to_broadcast([P, KD, NE]), ALU.mult)
            nc.vector.memset(banks[6][:, 0:3 * NE], 0.0).then_inc(gw_done, 1)
            nc.vector.memset(cur[:], 0.0)
            dve.wait_ge(krope_copied, 1)
            for h in range(HEADS + LAG + 3):
                if h < HEADS:
                    if h % 4 == 0:
                        g = h // 4
                        ahead(CH[("uq", g)] + 2)
                        ps = at_tile(dve, "qro", g)
                        nc.vector.tensor_tensor(rope_a[:, :], ps[:, 0:T], cn("cos"), ALU.mult)\
                            .then_inc(emptied["V"], 1)
                        ps = at_tile(dve, "qsw", g)
                        nc.vector.tensor_tensor(rope_b[:, :], ps[:, 0:T], cn("sin"), ALU.mult)\
                            .then_inc(emptied["V"], 1)
                        dve.wait_ge(emptied["V"], EMPTIED[TN[("qsw", g)]])
                        link(nc.vector.tensor_tensor(rope_a[:, :], rope_a[:, :], rope_b[:, :], ALU.add))
                        for i in range(4):
                            last = nc.vector.tensor_copy(qT[NOPE:QK, i, :], rope_a[ROPE * i:ROPE * i + ROPE, :])
                        last.then_inc(qrope_done, 1)
                    if h >= 3:
                        at(dve, "tile", TN[("pt", h - 3)])
                    i = 3 * (h % 3)
                    for b, (t0, n) in enumerate(TB):
                        c, kn = SC[b]
                        ps = at_tile(dve, "s", (h, b))
                        nc.vector.tensor_tensor_reduce(s_sb[0:n, h % 3, c:c + kn], ps[0:n, 0:kn],
                                                       cn(f"mask{b}")[0:n, :], 1.0, -3.0e38, ALU.add, ALU.max,
                                                       smax[0:n, i + b:i + b + 1]).then_inc(emptied["V"], 1)
                    dve.wait_ge(emptied["V"], EMPTIED[TN[("s", (h, 2))]])
                    nc.vector.tensor_scalar(nbias[:, i:i + 3], smax[:, i:i + 3], -(QK ** -0.5), None, ALU.mult)\
                        .then_inc(max_done, 1)
                if 1 <= h < HEADS + 1:
                    t = h - 1
                    i = 3 * (t % 3)
                    dve.wait_ge(exp_done, t + 1)
                    link(nc.vector.reciprocal(rcp[:, i:i + 3], rsum[:, i:i + 3]))
                    for b, (t0, n) in enumerate(TB):
                        c, kn = SC[b]
                        last = nc.vector.tensor_scalar(s_sb[0:n, t % 3, c:c + kn], s_sb[0:n, t % 3, c:c + kn],
                                                       rcp[0:n, i + b:i + b + 1], None, ALU.mult)
                    last.then_inc(prob_done, 1)
                if h >= LAG + 4 and h % 2 == 0:
                    k = (h - LAG - 4) // 2
                    dve.wait_ge(act_hi, PART["o"] + k + 1)
                    nc.vector.tensor_tensor(u_lo[:, k, :], sq[:, k, :], u_hi[:, k, :].bitcast(F32), ALU.subtract)\
                        .then_inc(act_lo, 1)
            for j in range(4):
                ahead(CH[("b_out", j)] + 2)
            residual("bo", "b_post")

            def split(it, c):
                dve.wait_ge(hi_done, it * EC + (NC0 + c + 1))
                s = (NC0 + c) % SPLIT
                nc.vector.tensor_tensor(w_lo[s][:], raw[(NC0 + c) % RAW][:], w_hi[s][:].bitcast(F32), ALU.subtract)\
                    .then_inc(lo_done, 1)

            for c in range(2):
                split(0, c)

            a_, g_, lg, p_, o1, o2, pos, t_ = (rt[:, k, :] for k in range(8))
            cols = rt[:, 9, :]
            m1, i1, m2, i2, s_, t3, c_ = (cols[:, 3 * k:3 * k + 3] for k in range(7))

            def v3(x):
                return x.rearrange("p (b e) -> p b e", b=3)

            def wide(x):
                return x[:, :, None].to_broadcast([P, 3, NE])

            dve.wait_ge(rstd_t, 1)
            nc.vector.reciprocal(mrs, mrs).then_inc(mrs_done, 1)
            dve.wait_ge(mrs_done, 1)
            at(dve, "logits")
            link(nc.vector.tensor_tensor(v3(lg), v3(banks[6][:, 0:3 * NE]), wide(mrs), ALU.mult))
            dve.wait_ge(in_rows, 48)
            link(nc.vector.tensor_tensor(v3(lg), v3(lg), rbias[:, None, :].to_broadcast([P, 3, NE]), ALU.add))
            link(nc.vector.tensor_reduce(m1, v3(lg), AX_X, ALU.max))
            nc.vector.tensor_tensor(v3(lg), v3(lg), wide(m1), ALU.subtract).then_inc(logit_in, 1)
            dve.wait_ge(logit_exp, 1)
            link(nc.vector.tensor_reduce(s_, v3(lg), AX_X, ALU.add))
            link(nc.vector.reciprocal(s_, s_))
            link(nc.vector.tensor_tensor(v3(p_), v3(lg), wide(s_), ALU.mult))
            for m_, i_, o_ in ((m1, i1, o1), (m2, i2, o2)):
                link(nc.vector.tensor_reduce(m_, v3(p_), AX_X, ALU.max))
                link(nc.vector.tensor_tensor(v3(t_), v3(p_), wide(m_), ALU.is_equal))
                link(nc.vector.scalar_tensor_tensor(out=t_, in0=t_, scalar=-float(NE), in1=cn("expert"),
                                                    op0=ALU.mult, op1=ALU.add))
                link(nc.vector.tensor_reduce(i_, v3(t_), AX_X, ALU.min))
                link(nc.vector.tensor_scalar(i_, i_, float(NE), None, ALU.add))
                link(nc.vector.tensor_tensor(v3(o_), v3(cn("expert")), wide(i_), ALU.is_equal))
                link(nc.vector.scalar_tensor_tensor(out=p_, in0=o_, scalar=-2.0, in1=p_, op0=ALU.mult, op1=ALU.add))
            link(nc.vector.tensor_tensor(t_, o1, o2, ALU.add))
            nc.vector.tensor_tensor(v3(a_), v3(t_), wide(cn("valid")), ALU.mult).then_inc(assigned, 1)
            link(nc.vector.tensor_tensor(s_, m1, m2, ALU.add))
            link(nc.vector.reciprocal(s_, s_))
            nc.vector.tensor_tensor(m1, m1, s_, ALU.mult)
            link(nc.vector.tensor_tensor(m2, m2, s_, ALU.mult))
            nc.vector.tensor_tensor(v3(o1), v3(o1), wide(m1), ALU.mult)
            link(nc.vector.tensor_tensor(v3(o2), v3(o2), wide(m2), ALU.mult))
            link(nc.vector.tensor_tensor(g_, o1, o2, ALU.add))
            at(dve, "positions")
            link(nc.vector.scalar_tensor_tensor(out=pos, in0=banks[7][:, 0:3 * NE], scalar=1.0, in1=a_,
                                                op0=ALU.add, op1=ALU.mult))
            link(nc.vector.tensor_scalar(pos, pos, -1.0, None, ALU.add))

            def choose(e, linked):
                for b in range(3):
                    nc.vector.tensor_scalar(cur[:, b:b + 1], v3(pos)[:, b, bass.ds(e, 1)], 0.0, None, ALU.add)
                for b in range(3):
                    ins = nc.vector.tensor_scalar(cur[:, 3 + b:4 + b], v3(g_)[:, b, bass.ds(e, 1)], 0.0, None, ALU.add)
                linked(ins)
                for b in range(3):
                    ins = nc.vector.tensor_scalar(sel[:, b, :], cn("iota"), cur[:, b:b + 1], None, ALU.is_equal)
                ins.then_inc(sel_done, 1)
                for b in range(3):
                    ins = nc.vector.tensor_scalar(v3(pos)[:, b, bass.ds(e, 1)], cur[:, b:b + 1], -float(P), None,
                                                  ALU.add)
                linked(ins)

            choose(0, link)
            link(nc.vector.tensor_reduce(c_[:, 0:1], banks[7][:, 3 * NE:4 * NE], AX_X, ALU.max))
            nc.vector.tensor_scalar(c_[:, 1:2], c_[:, 0:1], float(P), 1.0, ALU.is_gt, ALU.add)
            link(nc.vector.tensor_scalar(c_[:, 2:3], c_[:, 0:1], 2.0 * P, None, ALU.is_gt))
            link(nc.vector.tensor_tensor(c_[:, 1:2], c_[:, 1:2], c_[:, 2:3], ALU.add))
            nc.vector.tensor_copy(rounds_i[0:1, 0:1], c_[0:1, 1:2]).then_inc(rounds_ready, 1)

            def take_x():
                xf = x_lo[:].rearrange("p k n -> p (k n)")
                nc.vector.tensor_copy(xf[:, 0:512], banks[2][:, :])
                nc.vector.tensor_copy(xf[:, 512:1024], banks[3][:, :]).then_inc(x_lo_done, 1)

            at(dve, "first_x", 1)
            take_x()
            dve.wait_ge(added, 1)
            dve.wait_ge(rounds_ready, 1)
            rounds = dve.value_load(rounds_i[0:1, 0:1], min_val=1, max_val=3)

            LINKS = 2

            def expert(it, e):
                done = [0]

                def elink(ins):
                    ins.then_inc(loop_step, 1)
                    done[0] += 1
                    dve.wait_ge(loop_step, it * LINKS + done[0])

                for c in range(EC):
                    split(it, c + 2)
                    if c % 4 == 0 and 1 <= c // 4 <= UT:
                        j = c // 4 - 1
                        dve.wait_ge(silu_done, it * UT + (j + 1))
                        if j >= 2:
                            at_expert(dve, it, "turned", j - 2)
                        nc.vector.tensor_tensor(e_h[:, j % 2, :], banks[2 * (j % 2) + 1][:, :], e_silu[:], ALU.mult)\
                            .then_inc(eh_done, 1)
                    if c % 4 == 0 and 2 <= c // 4 <= UT + 1:
                        j = c // 4 - 2
                        dve.wait_ge(eh_hi_done, it * UT + (j + 1))
                        nc.vector.tensor_tensor(eh_lo[:, 4 * j:4 * j + 4, :],
                                                banks[6][:, :].rearrange("p (f n) -> p f n", f=4),
                                                eh_hi[:, 4 * j:4 * j + 4, :].bitcast(F32), ALU.subtract)\
                            .then_inc(eh_lo_done, 1)
                    if c == 4 * UT + 2:
                        at_expert(dve, it, "gate")
                        nc.vector.tensor_copy(cur[:, 6:7], banks[7][:, 0:1]).then_inc(gate_done, 1)
                    if c == 4 * UT + 6:
                        at_expert(dve, it, "selT")
                        choose((e + 1) % NE, elink)
                    if c == 4 * UT + 10:
                        at_expert(dve, it, "x", 1)
                        take_x()
                for n in range(2):
                    for b in range(3):
                        i = 3 * n + b
                        at_expert(dve, it, "scattered", i)
                        y = y_acc[:, b, NT * n:NT * n + NT]
                        nc.vector.tensor_tensor(y, y, banks[(6, 7, 2, 3, 4, 5)[i]][:, :], ALU.add)\
                            .then_inc(added, 1)
                assert done[0] == LINKS

            with dve.Fori(0, rounds) as r:
                with dve.Fori(0, NE) as e:
                    expert(r * NE + e, e)

            dve.wait_ge(fin_sum, 6)
            halves = small[:, 220:226].rearrange("p (b h) -> p b h", h=2)
            nc.vector.tensor_reduce(mss, halves, AX_X, ALU.add).then_inc(fin_std, 1)
            dve.wait_ge(fin_std, 2)
            link(nc.vector.reciprocal(mrs, mrs))
            for b, (t0, n) in enumerate(TB):
                link(nc.vector.scalar_tensor_tensor(out=y_acc[0:n, b, :], in0=y_acc[0:n, b, :],
                                                    scalar=mrs[0:n, b:b + 1], in1=grow[0:n, :],
                                                    op0=ALU.mult, op1=ALU.mult))
                nc.vector.tensor_tensor(y_acc[0:n, b, :], y_acc[0:n, b, :], h_tok[0:n, b, :], ALU.add)\
                    .then_inc(fin_done, 1)


_WEIGHTS = ["a_w_in", "a_gate_a_w", "a_gate_x_w", "a_w_out", "kv_w_dkv", "kv_w_ukv", "b_w_dq", "b_w_uq", "b_w_o",
            "f_w_gate_up", "f_w_down", "m_w_gate_up", "m_w_down"]
_VECTORS = {"a_pre": "a_pre_norm", "conv_b": "a_conv_b", "ga_b": "a_gate_a_b", "gx_b": "a_gate_x_b",
            "lam": "a_lambda", "a_post": "a_post_norm", "kv_norm": "kv_norm", "latent": "kv_latent_norm",
            "b_pre": "b_pre_norm", "q_norm": "b_q_norm", "b_post": "b_post_norm", "f_pre": "f_pre_norm",
            "f_post": "f_post_norm", "m_pre": "m_pre_norm"}


def shape_constants():
    c = np.zeros((P, NCONST), np.float32)

    def put(name, x):
        c[:, CONST[name][0]:CONST[name][1]] = x

    put("ident", np.eye(P))
    put("ones", 1.0)
    put("tri", np.arange(P)[:, None] < np.arange(P)[None, :])
    put("iota", np.arange(P)[None, :])
    put("valid", [[float(i < n) for _, n in TB] for i in range(P)])
    put("expert", np.tile(np.arange(NE) + NE, 3)[None, :])
    for b, (t0, n) in enumerate(TB):
        width = CONST[f"mask{b}"][1] - CONST[f"mask{b}"][0]
        put(f"mask{b}", np.where(np.arange(width)[None, :] <= t0 + np.arange(P)[:, None], 0.0, -1.0e30))
    half = ROPE // 2
    inv = np.float32(10000.0) ** (-np.arange(0, ROPE, 2, dtype=np.float32) / np.float32(ROPE))
    ang = (np.arange(T, dtype=np.float32)[:, None] * inv[None, :]).astype(np.float32)
    cos, sin = np.cos(ang).T, np.sin(ang).T
    assert cos.shape == (half, T)
    put("cos", np.tile(cos, (P // half, 1)))
    put("sin", np.tile(np.concatenate([-sin, sin]), (P // ROPE, 1)))
    return c


def kernel(**inputs):
    import concourse.bacc as _bacc
    from concourse.bass_utils import run_bass_kernel_spmd as _run

    x = {k: np.ascontiguousarray(v) for k, v in inputs.items()}
    params = np.zeros((P, NPARAM), np.float32)

    def put(name, v):
        params[:, PARAM[name][0]:PARAM[name][1]] = v

    for name, key in _VECTORS.items():
        put(name, x[key].reshape(-1, P).T)
    put("conv_w", x["a_conv_w"].reshape(-1, P).T)
    put("router_w", x["m_router_w"][0].reshape(KD, P, NE).transpose(1, 0, 2).reshape(P, KD * NE))
    put("eps", EPS)
    arrays = {n: x[n] for n in _WEIGHTS}
    arrays["params"] = params
    arrays["consts"] = shape_constants()
    arrays["gain_rows"] = np.concatenate([x["m_pre_norm"].reshape(1, -1), x["m_post_norm"].reshape(1, -1),
                                          x["m_router_b"].reshape(1, -1)], axis=1)
    arrays["tokens"] = np.concatenate([x["meta_tokens"], x["x"][0]], axis=0)
    nc = _bacc.Bacc("TRN2", target_bir_lowering=False, num_devices=1)
    aps = {n: nc.dram_tensor(f"in_{n}", a.shape, F32, kind="ExternalInput").ap() for n, a in arrays.items()}
    out = nc.dram_tensor("out_0", (SEQ, D), F32, kind="ExternalOutput").ap()
    yoco_kernel(nc, aps, aps["params"], aps["consts"], aps["gain_rows"], aps["tokens"], out)
    r = _run(nc, [{f"in_{n}": a for n, a in arrays.items()}], core_ids=[0])
    return r.results[0]["out_0"].reshape(1, SEQ, D)
```

```python
from contextlib import ExitStack

import numpy as np
import concourse.bass as bass
from concourse import mybir

ALU = mybir.AluOpType
ACT = mybir.ActivationFunctionType
F32 = mybir.dt.float32
F32R = mybir.dt.float32r
I32 = mybir.dt.int32
AX_X = mybir.AxisListType.X

P = 128
D = 1024
KD = D // P
META, SEQ = 16, 256
T = META + SEQ
TB = [(0, 128), (128, 128), (256, 16)]
RNN = 1280
RB = RNN // P
HB = RB // 2
CONV = 4
HEADS, NOPE, ROPE, VD = 16, 64, 32, 64
QK = NOPE + ROPE
LORA, QLORA = 256, 384
KL, KQ = LORA // P, QLORA // P
FF = 3072
KF = FF // P
NE, TOPK = 8, 2
EF = 3584
NT = 512
UT = EF // NT
KE = EF // P
EPS = 1e-6

CHUNK = 2048
RAW, SPLIT = 6, 3
LAG = 2
BANKS = 6

PARAM = {}
_n = 0
for _name, _w in (("a_pre", KD), ("conv_w", CONV * RB), ("conv_b", RB), ("ga_b", RB), ("gx_b", RB), ("lam", RB),
                  ("a_post", KD), ("kv_norm", KD), ("latent", KL), ("b_pre", KD), ("q_norm", KQ), ("b_post", KD),
                  ("f_pre", KD), ("f_post", KD), ("m_pre", KD), ("eps", 1), ("router_w", KD * NE)):
    PARAM[_name] = (_n, _n + _w)
    _n += _w
NPARAM = _n

CONST = {}
_n = 0
for _name, _w in (("ident", P), ("ones", P), ("tri", P), ("iota", P), ("valid", 3), ("expert", 3 * NE),
                  ("mask0", 128), ("mask1", 256), ("mask2", T), ("cos", T), ("sin", T)):
    CONST[_name] = (_n, _n + _w)
    _n += _w
NCONST = _n


def chunk_plan():
    plan = [("xr", j, KD * 256) for j in range(RB // 2)]
    plan += [("y", 0, KD * 256), ("ga", 0, RB * P), ("gx", 0, RB * P)]
    plan += [("y", j, KD * 256) for j in range(1, RB // 2)]
    plan += [("a_out", j, RB * P) for j in range(KD)]
    for j in range(KF // 2):
        plan += [("f_gate", j, KD * 256), ("f_up", j, KD * 256)]
    plan += [("f_down", j, KD * 256) for j in range(12)]
    plan += [("dkv", 0, KD * LORA), ("dkr", 0, KD * ROPE), ("dq", 0, KD * 256), ("dq", 1, KD * 128)]
    plan += [("ukv", j, KL * D) for j in range(2)]
    plan += [("uq", j, KQ * 4 * QK) for j in range(4)]
    plan += [("b_out", j, KD * 256) for j in range(4)]
    return plan


PLAN = chunk_plan()
CH = {(name, j): n for n, (name, j, _) in enumerate(PLAN)}
NC0 = len(PLAN)
EC = 4 * UT + KE // 2
assert EC % RAW == 0 and EC % SPLIT == 0


def tile_plan():
    plan = [("hT", c, "V") for c in range(KD)]
    plan += [("xr", m, "A") for m in range(RB)]
    plan += [("y", 0, "A"), ("y", 1, "A")] + [(g, m, "A") for m in range(RB) for g in ("r", "i")]
    plan += [("y", m, "A") for m in range(2, RB)] + [("a_out", m, "A") for m in range(KD)]
    for j in range(KF // 2):
        plan += [("f_g", 2 * j, "A"), ("f_g", 2 * j + 1, "A"), ("f_u", 2 * j, "V"), ("f_u", 2 * j + 1, "V")]
    plan += [("f_down", m, "A") for m in range(KD)] + [("ckv", m, "A") for m in range(KL)] + [("krope", 0, "V")]
    plan += [("cq", m, "A") for m in range(KQ)]
    for half in range(2):
        plan += [("kn", 4 * half + m, "A") for m in range(4)] + [("v", (b, half), "A") for b in range(3)]
    def queries(g):
        return [("qn", 2 * g, "A"), ("qn", 2 * g + 1, "A"), ("qro", g, "V"), ("qsw", g, "V")]
    plan += queries(0)
    for h in range(HEADS):
        plan += [("s", (h, b), "V") for b in range(3)]
        if h % 4 == 1 and h // 4 < 3:
            plan += queries(h // 4 + 1)
        if h >= LAG:
            plan += [("pt", h - LAG, "A")]
        if h > LAG:
            plan += [("o", h - LAG - 1, "A")]
    for h in range(HEADS - LAG, HEADS):
        plan += [("pt", h, "A"), ("o", h - 1, "A")]
    plan += [("o", HEADS - 1, "A")]
    plan += [("b_out", m, "A") for m in range(KD)]
    return plan


TILES = tile_plan()
TN = {(name, j): n for n, (name, j, _) in enumerate(TILES)}
EMPTIED = [sum(x[2] == TILES[n][2] for x in TILES[:n + 1]) for n in range(len(TILES))]


NORMS = [("a", KD), ("ao", KD), ("f", KD), ("fo", KD), ("b", KD), ("ckv", KL), ("cq", KQ), ("bo", KD)]
NORM = {name: i for i, (name, _) in enumerate(NORMS)}
PARTS = [("a", KD), ("f", KD), ("kv", KD), ("b", KD), ("ckv", KL), ("cq", KQ), ("o", KD)]
PART = {name: sum(k for _, k in PARTS[:i]) for i, (name, _) in enumerate(PARTS)}
NORMED = PART
SCATTER = (2, 6, 10, 14, 18, 22)
GELUS = [(0, 8), (8, RB)]
RES = {"ao": 0, "fo": KD, "bo": 2 * KD}
SQ = {"a": 0, "f": KD, "b": 2 * KD, "m": 3 * KD}



def pieces(name, k, src, dst):
    if name == "dkr":
        s = src[:, 0:k * ROPE].rearrange("p (k n) -> p k n", k=k)
        d = dst[:, 0:k * 3 * ROPE].rearrange("p (k n) -> p k n", k=k)
        h = ROPE // 2
        return [(d[:, :, 0:h], s[:, :, h:ROPE]), (d[:, :, h:ROPE], s[:, :, 0:h]),
                (d[:, :, ROPE:2 * ROPE], s), (d[:, :, 2 * ROPE:3 * ROPE], s)]
    if name == "uq":
        s = src[:, 0:k * 4 * QK].rearrange("p (k h n) -> p k h n", k=k, h=4)
        d = dst[:, 0:k * 512].rearrange("p (k m) -> p k m", k=k)
        n, ro, sw = (d[:, :, a:b].rearrange("p k (h n) -> p k h n", h=4)
                     for a, b in ((0, 4 * NOPE), (4 * NOPE, 4 * QK), (4 * QK, 512)))
        h = ROPE // 2
        return [(n, s[:, :, :, 0:NOPE]), (ro, s[:, :, :, NOPE:QK]), (sw[:, :, :, 0:h], s[:, :, :, NOPE + h:QK]),
                (sw[:, :, :, h:ROPE], s[:, :, :, NOPE:NOPE + h])]
    if name == "ukv":
        out = []
        for r in range(k):
            s = src[:, r * D:(r + 1) * D].rearrange("p (h n) -> p h n", h=8)
            for part in range(2):
                d = dst[:, r * D + 512 * part:r * D + 512 * part + 512].rearrange("p (h n) -> p h n", h=8)
                out.append((d, s[:, :, 64 * part:64 * part + 64]))
        return out
    return [(dst, src)]


def yoco_kernel(nc, w, params, consts, gain_rows, x_tok, out):
    with ExitStack() as ctx:
        def sb(name, shape, dt=F32, stack=None):
            return (stack or ctx).enter_context(nc.sbuf_tensor(name, shape, dt))

        def sem(name):
            return ctx.enter_context(nc.semaphore(name))

        raw = [sb(f"raw{i}", [P, CHUNK]) for i in range(RAW)]
        w_hi = [sb(f"w_hi{i}", [P, CHUNK], F32R) for i in range(SPLIT)]
        w_lo = [sb(f"w_lo{i}", [P, CHUNK], F32R) for i in range(SPLIT)]
        par = sb("par", [P, NPARAM])
        con = sb("con", [P, NCONST])
        small = sb("small", [P, 256])
        banks = [ctx.enter_context(nc.psum_tensor(f"bank{i}", [P, 512], F32)) for i in range(8)]

        def pr(name, c=None):
            a, b = PARAM[name]
            return par[:, a:b] if c is None else par[:, a + c:a + c + 1]

        def cn(name):
            a, b = CONST[name]
            return con[:, a:b]

        ident, ones, eps = cn("ident"), cn("ones"), pr("eps")

        body = ExitStack()
        hT = sb("hT", [P, KD, T], stack=body)
        rstd = sb("rstd", [P, 2, T], stack=body)
        u_hi = sb("u_hi", [P, KD, T], F32R, stack=body)
        u_lo = sb("u_lo", [P, KD, T], F32R, stack=body)
        mix_sq = sb("mix_sq", [P, 2 * KD, T], stack=body)
        mix = mix_sq[:, 0:KD, :]
        sq = mix_sq[:, KD:2 * KD, :]

        with ExitStack() as ph:
            x_in = sb("x_in", [P, 3, D], stack=ph)
        with ExitStack() as ph:
            xr_gy = sb("xr_gy", [P, RB, T + CONV - 1], stack=ph)
            xc = sb("xc", [P, RB, T], stack=ph)
            xc_hi = sb("xc_hi", [P, RB, T], F32R, stack=ph)
            xc_lo = sb("xc_lo", [P, RB, T], F32R, stack=ph)
            ig = sb("ig", [P, RB, T], stack=ph)
        r_la = mix_sq[:, 0:RB, :]
        th = mix_sq[:, RB:RB + HB, :]
        with ExitStack() as ph:
            f_silu = sb("f_silu", [P, 2, T], stack=ph)
            f_h = sb("f_h", [P, 4, T], stack=ph)
            hid_hi = sb("hid_hi", [P, KF, T], F32R, stack=ph)
            hid_lo = sb("hid_lo", [P, KF, T], F32R, stack=ph)
        with ExitStack() as ph:
            qT_odd = sb("qT_odd", [QK, 4, T], stack=ph)
        with ExitStack() as ph:
            ckv = sb("ckv", [P, KL, T], stack=ph)
            ckv_hi = sb("ckv_hi", [P, KL, 3 * P], F32R, stack=ph)
            ckv_lo = sb("ckv_lo", [P, KL, 3 * P], F32R, stack=ph)
            cq = sb("cq", [P, KQ, T], stack=ph)
            cq_hi = sb("cq_hi", [P, KQ, T], F32R, stack=ph)
            cq_lo = sb("cq_lo", [P, KQ, T], F32R, stack=ph)
            with ExitStack() as ph2:
                ub_hi = sb("ub_hi", [P, KD, T], F32R, stack=ph2)
                ub_lo = sb("ub_lo", [P, KD, T], F32R, stack=ph2)
            kT = sb("kT", [QK, HEADS, T], stack=ph)
            v_tok = sb("v_tok", [P, 3, D], stack=ph)
            qT_even = sb("qT_even", [QK, 4, T], stack=ph)
            rope_a = sb("rope_a", [P, T], stack=ph)
            pT = sb("pT", [P, 2, 432], stack=ph)
        s_sb = mix.rearrange("p k n -> p (k n)")[:, 0:3 * 656].rearrange("p (h n) -> p h n", h=3)
        body.close()
        qT = (qT_even, qT_odd)
        k_temp, rope_b = qT_even[:, 0, :], cq[:, 0, :]
        SC = [(0, 128), (128, 256), (384, T)]

        eh_hi = sb("eh_hi", [P, KE, P], F32R)
        h_tok = sb("h_tok", [P, 3, D])
        h_thi = sb("h_thi", [P, 3, D], F32R)
        h_tlo = sb("h_tlo", [P, 3, D], F32R)
        y_acc = sb("y_acc", [P, 3, D])
        x_hi = sb("x_hi", [P, KD, P], F32R)
        x_lo = sb("x_lo", [P, KD, P], F32R)
        eh_lo = sb("eh_lo", [P, KE, P], F32R)
        e_silu = sb("e_silu", [P, NT])
        e_h = sb("e_h", [P, 2, NT])
        y_exp = sb("y_exp", [P, D])
        sel = sb("sel", [P, 3, P], F32R)
        selT = sb("selT", [P, 3, P])
        grow = sb("grow", [P, D])
        rbias = sb("rbias", [P, NE])
        gw = sb("gw", [P, KD, NE])
        rt = sb("rt", [P, 10, 3 * NE])
        cur = sb("cur", [P, 8])
        rounds_i = sb("rounds_i", [1, 1], I32)

        landed = [sem(f"landed{i}") for i in range(RAW)]
        hi_done, lo_done = sem("hi_done"), sem("lo_done")
        in_const, in_par, in_x, in_rows = sem("in_const"), sem("in_par"), sem("in_x"), sem("in_rows")
        pe_done = sem("pe_done")
        emptied = {"A": sem("emptied_by_act"), "V": sem("emptied_by_dve")}
        dve_step = sem("dve_step")
        sq_ready, root_taken, norm_f32, act_hi, act_lo, res_scaled, res_done = (
            sem("sq_ready"), sem("root_taken"), sem("norm_f32"), sem("act_hi"), sem("act_lo"), sem("res_scaled"),
            sem("res_done"))
        conv_done, xc_hi_done, xc_lo_done = sem("conv_done"), sem("xc_hi_done"), sem("xc_lo_done")
        lam_abs, lam_exp = sem("lam_abs"), sem("lam_exp")
        loga_ready, a_ready, root_in, root_done, scan_done = (
            sem("loga_ready"), sem("a_ready"), sem("root_in"), sem("root_done"), sem("scan_done"))
        gated, gelu_done = sem("gated"), sem("gelu_done")
        z_f32, z_hi, z_lo = sem("z_f32"), sem("z_hi"), sem("z_lo")
        fhi_done, flo_done = sem("fhi_done"), sem("flo_done")
        krope_done, krope_copied, qrope_done = sem("krope_done"), sem("krope_copied"), sem("qrope_done")
        max_done, exp_done, prob_done = sem("max_done"), sem("exp_done"), sem("prob_done")
        gw_done, rstd_t = sem("gw_done"), sem("h_std_done")
        h_lo_done, logit_in, logit_exp, assigned = (
            sem("h_lo_done"), sem("logit_in"), sem("logit_exp"), sem("assigned"))
        rounds_ready = sem("rounds_ready")
        h_tok_done = sem("h_tok_done")
        sel_done, x_hi_done, x_lo_done, selT_done, gate_done = (
            sem("sel_done"), sem("x_hi_done"), sem("x_lo_done"), sem("selT_done"), sem("gate_done"))
        silu_done, eh_done, eh_hi_done, eh_lo_done = (
            sem("silu_done"), sem("eh_done"), sem("eh_hi_done"), sem("eh_lo_done"))
        y_done, added = sem("y_done"), sem("added")
        h_hi_done, xs_done = sem("h_hi_done"), sem("xs_done")
        pads_zeroed, mrs_done = sem("pads_zeroed"), sem("mrs_done")
        loop_step = sem("loop_step")
        fin_sum, fin_std, fin_done, out_written = (
            sem("fin_sum"), sem("fin_std"), sem("fin_done"), sem("out_written"))

        c8 = small[:, 0:RB]
        lt = [small[:, 16 * k + 16:16 * k + 16 + RB] for k in range(6)]
        smax, nbias, rsum, rcp = (small[:, 112 + 16 * k:112 + 16 * k + 9] for k in range(4))
        mss, mrs = small[:, 192:195], small[:, 208:211]

        def rows(a):
            return a.rearrange("(k p) n -> p k n", p=P)

        w_in, w_ao, w_gu, w_dn = (rows(w[n][0]) for n in ("a_w_in", "a_w_out", "f_w_gate_up", "f_w_down"))
        w_dq, w_uq, w_bo = (rows(w[n][0]) for n in ("b_w_dq", "b_w_uq", "b_w_o"))
        w_dkv, w_ukv = rows(w["kv_w_dkv"]), rows(w["kv_w_ukv"])
        ga, gx = (w[n][0].rearrange("n c d -> c n d") for n in ("a_gate_a_w", "a_gate_x_w"))

        def source(name, j):
            return {
                "xr": lambda: w_in[:, :, RNN + 256 * j:RNN + 256 * j + 256],
                "y": lambda: w_in[:, :, 256 * j:256 * j + 256],
                "ga": lambda: ga, "gx": lambda: gx,
                "a_out": lambda: w_ao[:, :, P * j:P * j + P],
                "f_gate": lambda: w_gu[:, :, 256 * j:256 * j + 256],
                "f_up": lambda: w_gu[:, :, FF + 256 * j:FF + 256 * j + 256],
                "f_down": lambda: w_dn[:, KD * (j % 3):KD * (j % 3) + KD, 256 * (j // 3):256 * (j // 3) + 256],
                "dkv": lambda: w_dkv[:, :, 0:LORA],
                "dkr": lambda: w_dkv[:, :, LORA:LORA + ROPE],
                "dq": lambda: w_dq[:, :, 256 * j:min(256 * j + 256, QLORA)],
                "ukv": lambda: w_ukv[:, :, D * j:D * j + D],
                "uq": lambda: w_uq[:, :, 4 * QK * j:4 * QK * (j + 1)],
                "b_out": lambda: w_bo[:, :, 256 * j:256 * j + 256],
            }[name]()

        def split_views(n, buf):
            name, j, cols = PLAN[n]
            k = source(name, j).shape[1]
            cols = {"dkr": KD * 3 * ROPE, "uq": KQ * 512}.get(name, cols)
            return buf[n % SPLIT][:, 0:cols].rearrange("p (k n) -> p k n", k=k)

        step = {}
        block = ctx.enter_context(nc.Block())

        @block.tensor
        def _(pe):
            count = [0]

            def mark(ins, *keys):
                ins.then_inc(pe_done, 1)
                count[0] += 1
                for key in keys:
                    step[key] = count[0]

            def bank_of(name, j):
                n = TN[(name, j)]
                if n >= BANKS:
                    pe.wait_ge(emptied[TILES[n - BANKS][2]], EMPTIED[n - BANKS])
                return banks[n % BANKS]

            def chunk(name, j):
                n = CH[(name, j)]
                pe.wait_ge(lo_done, n + 1)
                return split_views(n, w_hi), split_views(n, w_lo)

            def product(o, a, b, start, stop):
                nc.tensor.matmul(o, a[0], b[0], start=start, stop=False)
                nc.tensor.matmul(o, a[0], b[1], start=False, stop=False)
                return nc.tensor.matmul(o, a[1], b[0], start=False, stop=stop)

            def columns_tile(name, m, wc, c0, act, kn, width=P, *keys, need=None, ready=None):
                ps = bank_of(name, m)
                for k in range(kn):
                    if need:
                        pe.wait_ge(act_lo, PART[need] + k + 1)
                    if ready:
                        pe.wait_ge(ready, k + 1)
                    last = product(ps[0:width, 0:T], [x[:, k, c0:c0 + width] for x in wc],
                                   [x[:, k, 0:T] for x in act], k == 0, k == kn - 1)
                mark(last, ("tile", TN[(name, m)]), *keys)

            def sum_block(name, src, k):
                kn = NORMS[NORM[name]][1]
                ps = banks[6 + NORM[name] % 2]
                last = nc.tensor.matmul(ps[:, 0:T], ones, src, start=(k == 0), stop=(k == kn - 1))
                if k == kn - 1:
                    mark(last, ("sum", name))

            def sum_taken(name):
                for k in range(KD):
                    pe.wait_ge(sq_ready, SQ[name] + k + 1)
                    sum_block(name, sq[:, k, :], k)

            def sum_emptied(name, tile, m, src):
                pe.wait_ge(emptied["A"], EMPTIED[TN[(tile, m)]])
                sum_block(name, src, m)

            u = (u_hi, u_lo)
            pe.wait_ge(in_const, 16)
            pe.wait_ge(in_x, 48)
            for c in range(KD):
                ps = bank_of("hT", c)
                for b, (t0, n) in enumerate(TB):
                    last = nc.tensor.transpose(ps[:, t0:t0 + n], x_in[0:n, b, c * P:(c + 1) * P], ident[0:n, 0:n])
                mark(last, ("tile", TN[("hT", c)]))
            sum_taken("a")
            for j in range(RB // 2):
                wc = chunk("xr", j)
                for m in (2 * j, 2 * j + 1):
                    columns_tile("xr", m, wc, P * (m % 2), u, KD, P, *([("chunk", CH[("xr", j)])] if m % 2 else []),
                                 need=None if m else "a")
            for m in range(2):
                columns_tile("y", m, chunk("y", 0), P * m, u, KD, P, *([("chunk", CH[("y", 0)])] if m else []))
            wa, wx = chunk("ga", 0), chunk("gx", 0)
            for m in range(RB):
                pe.wait_ge(xc_lo_done, m + 1)
                for name, wc, key in (("r", wa, "ga"), ("i", wx, "gx")):
                    ps = bank_of(name, m)
                    last = product(ps[:, 0:T], [x[:, m, :] for x in wc], (xc_hi[:, m, :], xc_lo[:, m, :]), True, True)
                    mark(last, ("tile", TN[(name, m)]), *([("chunk", CH[(key, 0)])] if m == RB - 1 else []))
            for j in range(1, RB // 2):
                wc = chunk("y", j)
                for m in (2 * j, 2 * j + 1):
                    columns_tile("y", m, wc, P * (m % 2), u, KD, P, *([("chunk", CH[("y", j)])] if m % 2 else []))
            for m in range(KD):
                columns_tile("a_out", m, chunk("a_out", m), 0, (xc_hi, xc_lo), RB, P, ("chunk", CH[("a_out", m)]),
                             ready=None if m else z_lo)
                if m:
                    sum_emptied("ao", "a_out", m - 1, sq[:, m - 1, :])
            sum_emptied("ao", "a_out", KD - 1, sq[:, KD - 1, :])
            sum_taken("f")
            for j in range(KF // 2):
                for name, key in (("f_g", "f_gate"), ("f_u", "f_up")):
                    wc = chunk(key, j)
                    for m in (2 * j, 2 * j + 1):
                        columns_tile(name, m, wc, P * (m % 2), u, KD, P, *([("chunk", CH[(key, j)])] if m % 2 else []),
                                     need="f" if (name, m) == ("f_g", 0) else None)
            for q in range(KD // 2):
                ps = [bank_of("f_down", 2 * q + i) for i in range(2)]
                for r in range(3):
                    wc = chunk("f_down", 3 * q + r)
                    if q == 0:
                        pe.wait_ge(flo_done, KD * (r + 1))
                    for i in range(2):
                        for k in range(KD):
                            f = KD * r + k
                            last = product(ps[i][:, 0:T], [x[:, k, P * i:P * i + P] for x in wc],
                                           (hid_hi[:, f, :], hid_lo[:, f, :]), f == 0, f == KF - 1)
                        if r == 2:
                            mark(last, ("tile", TN[("f_down", 2 * q + i)]),
                                 *([("chunk", CH[("f_down", 3 * q + r)])] if i else []))
                    if r < 2:
                        mark(last, ("chunk", CH[("f_down", 3 * q + r)]))
                if q:
                    for m in (2 * q - 2, 2 * q - 1):
                        sum_emptied("fo", "f_down", m, sq[:, m, :])
            for m in (KD - 2, KD - 1):
                sum_emptied("fo", "f_down", m, sq[:, m, :])
            sum_taken("b")
            wc = chunk("dkv", 0)
            for m in range(KL):
                columns_tile("ckv", m, wc, P * m, u, KD, P, *([("chunk", CH[("dkv", 0)])] if m else []),
                             need=None if m else "kv")
            columns_tile("krope", 0, chunk("dkr", 0), 0, u, KD, QK, ("chunk", CH[("dkr", 0)]))
            for m in range(KQ):
                columns_tile("cq", m, chunk("dq", m // 2), P * (m % 2), (ub_hi, ub_lo), KD, P,
                             *([("chunk", CH[("dq", m // 2)])] if m else []), need=None if m else "b")
                if m == 0:
                    for k in range(KL):
                        sum_emptied("ckv", "ckv", k, sq[:, k, :])
            for k in range(KQ):
                sum_emptied("cq", "cq", k, sq[:, KL + k, :])
            pe.wait_ge(act_lo, PART["ckv"] + KL)
            for half in range(2):
                wc = chunk("ukv", half)
                for m in range(4 * half, 4 * half + 4):
                    columns_tile("kn", m, wc, P * (m % 4), (ckv_hi, ckv_lo), KL)
                for b, (t0, n) in enumerate(TB):
                    ps = bank_of("v", (b, half))
                    for k in range(KL):
                        last = product(ps[:, :], [x[:, k, t0:t0 + P] for x in (ckv_hi, ckv_lo)],
                                       [x[:, k, 512:1024] for x in wc], k == 0, k == KL - 1)
                    mark(last, ("tile", TN[("v", (b, half))]), *([("chunk", CH[("ukv", half)])] if b == 2 else []))

            def turn_probs(h):
                pe.wait_ge(prob_done, h + 1)
                ps = bank_of("pt", h)
                p = s_sb[:, h % 3, :]
                for b, (t0, n) in enumerate(TB):
                    for kb in range(b + 1):
                        c, kn = SC[b][0] + P * kb, TB[kb][1]
                        o = (0, 144, 160)[kb] + t0
                        last = nc.tensor.transpose(ps[0:kn, o:o + n], p[0:n, c:c + kn], ident[0:n, 0:n])
                mark(last, ("tile", TN[("pt", h)]))

            def weigh(h):
                ps = bank_of("o", h)
                pe.wait_ge(emptied["A"], EMPTIED[TN[("pt", h)]])
                for kb, (t0, kn) in enumerate(TB):
                    o = (0, 144, 160)[kb] + t0
                    last = nc.tensor.matmul(ps[0:VD, t0:T], v_tok[0:kn, kb, VD * h:VD * h + VD], pT[0:kn, h % 2, o:o + T - t0],
                                            start=(kb == 0), stop=(kb == 2))
                mark(last, ("tile", TN[("o", h)]))

            pe.wait_ge(act_lo, PART["cq"] + KQ)
            def queries(g):
                wc = chunk("uq", g)
                for i, (name, m) in enumerate((("qn", 2 * g), ("qn", 2 * g + 1), ("qro", g), ("qsw", g))):
                    columns_tile(name, m, wc, P * i, (cq_hi, cq_lo), KQ, P, *([("chunk", CH[("uq", g)])] if i == 3 else []))

            queries(0)
            for h in range(HEADS):
                g = h // 4
                if h % 4 == 0:
                    pe.wait_ge(emptied["A"], EMPTIED[TN[("qn", 2 * g + 1)]])
                    pe.wait_ge(qrope_done, g + 1)
                    pe.wait_ge(krope_copied, 1)
                for b, (t0, n) in enumerate(TB):
                    ps = bank_of("s", (h, b))
                    mark(nc.tensor.matmul(ps[0:n, 0:SC[b][1]], qT[g % 2][:, h % 4, t0:t0 + n], kT[:, h, 0:SC[b][1]],
                                          start=True, stop=True), ("tile", TN[("s", (h, b))]))
                if h % 4 == 1 and g < 3:
                    queries(g + 1)
                if h >= LAG:
                    turn_probs(h - LAG)
                if h > LAG:
                    weigh(h - LAG - 1)
            for h in range(HEADS - LAG, HEADS):
                turn_probs(h)
                weigh(h - 1)
            weigh(HEADS - 1)
            for j in range(4):
                wc = chunk("b_out", j)
                for m in (2 * j, 2 * j + 1):
                    columns_tile("b_out", m, wc, P * (m % 2), u, KD, P, *([("chunk", CH[("b_out", j)])] if m % 2 else []),
                                 need=None if m else "o")
                if j:
                    for m in (2 * j - 2, 2 * j - 1):
                        sum_emptied("bo", "b_out", m, sq[:, m, :])
            for m in (KD - 2, KD - 1):
                sum_emptied("bo", "b_out", m, sq[:, m, :])

            def token_squares(k):
                pe.wait_ge(sq_ready, SQ["m"] + k + 1)
                for b, (t0, n) in enumerate(TB):
                    last = nc.tensor.matmul(banks[6][0:n, 3 * NE + b:3 * NE + b + 1], sq[:, k, t0:t0 + n],
                                            ones[:, 0:1], start=False, stop=False)
                return last

            pe.wait_ge(gw_done, 1)
            zeros = cn("mask1")[:, 0:3 * NE + 3]
            nc.tensor.matmul(banks[6][:, 0:3 * NE + 3], ones, zeros, start=True, stop=False)
            for k in range(KD):
                pe.wait_ge(res_done, RES["bo"] + k + 1)
                for b, (t0, n) in enumerate(TB):
                    nc.tensor.matmul(banks[6][0:n, NE * b:NE * b + NE], hT[:, k, t0:t0 + n], gw[:, k, :],
                                     start=False, stop=False)
                for b, (t0, n) in enumerate(TB):
                    last = nc.tensor.transpose(banks[2 * b + k // 4][0:n, P * (k % 4):P * (k % 4) + P],
                                               hT[:, k, t0:t0 + n], ident)
                    if k % 4 == 3:
                        mark(last, ("h_tok", b, k // 4))
                if k:
                    token_squares(k - 1)
            token_squares(KD - 1)
            last = nc.tensor.matmul(banks[6][:, 0:3 * NE + 3], ones, zeros, start=False, stop=True)
            mark(last, "logits")
            pe.wait_ge(assigned, 1)
            a = rt[:, 0, :]
            nc.tensor.matmul(banks[7][:, 0:3 * NE], cn("tri"), a, start=True, stop=True)
            last = nc.tensor.matmul(banks[7][:, 3 * NE:6 * NE], ones, a, start=True, stop=True)
            mark(last, "positions")
            pe.wait_ge(h_tok_done, 6)

            def gather(half):
                for part, src in enumerate((h_thi, h_tlo)):
                    for b in range(3):
                        last = nc.tensor.matmul(banks[half][:, :], sel[:, b, :], src[:, b, NT * half:NT * half + NT],
                                                start=(part == 0 and b == 0), stop=(part == 1 and b == 2))
                return last

            def slot_norms():
                for b in range(3):
                    nc.tensor.matmul(banks[7][:, 1:2], sel[:, b, :].bitcast(F32), mrs[:, b:b + 1],
                                     start=(b == 0), stop=(b == 2))

            def turn_x(half):
                for f in range(4):
                    c = NT * half + P * f
                    last = nc.tensor.transpose(banks[2 + half][:, P * f:P * f + P], y_exp[:, c:c + P], ident)
                return last

            def scatter(bank, b, n):
                return nc.tensor.matmul(bank[:, :], selT[:, b, :], y_exp[:, NT * n:NT * n + NT], start=True, stop=True)

            pe.wait_ge(h_lo_done, 3)
            pe.wait_ge(sel_done, 1)
            slot_norms()
            for half in range(2):
                mark(gather(half), ("first_xs", half))
            for half in range(2):
                pe.wait_ge(xs_done, half + 1)
                last = turn_x(half)
            mark(last, "first_x")
            pe.wait_ge(rounds_ready, 1)
            rounds = pe.value_load(rounds_i[0:1, 0:1], min_val=1, max_val=3)
            base = step["loop"] = count[0]

            def expert(it):
                def emark(ins, *keys):
                    mark(ins, *(("e",) + key for key in keys))

                def echunk(c):
                    pe.wait_ge(lo_done, it * EC + (NC0 + c + 1))
                    s = (NC0 + c) % SPLIT
                    k = 4 if c < 4 * UT else 2
                    return [x[s][:].rearrange("p (k n) -> p k n", k=k) for x in (w_hi, w_lo)]

                pe.wait_ge(x_hi_done, it + 1)
                pe.wait_ge(x_lo_done, it + 1)

                def turn(j):
                    pe.wait_ge(eh_done, it * UT + (j + 1))
                    if j:
                        pe.wait_ge(eh_lo_done, it * UT + j)
                    for f in range(4):
                        last = nc.tensor.transpose(banks[6][:, P * f:P * f + P], e_h[:, j % 2, P * f:P * f + P], ident)
                    emark(last, ("turned", j))

                for j in range(UT):
                    if j >= 2:
                        pe.wait_ge(eh_done, it * UT + (j - 1))
                    for g in range(2):
                        ps = banks[2 * (j % 2) + g]
                        for kh in range(2):
                            c = 4 * j + 2 * g + kh
                            wc = echunk(c)
                            for k in range(4):
                                kk = 4 * kh + k
                                last = product(ps[:, :], (x_hi[:, kk, :], x_lo[:, kk, :]), [x[:, k, :] for x in wc],
                                               kk == 0, kk == KD - 1)
                            emark(last, ("chunk", c), *([("up", j)] if g and kh else []))
                            if c in SCATTER:
                                i = SCATTER.index(c)
                                if i == 0:
                                    pe.wait_ge(selT_done, it + 1)
                                    pe.wait_ge(y_done, it * 2 + 2)
                                if i >= 3:
                                    pe.wait_ge(added, it * 6 + (i - 1))
                                emark(scatter(banks[(7, 4, 5)[i % 3]], i % 3, i // 3), ("scattered", i))
                    if j:
                        turn(j - 1)
                for d in range(KE // 2):
                    wc = echunk(4 * UT + d)
                    if d == 0:
                        pe.wait_ge(added, it * 6 + 7)
                    if d == 1:
                        for b in range(3):
                            last = nc.tensor.matmul(banks[7][:, 0:1], sel[:, b, :].bitcast(F32), cur[:, 3 + b:4 + b],
                                                    start=(b == 0), stop=(b == 2))
                        emark(last, ("gate",))
                        for b in range(3):
                            last = nc.tensor.transpose(banks[2][:, P * b:P * b + P], sel[:, b, :].bitcast(F32), ident)
                        emark(last, ("selT",))
                    if d == 3:
                        turn(UT - 1)
                    if d == 5:
                        pe.wait_ge(sel_done, it + 2)
                        slot_norms()
                    if d in (5, 6):
                        emark(gather(d - 5), ("xs", d - 5))
                    if d in (8, 9):
                        pe.wait_ge(xs_done, it * 2 + (d - 8 + 3))
                        last = turn_x(d - 8)
                        if d == 9:
                            emark(last, ("x",))
                    pe.wait_ge(eh_lo_done, it * UT + ((2 * d + 1) // 4 + 1))
                    for n in range(2):
                        for f in range(2):
                            ff = 2 * d + f
                            last = product(banks[4 + n][:, :], (eh_hi[:, ff, :], eh_lo[:, ff, :]),
                                           [x[:, f, NT * n:NT * n + NT] for x in wc], ff == 0, ff == KE - 1)
                    emark(last, ("chunk", 4 * UT + d))

            with pe.Fori(0, rounds) as r:
                with pe.Fori(0, NE) as e:
                    expert(r * NE + e)
            step["per_expert"] = count[0] - base
            last_it = rounds * NE
            pe.wait_ge(selT_done, last_it + 1)
            pe.wait_ge(y_done, last_it * 2 + 2)
            pe.wait_ge(x_lo_done, last_it + 1)
            for i in range(6):
                mark(scatter(banks[(7, 6, 5, 4, 3, 2)[i]], i // 2, i % 2), ("last_scattered", i))

        def at(eng, *key):
            eng.wait_ge(pe_done, step[key if len(key) > 1 else key[0]])

        def at_tile(eng, name, j):
            at(eng, "tile", TN[(name, j)])
            return banks[TN[(name, j)] % BANKS]

        def at_expert(eng, it, *key):
            eng.wait_ge(pe_done, it * step["per_expert"] + step[("e",) + key])

        def at_last(eng, rounds, i):
            eng.wait_ge(pe_done, rounds * (NE * step["per_expert"]) + (step[("last_scattered", i)] - step["per_expert"]))

        def slot_free(eng, n):
            if n >= SPLIT:
                at(eng, "chunk", n - SPLIT)

        def slot_free_in_loop(eng, it, c):
            if c >= SPLIT:
                at_expert(eng, it, "chunk", c - SPLIT)
            else:
                eng.wait_ge(pe_done, it * step["per_expert"] + (step[("e", "chunk", EC + c - SPLIT)] - step["per_expert"]))

        @block.sync
        def _(sp):
            sp.dma_start(con[:], consts).then_inc(in_const, 16)
            for b, (t0, n) in enumerate(TB):
                sp.dma_start(x_in[0:n, b, :], x_tok[t0:t0 + n, :]).then_inc(in_x, 16)
            sp.dma_start(par[:], params).then_inc(in_par, 16)

            for n, (name, j, cols) in enumerate(PLAN):
                if n >= RAW:
                    sp.wait_ge(lo_done, n - RAW + 1)
                src = source(name, j)
                sp.dma_start(raw[n % RAW][:, 0:cols].rearrange("p (k n) -> p k n", k=src.shape[1]), src)\
                    .then_inc(landed[n % RAW], 16)

            def expert_loads(it, e, chunks=EC):
                up = w["m_w_gate_up"][0, bass.ds(e, 1)].rearrange("a (k p) n -> p (a k) n", p=P)
                dn = w["m_w_down"][0, bass.ds(e, 1)].rearrange("a (k p) n -> p (a k) n", p=P)
                for c in range(chunks):
                    slot = (NC0 + c) % RAW
                    sp.wait_ge(lo_done, it * EC + (NC0 + c - RAW + 1))
                    if c < 4 * UT:
                        j, g, kh = c // 4, c // 2 % 2, c % 2
                        src = up[:, 4 * kh:4 * kh + 4, EF * g + NT * j:EF * g + NT * j + NT]
                    else:
                        f = 2 * (c - 4 * UT)
                        src = dn[:, f:f + 2, :]
                    sp.dma_start(raw[slot][:].rearrange("p (k n) -> p k n", k=src.shape[1]), src)\
                        .then_inc(landed[slot], 16)

            with sp.Fori(0, NE) as e:
                expert_loads(e, e)
            sp.wait_ge(rounds_ready, 1)
            rounds = sp.value_load(rounds_i[0:1, 0:1], min_val=1, max_val=3)
            with sp.If(rounds > 1):
                with sp.Fori(1, rounds) as r:
                    with sp.Fori(0, NE) as e:
                        expert_loads(r * NE + e, e)
            expert_loads(rounds * NE, 0, 2)
            sp.wait_ge(fin_done, 1)
            sp.dma_start(out[0:P - META, :], y_acc[META:P, 0, :]).then_inc(out_written, 16)
            sp.wait_ge(fin_done, 2)
            sp.dma_start(out[P - META:2 * P - META, :], y_acc[:, 1, :]).then_inc(out_written, 16)
            sp.wait_ge(fin_done, 3)
            sp.dma_start(out[2 * P - META:SEQ, :], y_acc[0:META, 2, :]).then_inc(out_written, 16)
            sp.wait_ge(out_written, 48)

        @block.gpsimd
        def _(pool):
            pool.wait_ge(krope_done, 1)
            at(pool, "tile", TN[("cq", KQ - 1)])
            nc.gpsimd.tensor_copy(kT[NOPE:QK, :, :], rope_a[NOPE:QK, None, :].to_broadcast([ROPE, HEADS, T]))\
                .then_inc(krope_copied, 1)
            pool.wait_ge(res_done, RES["bo"] + 1)
            pool.dma_start(grow[:], gain_rows[0:1, 0:D].to_broadcast([P, D])).then_inc(in_rows, 16)
            pool.dma_start(rbias[:], gain_rows[0:1, D:D + NE].to_broadcast([P, NE])).then_inc(in_rows, 16)
            nc.gpsimd.memset(selT[:], 0.0).then_inc(selT_done, 1)
            nc.gpsimd.memset(y_exp[:], 0.0).then_inc(y_done, 2)
            pool.wait_ge(res_done, RES["bo"] + KD)
            nc.gpsimd.memset(y_acc[:], 0.0).then_inc(added, 1)
            nc.gpsimd.memset(h_tlo[:, 2, :].bitcast(F32), 0.0)
            at(pool, "logits")
            nc.gpsimd.memset(h_thi[:, 2, :].bitcast(F32), 0.0).then_inc(pads_zeroed, 1)
            for b, (t0, n) in enumerate(TB):
                pool.wait_ge(h_hi_done, b + 1)
                nc.gpsimd.tensor_tensor(h_tlo[0:n, b, :], h_tok[0:n, b, :], h_thi[0:n, b, :].bitcast(F32),
                                        ALU.subtract).then_inc(h_lo_done, 1)

        @block.scalar
        def _(act):
            issued = [0]

            def ahead(n):
                while issued[0] <= min(n, NC0 - 1):
                    c = issued[0]
                    name, j, cols = PLAN[c]
                    act.wait_ge(landed[c % RAW], 16 * (c // RAW + 1))
                    slot_free(act, c)
                    src, dst = raw[c % RAW][:, 0:cols], w_hi[c % SPLIT]
                    dst = dst[:, 0:cols] if name not in ("dkr", "uq") else dst[:, :]
                    for d, s in pieces(name, source(name, j).shape[1], src, dst):
                        last = nc.scalar.copy(d, s)
                    last.then_inc(hi_done, 1)
                    issued[0] += 1

            def empty(name, j, dst, func=ACT.Copy, rows=None, **kw):
                ps = at_tile(act, name, j)
                nc.scalar.activation(dst, ps[rows or slice(0, P), 0:dst.shape[-1]], func, **kw)\
                    .then_inc(emptied["A"], 1)

            def empty_squared(name, m, dst, square):
                ps = at_tile(act, name, m)
                nc.scalar.activation(dst, ps[:, 0:T], ACT.Copy)
                nc.scalar.activation(square, ps[:, 0:T], ACT.Square).then_inc(emptied["A"], 1)

            def squares(after, n):
                for k in range(KD):
                    act.wait_ge(after, n + k + 1)
                    nc.scalar.activation(sq[:, k, :], hT[:, k, :], ACT.Square).then_inc(sq_ready, 1)

            def root(name):
                i, kn = NORM[name], NORMS[NORM[name]][1]
                at(act, "sum", name)
                nc.scalar.activation(rstd[:, i % 2, :], banks[6 + i % 2][:, 0:T], ACT.Sqrt, bias=eps,
                                     scale=1.0 / (kn * P)).then_inc(root_taken, 1)

            def rounded(name, dst, src, kn):
                for k in range(kn):
                    act.wait_ge(norm_f32, NORMED[name] + k + 1)
                    nc.scalar.copy(dst[:, k, 0:T], src[:, k, :]).then_inc(act_hi, 1)

            primed = [0]

            def prime(func):
                c = 230 + primed[0]
                nc.scalar.activation(small[0:1, c:c + 1], eps[0:1, :], func)
                primed[0] += 1

            ahead(1)
            squares(emptied["V"], 0)
            ahead(2)
            act.wait_ge(in_par, 16)
            root("a")
            rounded("a", u_hi, sq, KD)
            act.wait_ge(lam_abs, 1)
            nc.scalar.activation(lt[2], lt[1], ACT.Exp, scale=-1.0).then_inc(lam_exp, 1)
            for j in range(RB // 2):
                ahead(CH[("xr", j)] + 2)
                for m in (2 * j, 2 * j + 1):
                    empty("xr", m, xr_gy[:, m, CONV - 1:])
                for m in range(2 * j - 2, 2 * j) if j else ():
                    act.wait_ge(conv_done, m + 1)
                    nc.scalar.copy(xc_hi[:, m, :], xc[:, m, :]).then_inc(xc_hi_done, 1)
            ahead(CH[("gx", 0)])
            for m in (RB - 2, RB - 1):
                act.wait_ge(conv_done, m + 1)
                nc.scalar.copy(xc_hi[:, m, :], xc[:, m, :]).then_inc(xc_hi_done, 1)
            prime(ACT.Sigmoid)

            def take_y(j):
                for m in (2 * j, 2 * j + 1):
                    empty("y", m, xr_gy[:, m, 0:T])

            take_y(0)
            ahead(CH[("y", 1)])
            for m in range(RB):
                empty("r", m, r_la[:, m, :], ACT.Sigmoid, bias=pr("ga_b", m))
                empty("i", m, ig[:, m, :], ACT.Sigmoid, bias=pr("gx_b", m))

            for half in range(2):
                act.wait_ge(loga_ready, half + 1)
                if half:
                    act.wait_ge(scan_done, 1)
                a = r_la[:, half * HB:half * HB + HB, :]
                nc.scalar.activation(th, a, ACT.Tanh)
                nc.scalar.activation(a, a, ACT.Exp).then_inc(a_ready, 1)
                ahead(CH[("y", half + 2)])
                take_y(half + 1)
                act.wait_ge(root_in, half + 1)
                nc.scalar.activation(th, th, ACT.Sqrt, scale=-1.0).then_inc(root_done, 1)
            ahead(CH[("y", 4)])
            take_y(3)
            for m0, m1 in GELUS:
                if m0 == 8:
                    ahead(CH[("a_out", 1)])
                    take_y(4)
                y = xr_gy[:, m0:m1, 0:T]
                act.wait_ge(emptied["A"], EMPTIED[TN[("y", m1 - 1)]])
                nc.scalar.activation(y, y, ACT.Gelu_apprx_tanh).then_inc(gelu_done, 1)
            for m in range(RB):
                act.wait_ge(z_f32, m + 1)
                nc.scalar.copy(xc_hi[:, m, :], xc[:, m, :]).then_inc(z_hi, 1)
            prime(ACT.Sqrt)
            for m in range(KD):
                ahead(CH[("a_out", m)] + 2)
                empty_squared("a_out", m, mix[:, m, :], sq[:, m, :])
            root("ao")
            squares(res_done, RES["ao"])
            root("f")
            rounded("f", u_hi, sq, KD)
            prime(ACT.Silu)

            def f_round(m):
                act.wait_ge(emptied["V"], EMPTIED[TN[("f_u", m)]])
                nc.scalar.copy(hid_hi[:, m, :], f_h[:, m % 4, :]).then_inc(fhi_done, 1)

            for j in range(KF // 2):
                ahead(CH[("f_gate", j)] + 2)
                for m in (2 * j, 2 * j + 1):
                    if m >= 2:
                        act.wait_ge(emptied["V"], EMPTIED[TN[("f_u", m - 2)]])
                    empty("f_g", m, f_silu[:, m % 2, :], ACT.Silu)
                ahead(CH[("f_up", j)] + 2)
                if j:
                    f_round(2 * j - 2)
                    f_round(2 * j - 1)
            f_round(KF - 2)
            f_round(KF - 1)
            prime(ACT.Sqrt)
            for q in range(KD // 2):
                for r in range(3):
                    ahead(CH[("f_down", 3 * q + r)] + 2)
                for m in (2 * q, 2 * q + 1):
                    empty_squared("f_down", m, mix[:, m, :], sq[:, m, :])
            root("fo")
            squares(res_done, RES["fo"])
            root("b")
            rounded("kv", u_hi, sq, KD)
            rounded("b", ub_hi, mix, KD)
            ahead(CH[("dkv", 0)] + 2)
            for m in range(KL):
                empty_squared("ckv", m, ckv[:, m, :], sq[:, m, :])
            ahead(CH[("dkr", 0)] + 2)
            for m in range(KQ):
                ahead(CH[("dq", m // 2)] + 2)
                empty_squared("cq", m, cq[:, m, :], sq[:, KL + m, :])
                if m == 0:
                    root("ckv")
            root("cq")
            prime(ACT.Exp)
            rounded("ckv", ckv_hi, ckv, KL)
            rounded("cq", cq_hi, cq, KQ)
            for half in range(2):
                ahead(CH[("ukv", half)] + 2)
                for m in range(4 * half, 4 * half + 4):
                    ps = at_tile(act, "kn", m)
                    nc.scalar.copy(kT[0:NOPE, 2 * m, :], ps[0:NOPE, 0:T])
                    nc.scalar.copy(kT[0:NOPE, 2 * m + 1, :], ps[NOPE:P, 0:T]).then_inc(emptied["A"], 1)
                for b, (t0, n) in enumerate(TB):
                    empty("v", (b, half), v_tok[0:n, b, 512 * half:512 * half + 512], rows=slice(0, n))
            def take_queries(g):
                ahead(CH[("uq", g)])
                for m in (2 * g, 2 * g + 1):
                    ps = at_tile(act, "qn", m)
                    i = 2 * (m % 2)
                    nc.scalar.copy(qT[g % 2][0:NOPE, i, :], ps[0:NOPE, 0:T])
                    nc.scalar.copy(qT[g % 2][0:NOPE, i + 1, :], ps[NOPE:P, 0:T]).then_inc(emptied["A"], 1)

            take_queries(0)
            ahead(CH[("uq", 1)])
            for h in range(HEADS + LAG + 2):
                if h < HEADS:
                    act.wait_ge(max_done, h + 1)
                    for b, (t0, n) in enumerate(TB):
                        c, kn = SC[b]
                        i = 3 * (h % 3) + b
                        last = nc.scalar.activation(s_sb[0:n, h % 3, c:c + kn], s_sb[0:n, h % 3, c:c + kn], ACT.Exp,
                                                    bias=nbias[0:n, i:i + 1], scale=QK ** -0.5,
                                                    accum_out=rsum[0:n, i:i + 1])
                    last.then_inc(exp_done, 1)
                if h % 4 == 1 and h // 4 < 3:
                    take_queries(h // 4 + 1)
                if h % 4 == 3:
                    ahead(CH[("uq", 0)] + h // 4 + 2)
                if LAG <= h < HEADS + LAG:
                    t = h - LAG
                    ps = at_tile(act, "pt", t)
                    if t >= 2:
                        at(act, "tile", TN[("o", t - 2)])
                    nc.scalar.copy(pT[:, t % 2, 0:416], ps[:, 0:416])
                    nc.scalar.copy(pT[0:META, t % 2, 416:432], ps[0:META, 416:432]).then_inc(emptied["A"], 1)
                if LAG < h < HEADS + LAG + 1:
                    t = h - LAG - 1
                    r = VD * (t % 2)
                    empty("o", t, sq[r:r + VD, t // 2, :], rows=slice(0, VD))
                if h >= LAG + 3 and h % 2:
                    k = (h - LAG - 3) // 2
                    act.wait_ge(emptied["A"], EMPTIED[TN[("o", 2 * k + 1)]])
                    nc.scalar.copy(u_hi[:, k, :], sq[:, k, :]).then_inc(act_hi, 1)
            prime(ACT.Sqrt)
            for j in range(4):
                ahead(CH[("b_out", j)] + 2)
                for m in (2 * j, 2 * j + 1):
                    empty_squared("b_out", m, mix[:, m, :], sq[:, m, :])

            def split(it, c, free):
                slot = (NC0 + c) % RAW
                act.wait_ge(landed[slot], it * (16 * EC // RAW) + 16 * ((NC0 + c) // RAW + 1))
                free()
                nc.scalar.copy(w_hi[(NC0 + c) % SPLIT][:], raw[slot][:]).then_inc(hi_done, 1)

            root("bo")
            squares(res_done, RES["bo"])
            at(act, "logits")
            nc.scalar.activation(mrs, banks[6][:, 3 * NE:3 * NE + 3], ACT.Sqrt, bias=eps, scale=1.0 / D)\
                .then_inc(rstd_t, 1)
            act.wait_ge(h_tok_done, 6)
            act.wait_ge(pads_zeroed, 1)
            for b, (t0, n) in enumerate(TB):
                nc.scalar.copy(h_thi[0:n, b, :], h_tok[0:n, b, :]).then_inc(h_hi_done, 1)
            prime(ACT.Exp)
            act.wait_ge(logit_in, 1)
            nc.scalar.activation(rt[:, 2, :], rt[:, 2, :], ACT.Exp).then_inc(logit_exp, 1)
            for c in range(2):
                split(0, c, lambda: slot_free(act, NC0 + c))

            def take_slots(half):
                nc.scalar.copy(y_exp[:, NT * half:NT * half + NT], banks[half][:, :]).then_inc(xs_done, 1)

            def take_x():
                for k in range(KD):
                    last = nc.scalar.activation(x_hi[:, k, :], banks[2 + k // 4][:, P * (k % 4):P * (k % 4) + P], ACT.Copy,
                                                scale=pr("m_pre", k))
                last.then_inc(x_hi_done, 1)

            prime(ACT.Silu)
            act.wait_ge(y_done, 2)
            for half in range(2):
                at(act, "first_xs", half)
                take_slots(half)
            at(act, "first_x")
            take_x()
            act.wait_ge(rounds_ready, 1)
            rounds = act.value_load(rounds_i[0:1, 0:1], min_val=1, max_val=3)

            def expert(it):
                for c in range(EC):
                    split(it, c + 2, lambda: slot_free_in_loop(act, it, c + 2))
                    if c % 4 == 0 and 1 <= c // 4 <= UT:
                        j = c // 4 - 1
                        at_expert(act, it, "up", j)
                        if j:
                            act.wait_ge(eh_done, it * UT + j)
                        nc.scalar.activation(e_silu[:], banks[2 * (j % 2)][:, :], ACT.Silu,
                                             scale=cur[:, 7:8]).then_inc(silu_done, 1)
                    if c % 4 == 0 and 2 <= c // 4 <= UT + 1:
                        j = c // 4 - 2
                        at_expert(act, it, "turned", j)
                        nc.scalar.copy(eh_hi[:, 4 * j:4 * j + 4, :],
                                       banks[6][:, :].rearrange("p (f n) -> p f n", f=4)).then_inc(eh_hi_done, 1)
                    if c == 4 * UT + 2:
                        at_expert(act, it, "selT")
                        nc.scalar.copy(selT[:], banks[2][:, 0:3 * P].rearrange("p (b n) -> p b n", b=3))\
                            .then_inc(selT_done, 1)
                    if c in (4 * UT + 6, 4 * UT + 7):
                        half = c - (4 * UT + 6)
                        at_expert(act, it, "xs", half)
                        take_slots(half)
                    if c == 4 * UT + 10:
                        at_expert(act, it, "x")
                        take_x()
                at_expert(act, it, "chunk", EC - 1)
                act.wait_ge(gate_done, it + 1)
                for n in range(2):
                    nc.scalar.activation(y_exp[:, NT * n:NT * n + NT], banks[4 + n][:, :], ACT.Copy,
                                         scale=cur[:, 6:7]).then_inc(y_done, 1)

            with act.Fori(0, rounds) as r:
                with act.Fori(0, NE) as e:
                    expert(r * NE + e)

            for b, (t0, n) in enumerate(TB):
                for half in range(2):
                    i = 2 * b + half
                    act.wait_ge(added, rounds * (NE * 6) + (i + 2))
                    nc.scalar.activation(e_h[0:n, half, :], y_acc[0:n, b, 512 * half:512 * half + 512],
                                         ACT.Square, accum_out=small[0:n, 220 + i:221 + i]).then_inc(fin_sum, 1)
                    act.wait_ge(fin_sum, i + 1)
            prime(ACT.Sqrt)
            act.wait_ge(fin_std, 1)
            nc.scalar.activation(mrs, mss, ACT.Sqrt, bias=eps, scale=1.0 / D).then_inc(fin_std, 1)

        @block.vector
        def _(dve):
            issued = [0]
            steps = [0]

            def link(ins):
                ins.then_inc(dve_step, 1)
                steps[0] += 1
                dve.wait_ge(dve_step, steps[0])

            def ahead(n):
                while issued[0] <= min(n, NC0 - 1):
                    c = issued[0]
                    name, j, cols = PLAN[c]
                    dve.wait_ge(hi_done, c + 1)
                    k = source(name, j).shape[1]
                    full = name in ("dkr", "uq")
                    src, hi, lo = raw[c % RAW][:, 0:cols], w_hi[c % SPLIT][:], w_lo[c % SPLIT][:]
                    if not full:
                        hi, lo = hi[:, 0:cols], lo[:, 0:cols]
                    for (d, s), (h, _) in zip(pieces(name, k, src, lo), pieces(name, k, src, hi.bitcast(F32))):
                        last = nc.vector.tensor_tensor(d, s, h, ALU.subtract)
                    last.then_inc(lo_done, 1)
                    issued[0] += 1

            def reciprocal_of_root(name):
                i = NORM[name]
                dve.wait_ge(root_taken, i + 1)
                link(nc.vector.reciprocal(rstd[:, i % 2, :], rstd[:, i % 2, :]))
                return rstd[:, i % 2, :]

            def scaled(dst, src, gain, k, r):
                return nc.vector.scalar_tensor_tensor(out=dst[:, k, :], in0=src[:, k, :], scalar=pr(gain, k),
                                                      in1=r, op0=ALU.mult, op1=ALU.mult)

            def normalise(parts, r):
                blocks = [(p, k) for p in parts for k in range(p[6])]
                for i in range(len(blocks) + 2):
                    if i < len(blocks):
                        (name, lo, hi, dst, src, gain, _), k = blocks[i]
                        scaled(dst, src, gain, k, r).then_inc(norm_f32, 1)
                    if i >= 2:
                        (name, lo, hi, dst, src, gain, _), k = blocks[i - 2]
                        dve.wait_ge(act_hi, PART[name] + k + 1)
                        nc.vector.tensor_tensor(lo[:, k, 0:T], dst[:, k, :], hi[:, k, 0:T].bitcast(F32),
                                                ALU.subtract).then_inc(act_lo, 1)

            def residual(name, gain):
                r = reciprocal_of_root(name)
                for k in range(KD + 1):
                    if k < KD:
                        scaled(mix, mix, gain, k, r).then_inc(res_scaled, 1)
                    if k:
                        dve.wait_ge(res_scaled, RES[name] + k)
                        nc.vector.tensor_tensor(hT[:, k - 1, :], hT[:, k - 1, :], mix[:, k - 1, :], ALU.add)\
                            .then_inc(res_done, 1)
                dve.wait_ge(res_done, RES[name] + KD)

            link(nc.vector.memset(small[:], 0.0))
            link(nc.vector.memset(rsum, 1.0))
            for c in range(KD):
                ps = at_tile(dve, "hT", c)
                nc.vector.tensor_copy(hT[:, c, :], ps[:, 0:T]).then_inc(emptied["V"], 1)
            link(nc.vector.memset(xr_gy[:, :, 0:CONV - 1], 0.0))
            ahead(1)
            dve.wait_ge(in_par, 16)
            link(nc.vector.tensor_scalar(lt[0], pr("lam"), -1.0, None, ALU.mult))
            nc.vector.tensor_tensor(lt[1], pr("lam"), lt[0], ALU.max).then_inc(lam_abs, 1)
            normalise([("a", u_lo, u_hi, sq, hT, "a_pre", KD)], reciprocal_of_root("a"))
            ahead(2)

            def softplus():
                dve.wait_ge(lam_exp, 1)
                link(nc.vector.tensor_scalar(lt[3], lt[2], 2.0, None, ALU.add))
                link(nc.vector.reciprocal(lt[3], lt[3]))
                link(nc.vector.tensor_tensor(lt[3], lt[2], lt[3], ALU.mult))
                link(nc.vector.tensor_tensor(lt[4], lt[3], lt[3], ALU.mult))
                link(nc.vector.tensor_scalar(lt[5], lt[4], 1.0 / 19, None, ALU.mult))
                for d in (17, 15, 13, 11, 9, 7, 5, 3):
                    link(nc.vector.scalar_tensor_tensor(out=lt[5], in0=lt[5], scalar=1.0 / d, in1=lt[4],
                                                        op0=ALU.add, op1=ALU.mult))
                link(nc.vector.scalar_tensor_tensor(out=lt[5], in0=lt[5], scalar=1.0, in1=lt[3],
                                                    op0=ALU.add, op1=ALU.mult))
                link(nc.vector.tensor_scalar(lt[0], lt[0], 0.0, None, ALU.max))
                link(nc.vector.scalar_tensor_tensor(out=c8, in0=lt[5], scalar=2.0, in1=lt[0],
                                                    op0=ALU.mult, op1=ALU.add))
                link(nc.vector.tensor_scalar(c8, c8, -8.0, None, ALU.mult))

            def conv(m):
                dve.wait_ge(emptied["A"], EMPTIED[TN[("xr", m)]])
                link(nc.vector.tensor_scalar(xc[:, m, :], xr_gy[:, m, 0:T], pr("conv_w", m), pr("conv_b", m),
                                             ALU.mult, ALU.add))
                for k in range(1, CONV):
                    ins = nc.vector.scalar_tensor_tensor(out=xc[:, m, :], in0=xr_gy[:, m, k:k + T],
                                                         scalar=pr("conv_w", RB * k + m), in1=xc[:, m, :],
                                                         op0=ALU.mult, op1=ALU.add)
                    if k < CONV - 1:
                        link(ins)
                ins.then_inc(conv_done, 1)

            def conv_low(m):
                dve.wait_ge(xc_hi_done, m + 1)
                nc.vector.tensor_tensor(xc_lo[:, m, :], xc[:, m, :], xc_hi[:, m, :].bitcast(F32), ALU.subtract)\
                    .then_inc(xc_lo_done, 1)

            for j in range(RB // 2):
                ahead(CH[("xr", j)] + 2)
                conv(2 * j)
                conv(2 * j + 1)
                if j:
                    conv_low(2 * j - 2)
                    conv_low(2 * j - 1)
            ahead(CH[("gx", 0)])
            conv_low(RB - 2)
            conv_low(RB - 1)
            softplus()
            ahead(CH[("y", 1)])
            for half in range(2):
                hs = slice(half * HB, half * HB + HB)
                dve.wait_ge(emptied["A"], EMPTIED[TN[("i", half * HB + HB - 1)]])
                nc.vector.tensor_tensor(r_la[:, hs, :], r_la[:, hs, :], c8[:, hs, None].to_broadcast([P, HB, T]),
                                        ALU.mult).then_inc(loga_ready, 1)
                nc.vector.tensor_tensor(ig[:, hs, :], ig[:, hs, :], xc[:, hs, :], ALU.mult).then_inc(gated, 1)
            for half in range(2):
                hs = slice(half * HB, half * HB + HB)
                if half == 0:
                    dve.wait_ge(gated, 2)
                dve.wait_ge(a_ready, half + 1)
                link(nc.vector.tensor_tensor(xc[:, hs, :], r_la[:, hs, :], r_la[:, hs, :], ALU.mult))
                nc.vector.scalar_tensor_tensor(out=th, in0=xc[:, hs, :], scalar=1.0, in1=th, op0=ALU.add,
                                               op1=ALU.mult).then_inc(root_in, 1)
                ahead(CH[("y", half + 2)])
                dve.wait_ge(root_done, half + 1)
                link(nc.vector.tensor_tensor(ig[:, hs, :], ig[:, hs, :], th, ALU.mult))
                for i in range(half * HB, half * HB + HB):
                    last = nc.vector.tensor_tensor_scan(xc[:, i, :], r_la[:, i, :], ig[:, i, :], 0.0,
                                                        ALU.mult, ALU.add)
                last.then_inc(scan_done, 1)
            ahead(CH[("y", 4)])
            dve.wait_ge(scan_done, 2)
            for g, (m0, m1) in enumerate(GELUS):
                dve.wait_ge(gelu_done, g + 1)
                for m in range(m0, m1):
                    nc.vector.tensor_tensor(xc[:, m, :], xc[:, m, :], xr_gy[:, m, 0:T], ALU.mult).then_inc(z_f32, 1)
                if m0 == 0:
                    ahead(CH[("a_out", 1)])
            for m in range(RB):
                dve.wait_ge(z_hi, m + 1)
                nc.vector.tensor_tensor(xc_lo[:, m, :], xc[:, m, :], xc_hi[:, m, :].bitcast(F32), ALU.subtract)\
                    .then_inc(z_lo, 1)
            for m in range(KD):
                ahead(CH[("a_out", m)] + 2)
            residual("ao", "a_post")
            normalise([("f", u_lo, u_hi, sq, hT, "f_pre", KD)], reciprocal_of_root("f"))

            def f_low(m):
                dve.wait_ge(fhi_done, m + 1)
                nc.vector.tensor_tensor(hid_lo[:, m, :], f_h[:, m % 4, :], hid_hi[:, m, :].bitcast(F32), ALU.subtract)\
                    .then_inc(flo_done, 1)

            for j in range(KF // 2):
                ahead(CH[("f_gate", j)] + 2)
                ahead(CH[("f_up", j)] + 2)
                for m in (2 * j, 2 * j + 1):
                    ps = at_tile(dve, "f_u", m)
                    dve.wait_ge(emptied["A"], EMPTIED[TN[("f_g", m)]])
                    if m >= 4:
                        dve.wait_ge(flo_done, m - 3)
                    nc.vector.tensor_tensor(f_h[:, m % 4, :], ps[:, 0:T], f_silu[:, m % 2, :], ALU.mult)\
                        .then_inc(emptied["V"], 1)
                if j:
                    f_low(2 * j - 2)
                    f_low(2 * j - 1)
            f_low(KF - 2)
            f_low(KF - 1)
            for q in range(KD // 2):
                for r in range(3):
                    ahead(CH[("f_down", 3 * q + r)] + 2)
            residual("fo", "f_post")
            normalise([("kv", u_lo, u_hi, sq, hT, "kv_norm", KD), ("b", ub_lo, ub_hi, mix, hT, "b_pre", KD)],
                      reciprocal_of_root("b"))
            nc.vector.memset(ckv_hi[:, :, T:].bitcast(F32), 0.0)
            nc.vector.memset(ckv_lo[:, :, T:].bitcast(F32), 0.0)
            ahead(CH[("dkv", 0)] + 2)
            ahead(CH[("dkr", 0)] + 2)
            ps = at_tile(dve, "krope", 0)
            nc.vector.tensor_tensor(rope_a[NOPE:QK, :], ps[NOPE:QK, 0:T], cn("cos")[NOPE:QK, :], ALU.mult)
            ins = nc.vector.tensor_tensor(k_temp[NOPE:QK, :], ps[0:ROPE, 0:T], cn("sin")[0:ROPE, :], ALU.mult)
            ins.then_inc(emptied["V"], 1)
            dve.wait_ge(emptied["V"], EMPTIED[TN[("krope", 0)]])
            nc.vector.tensor_tensor(rope_a[NOPE:QK, :], rope_a[NOPE:QK, :], k_temp[NOPE:QK, :], ALU.add)\
                .then_inc(krope_done, 1)
            ahead(CH[("dq", 1)] + 2)
            normalise([("ckv", ckv_lo, ckv_hi, ckv, ckv, "latent", KL)], reciprocal_of_root("ckv"))
            normalise([("cq", cq_lo, cq_hi, cq, cq, "q_norm", KQ)], reciprocal_of_root("cq"))
            ahead(CH[("ukv", 0)] + 2)
            ahead(CH[("ukv", 1)] + 2)
            nc.vector.tensor_tensor(gw[:], pr("router_w").rearrange("p (k e) -> p k e", k=KD),
                                    pr("m_pre")[:, :, None].to_broadcast([P, KD, NE]), ALU.mult)
            nc.vector.memset(banks[6][:, 0:3 * NE + 3], 0.0).then_inc(gw_done, 1)
            nc.vector.memset(cur[:], 0.0)
            dve.wait_ge(krope_copied, 1)
            def rotate_queries(g):
                ahead(CH[("uq", g)])
                ps = at_tile(dve, "qro", g)
                nc.vector.tensor_tensor(rope_a[:, :], ps[:, 0:T], cn("cos"), ALU.mult).then_inc(emptied["V"], 1)
                ps = at_tile(dve, "qsw", g)
                nc.vector.tensor_tensor(rope_b[:, :], ps[:, 0:T], cn("sin"), ALU.mult).then_inc(emptied["V"], 1)
                dve.wait_ge(emptied["V"], EMPTIED[TN[("qsw", g)]])
                link(nc.vector.tensor_tensor(rope_a[:, :], rope_a[:, :], rope_b[:, :], ALU.add))
                for i in range(4):
                    last = nc.vector.tensor_copy(qT[g % 2][NOPE:QK, i, :], rope_a[ROPE * i:ROPE * i + ROPE, :])
                last.then_inc(qrope_done, 1)

            rotate_queries(0)
            ahead(CH[("uq", 1)])
            for h in range(HEADS + LAG + 3):
                if h < HEADS:
                    if h >= 3:
                        at(dve, "tile", TN[("pt", h - 3)])
                    i = 3 * (h % 3)
                    for b, (t0, n) in enumerate(TB):
                        c, kn = SC[b]
                        ps = at_tile(dve, "s", (h, b))
                        nc.vector.tensor_tensor_reduce(s_sb[0:n, h % 3, c:c + kn], ps[0:n, 0:kn],
                                                       cn(f"mask{b}")[0:n, :], 1.0, -3.0e38, ALU.add, ALU.max,
                                                       smax[0:n, i + b:i + b + 1]).then_inc(emptied["V"], 1)
                    dve.wait_ge(emptied["V"], EMPTIED[TN[("s", (h, 2))]])
                    nc.vector.tensor_scalar(nbias[:, i:i + 3], smax[:, i:i + 3], -(QK ** -0.5), None, ALU.mult)\
                        .then_inc(max_done, 1)
                if h % 4 == 1 and h // 4 < 3:
                    rotate_queries(h // 4 + 1)
                if 1 <= h < HEADS + 1:
                    t = h - 1
                    i = 3 * (t % 3)
                    dve.wait_ge(exp_done, t + 1)
                    link(nc.vector.reciprocal(rcp[:, i:i + 3], rsum[:, i:i + 3]))
                    for b, (t0, n) in enumerate(TB):
                        c, kn = SC[b]
                        last = nc.vector.tensor_scalar(s_sb[0:n, t % 3, c:c + kn], s_sb[0:n, t % 3, c:c + kn],
                                                       rcp[0:n, i + b:i + b + 1], None, ALU.mult)
                    last.then_inc(prob_done, 1)
                if h % 4 == 3:
                    ahead(CH[("uq", 0)] + h // 4 + 2)
                if h >= LAG + 4 and h % 2 == 0:
                    k = (h - LAG - 4) // 2
                    dve.wait_ge(act_hi, PART["o"] + k + 1)
                    nc.vector.tensor_tensor(u_lo[:, k, :], sq[:, k, :], u_hi[:, k, :].bitcast(F32), ALU.subtract)\
                        .then_inc(act_lo, 1)
            for j in range(4):
                ahead(CH[("b_out", j)] + 2)
            residual("bo", "b_post")

            def split(it, c):
                dve.wait_ge(hi_done, it * EC + (NC0 + c + 1))
                s = (NC0 + c) % SPLIT
                nc.vector.tensor_tensor(w_lo[s][:], raw[(NC0 + c) % RAW][:], w_hi[s][:].bitcast(F32), ALU.subtract)\
                    .then_inc(lo_done, 1)

            a_, g_, lg, p_, o1, o2, pos, t_ = (rt[:, k, :] for k in range(8))
            cols = rt[:, 9, :]
            m1, i1, m2, i2, s_, t3, c_ = (cols[:, 3 * k:3 * k + 3] for k in range(7))

            def v3(x):
                return x.rearrange("p (b e) -> p b e", b=3)

            def wide(x):
                return x[:, :, None].to_broadcast([P, 3, NE])

            for half in range(2):
                for b, (t0, n) in enumerate(TB):
                    at(dve, "h_tok", b, half)
                    nc.vector.tensor_copy(h_tok[0:n, b, 512 * half:512 * half + 512], banks[2 * b + half][0:n, :])\
                        .then_inc(h_tok_done, 1)
            dve.wait_ge(rstd_t, 1)
            nc.vector.reciprocal(mrs, mrs).then_inc(mrs_done, 1)
            dve.wait_ge(mrs_done, 1)
            at(dve, "logits")
            link(nc.vector.tensor_tensor(v3(lg), v3(banks[6][:, 0:3 * NE]), wide(mrs), ALU.mult))
            dve.wait_ge(in_rows, 32)
            link(nc.vector.tensor_tensor(v3(lg), v3(lg), rbias[:, None, :].to_broadcast([P, 3, NE]), ALU.add))
            link(nc.vector.tensor_reduce(m1, v3(lg), AX_X, ALU.max))
            nc.vector.tensor_tensor(v3(lg), v3(lg), wide(m1), ALU.subtract).then_inc(logit_in, 1)
            dve.wait_ge(logit_exp, 1)
            link(nc.vector.tensor_reduce(s_, v3(lg), AX_X, ALU.add))
            link(nc.vector.reciprocal(s_, s_))
            link(nc.vector.tensor_tensor(v3(p_), v3(lg), wide(s_), ALU.mult))
            for m_, i_, o_ in ((m1, i1, o1), (m2, i2, o2)):
                link(nc.vector.tensor_reduce(m_, v3(p_), AX_X, ALU.max))
                link(nc.vector.tensor_tensor(v3(t_), v3(p_), wide(m_), ALU.is_equal))
                link(nc.vector.scalar_tensor_tensor(out=t_, in0=t_, scalar=-float(NE), in1=cn("expert"),
                                                    op0=ALU.mult, op1=ALU.add))
                link(nc.vector.tensor_reduce(i_, v3(t_), AX_X, ALU.min))
                link(nc.vector.tensor_scalar(i_, i_, float(NE), None, ALU.add))
                link(nc.vector.tensor_tensor(v3(o_), v3(cn("expert")), wide(i_), ALU.is_equal))
                link(nc.vector.scalar_tensor_tensor(out=p_, in0=o_, scalar=-2.0, in1=p_, op0=ALU.mult, op1=ALU.add))
            link(nc.vector.tensor_tensor(t_, o1, o2, ALU.add))
            nc.vector.tensor_tensor(v3(a_), v3(t_), wide(cn("valid")), ALU.mult).then_inc(assigned, 1)
            link(nc.vector.tensor_tensor(s_, m1, m2, ALU.add))
            link(nc.vector.reciprocal(s_, s_))
            nc.vector.tensor_tensor(m1, m1, s_, ALU.mult)
            link(nc.vector.tensor_tensor(m2, m2, s_, ALU.mult))
            nc.vector.tensor_tensor(v3(o1), v3(o1), wide(m1), ALU.mult)
            link(nc.vector.tensor_tensor(v3(o2), v3(o2), wide(m2), ALU.mult))
            link(nc.vector.tensor_tensor(g_, o1, o2, ALU.add))
            at(dve, "positions")
            inside, total = v3(banks[7][:, 0:3 * NE]), v3(banks[7][:, 3 * NE:6 * NE])
            nc.vector.memset(v3(t_)[:, 0, :], 0.0)
            link(nc.vector.tensor_copy(v3(t_)[:, 1, :], total[:, 0, :]))
            link(nc.vector.tensor_tensor(v3(t_)[:, 2, :], total[:, 1, :], v3(t_)[:, 1, :], ALU.add))
            nc.vector.tensor_tensor(o1[:, 0:NE], total[:, 2, :], v3(t_)[:, 2, :], ALU.add)
            link(nc.vector.tensor_tensor(v3(pos), inside, v3(t_), ALU.add))
            nc.vector.tensor_reduce(c_[:, 0:1], o1[:, 0:NE], AX_X, ALU.max)
            link(nc.vector.scalar_tensor_tensor(out=pos, in0=pos, scalar=1.0, in1=a_, op0=ALU.add, op1=ALU.mult))
            link(nc.vector.tensor_scalar(pos, pos, -1.0, None, ALU.add))

            def choose(e, linked):
                for b in range(3):
                    nc.vector.tensor_scalar(cur[:, b:b + 1], v3(pos)[:, b, bass.ds(e, 1)], 0.0, None, ALU.add)
                for b in range(3):
                    ins = nc.vector.tensor_scalar(cur[:, 3 + b:4 + b], v3(g_)[:, b, bass.ds(e, 1)], 0.0, None, ALU.add)
                linked(ins)
                for b in range(3):
                    ins = nc.vector.tensor_scalar(sel[:, b, :], cn("iota"), cur[:, b:b + 1], None, ALU.is_equal)
                ins.then_inc(sel_done, 1)
                for b in range(3):
                    ins = nc.vector.tensor_scalar(v3(pos)[:, b, bass.ds(e, 1)], cur[:, b:b + 1], -float(P), None,
                                                  ALU.add)
                linked(ins)

            choose(0, link)
            split(0, 0)
            split(0, 1)
            nc.vector.tensor_scalar(c_[:, 1:2], c_[:, 0:1], float(P), 1.0, ALU.is_gt, ALU.add)
            link(nc.vector.tensor_scalar(c_[:, 2:3], c_[:, 0:1], 2.0 * P, None, ALU.is_gt))
            link(nc.vector.tensor_tensor(c_[:, 1:2], c_[:, 1:2], c_[:, 2:3], ALU.add))
            nc.vector.tensor_copy(rounds_i[0:1, 0:1], c_[0:1, 1:2]).then_inc(rounds_ready, 1)

            def take_x(n):
                dve.wait_ge(x_hi_done, n)
                nc.vector.tensor_copy(cur[:, 7:8], banks[7][:, 1:2])
                for k in range(KD):
                    last = nc.vector.scalar_tensor_tensor(
                        out=x_lo[:, k, :], in0=banks[2 + k // 4][:, P * (k % 4):P * (k % 4) + P], scalar=pr("m_pre", k),
                        in1=x_hi[:, k, :].bitcast(F32), op0=ALU.mult, op1=ALU.subtract)
                last.then_inc(x_lo_done, 1)

            at(dve, "first_x")
            take_x(1)
            dve.wait_ge(added, 1)
            dve.wait_ge(rounds_ready, 1)
            rounds = dve.value_load(rounds_i[0:1, 0:1], min_val=1, max_val=3)

            LINKS = 2

            def expert(it, e):
                done = [0]

                def elink(ins):
                    ins.then_inc(loop_step, 1)
                    done[0] += 1
                    dve.wait_ge(loop_step, it * LINKS + done[0])

                for c in range(EC):
                    split(it, c + 2)
                    if c - 2 in SCATTER:
                        i = SCATTER.index(c - 2)
                        at_expert(dve, it, "scattered", i)
                        y = y_acc[:, i % 3, NT * (i // 3):NT * (i // 3) + NT]
                        nc.vector.tensor_tensor(y, y, banks[(7, 4, 5)[i % 3]][:, :], ALU.add).then_inc(added, 1)
                    if c % 4 == 0 and 1 <= c // 4 <= UT:
                        j = c // 4 - 1
                        dve.wait_ge(silu_done, it * UT + (j + 1))
                        if j >= 2:
                            at_expert(dve, it, "turned", j - 2)
                        nc.vector.scalar_tensor_tensor(out=e_h[:, j % 2, :], in0=banks[2 * (j % 2) + 1][:, :],
                                                       scalar=cur[:, 7:8], in1=e_silu[:], op0=ALU.mult, op1=ALU.mult)\
                            .then_inc(eh_done, 1)
                    if c % 4 == 0 and 2 <= c // 4 <= UT + 1:
                        j = c // 4 - 2
                        dve.wait_ge(eh_hi_done, it * UT + (j + 1))
                        nc.vector.tensor_tensor(eh_lo[:, 4 * j:4 * j + 4, :],
                                                banks[6][:, :].rearrange("p (f n) -> p f n", f=4),
                                                eh_hi[:, 4 * j:4 * j + 4, :].bitcast(F32), ALU.subtract)\
                            .then_inc(eh_lo_done, 1)
                    if c == 4 * UT + 2:
                        at_expert(dve, it, "gate")
                        nc.vector.tensor_copy(cur[:, 6:7], banks[7][:, 0:1]).then_inc(gate_done, 1)
                    if c == 4 * UT + 3:
                        at_expert(dve, it, "selT")
                        choose((e + 1) % NE, elink)
                    if c == 4 * UT + 10:
                        at_expert(dve, it, "x")
                        take_x(it + 2)
                assert done[0] == LINKS

            with dve.Fori(0, rounds) as r:
                with dve.Fori(0, NE) as e:
                    expert(r * NE + e, e)

            for i in range(6):
                at_last(dve, rounds, i)
                y = y_acc[:, i // 2, NT * (i % 2):NT * (i % 2) + NT]
                nc.vector.tensor_tensor(y, y, banks[(7, 6, 5, 4, 3, 2)[i]][:, :], ALU.add).then_inc(added, 1)
            dve.wait_ge(fin_sum, 6)
            halves = small[:, 220:226].rearrange("p (b h) -> p b h", h=2)
            nc.vector.tensor_reduce(mss, halves, AX_X, ALU.add).then_inc(fin_std, 1)
            dve.wait_ge(fin_std, 2)
            link(nc.vector.reciprocal(mrs, mrs))
            for b, (t0, n) in enumerate(TB):
                link(nc.vector.scalar_tensor_tensor(out=y_acc[0:n, b, :], in0=y_acc[0:n, b, :],
                                                    scalar=mrs[0:n, b:b + 1], in1=grow[0:n, :],
                                                    op0=ALU.mult, op1=ALU.mult))
                nc.vector.tensor_tensor(y_acc[0:n, b, :], y_acc[0:n, b, :], h_tok[0:n, b, :], ALU.add)\
                    .then_inc(fin_done, 1)


_WEIGHTS = ["a_w_in", "a_gate_a_w", "a_gate_x_w", "a_w_out", "kv_w_dkv", "kv_w_ukv", "b_w_dq", "b_w_uq", "b_w_o",
            "f_w_gate_up", "f_w_down", "m_w_gate_up", "m_w_down"]
_VECTORS = {"a_pre": "a_pre_norm", "conv_b": "a_conv_b", "ga_b": "a_gate_a_b", "gx_b": "a_gate_x_b",
            "lam": "a_lambda", "a_post": "a_post_norm", "kv_norm": "kv_norm", "latent": "kv_latent_norm",
            "b_pre": "b_pre_norm", "q_norm": "b_q_norm", "b_post": "b_post_norm", "f_pre": "f_pre_norm",
            "f_post": "f_post_norm", "m_pre": "m_pre_norm"}


def shape_constants():
    c = np.zeros((P, NCONST), np.float32)

    def put(name, x):
        c[:, CONST[name][0]:CONST[name][1]] = x

    put("ident", np.eye(P))
    put("ones", 1.0)
    put("tri", np.arange(P)[:, None] < np.arange(P)[None, :])
    put("iota", np.arange(P)[None, :])
    put("valid", [[float(i < n) for _, n in TB] for i in range(P)])
    put("expert", np.tile(np.arange(NE) + NE, 3)[None, :])
    for b, (t0, n) in enumerate(TB):
        width = CONST[f"mask{b}"][1] - CONST[f"mask{b}"][0]
        put(f"mask{b}", np.where(np.arange(width)[None, :] <= t0 + np.arange(P)[:, None], 0.0, -1.0e30))
    half = ROPE // 2
    inv = np.float32(10000.0) ** (-np.arange(0, ROPE, 2, dtype=np.float32) / np.float32(ROPE))
    ang = (np.arange(T, dtype=np.float32)[:, None] * inv[None, :]).astype(np.float32)
    cos, sin = np.cos(ang).T, np.sin(ang).T
    assert cos.shape == (half, T)
    put("cos", np.tile(cos, (P // half, 1)))
    put("sin", np.tile(np.concatenate([-sin, sin]), (P // ROPE, 1)))
    return c


def kernel(**inputs):
    import concourse.bacc as _bacc
    from concourse.bass_utils import run_bass_kernel_spmd as _run

    x = {k: np.ascontiguousarray(v) for k, v in inputs.items()}
    params = np.zeros((P, NPARAM), np.float32)

    def put(name, v):
        params[:, PARAM[name][0]:PARAM[name][1]] = v

    for name, key in _VECTORS.items():
        put(name, x[key].reshape(-1, P).T)
    put("conv_w", x["a_conv_w"].reshape(-1, P).T)
    put("router_w", x["m_router_w"][0].reshape(KD, P, NE).transpose(1, 0, 2).reshape(P, KD * NE))
    put("eps", EPS)
    arrays = {n: x[n] for n in _WEIGHTS}
    arrays["params"] = params
    arrays["consts"] = shape_constants()
    arrays["gain_rows"] = np.concatenate([x["m_post_norm"].reshape(1, -1), x["m_router_b"].reshape(1, -1)], axis=1)
    arrays["tokens"] = np.concatenate([x["meta_tokens"], x["x"][0]], axis=0)
    nc = _bacc.Bacc("TRN2", target_bir_lowering=False, num_devices=1)
    aps = {n: nc.dram_tensor(f"in_{n}", a.shape, F32, kind="ExternalInput").ap() for n, a in arrays.items()}
    out = nc.dram_tensor("out_0", (SEQ, D), F32, kind="ExternalOutput").ap()
    yoco_kernel(nc, aps, aps["params"], aps["consts"], aps["gain_rows"], aps["tokens"], out)
    r = _run(nc, [{f"in_{n}": a for n, a in arrays.items()}], core_ids=[0])
    return r.results[0]["out_0"].reshape(1, SEQ, D)
```
